# Optimizing a Trainium2 kernel written in Bass

```python
import jax
import jax.numpy as jnp
from jax import lax
import numpy as np
import math
import jax, jax.numpy as jnp

D_MODEL = 1024
BATCH = 1
SEQ = 512
DEPTH = 2

GRID_W = 64
CTX_LEN = 256
EPS = 1e-6
ROPE_THETA = 10000.0
Q_BLOCK = 128

A_HEADS = 8
A_NOPE = 64
A_ROPE = 32
A_V = 64
A_QK = A_NOPE + A_ROPE
KV_LORA = 256
Q_LORA = 768
A_WIDTH = A_HEADS * A_V

B_HEADS = 4
B_DK = 64
B_DV = 128
B_KW = B_HEADS * B_DK
B_WIDTH = B_HEADS * B_DV
GATE_RANK = 16
GATE_TAU = 16.0
CHUNK = 64

C_HEADS = 16
C_HD = 64
C_WIDTH = C_HEADS * C_HD
WIN_ROWS = 8
WIN_COLS = 16

EVEN_SPLITS = (Q_LORA, KV_LORA, A_ROPE, A_WIDTH, B_KW, B_KW, B_WIDTH, 2 * GATE_RANK, B_WIDTH)
EVEN_IN = sum(EVEN_SPLITS)
ODD_IN = 4 * C_WIDTH
N_EVEN = (DEPTH + 1) // 2
N_ODD = DEPTH // 2


def rms_norm(x, gain):
    xf = x.astype(jnp.float32)
    y = xf * lax.rsqrt(jnp.mean(xf * xf, axis=-1, keepdims=True) + EPS)
    return (y * gain.astype(jnp.float32)).astype(x.dtype)

def split_cols(u, sizes):
    idx = np.cumsum(sizes)[:-1].tolist()
    return jnp.split(u, idx, axis=-1)

def modulation(cond, w, b):
    m = jnp.dot(jax.nn.silu(cond), w) + b
    return jnp.split(m[..., None, :], 3, axis=-1)

def axial_rope_tables(n):
    t = jnp.arange(n)
    row = (t // GRID_W).astype(jnp.float32)
    col = (t % GRID_W).astype(jnp.float32)
    d_ax = A_ROPE // 2
    inv = ROPE_THETA ** (-jnp.arange(0, d_ax, 2, dtype=jnp.float32) / d_ax)
    ang = jnp.stack([row[:, None] * inv, col[:, None] * inv], axis=1)
    return jnp.cos(ang), jnp.sin(ang)

def apply_axial_rope(x, cos, sin):
    shp = x.shape
    xr = x.astype(jnp.float32).reshape(shp[:-1] + (2, 2, shp[-1] // 4))
    x1, x2 = xr[..., 0, :], xr[..., 1, :]
    cs, sn = cos[None, :, None], sin[None, :, None]
    out = jnp.stack([x1 * cs - x2 * sn, x2 * cs + x1 * sn], axis=-2)
    return out.reshape(shp).astype(x.dtype)

def block_attention(q, k, v, scale):
    bsz, n, h, dq = q.shape
    nb = n // Q_BLOCK
    qb = q.reshape(bsz, nb, Q_BLOCK, h, dq).transpose(1, 0, 2, 3, 4)

    def one(qi):
        s = jnp.einsum('bqhd,bkhd->bhqk', qi, k, preferred_element_type=jnp.float32) * scale
        p = jax.nn.softmax(s, axis=-1).astype(v.dtype)
        return jnp.einsum('bhqk,bkhd->bqhd', p, v)

    o = lax.map(one, qb)
    return o.transpose(1, 0, 2, 3, 4).reshape(bsz, n, h, v.shape[-1])

def mla_heads(q_lat, kv_lat, k_rope, q_norm, w_uq, kv_norm, w_ukv, q_gain, k_gain, rope):
    bsz, n, _ = q_lat.shape
    q = jnp.dot(rms_norm(q_lat, q_norm), w_uq).reshape(bsz, n, A_HEADS, A_QK)
    kv = jnp.dot(rms_norm(kv_lat, kv_norm), w_ukv).reshape(bsz, n, A_HEADS, A_NOPE + A_V)
    k = jnp.concatenate(
        [kv[..., :A_NOPE], jnp.broadcast_to(k_rope[:, :, None, :], (bsz, n, A_HEADS, A_ROPE))], axis=-1)
    q = rms_norm(q, q_gain)
    k = rms_norm(k, k_gain)
    if rope is not None:
        cos, sin = rope
        q = jnp.concatenate([q[..., :A_NOPE], apply_axial_rope(q[..., A_NOPE:], cos, sin)], axis=-1)
        k = jnp.concatenate([k[..., :A_NOPE], apply_axial_rope(k[..., A_NOPE:], cos, sin)], axis=-1)
    return q, k, kv[..., A_NOPE:]

def gla_inputs(gq, gk, gv, g_lr, gate_w, gate_b):
    bsz, n, _ = gq.shape
    q = gq.reshape(bsz, n, B_HEADS, B_DK) * (B_DK ** -0.5)
    k = gk.reshape(bsz, n, B_HEADS, B_DK)
    v = gv.reshape(bsz, n, B_HEADS, B_DV)
    r = g_lr.reshape(bsz, n, 2, GATE_RANK)
    logits = jnp.einsum('bnzr,zrk->bnzk', r, gate_w) + gate_b
    g = (jax.nn.log_sigmoid(logits.astype(jnp.float32)) / GATE_TAU).reshape(bsz, n, 2, B_HEADS, B_DK)
    return q, k, v, g[:, :, 0], g[:, :, 1]

def gla_scan(q, k, v, g, s0):
    bsz, n, h, dk = q.shape
    dv = v.shape[-1]
    nc = n // CHUNK

    def to_chunks(t):
        return t.astype(jnp.float32).reshape(bsz, nc, CHUNK, h, t.shape[-1]).transpose(1, 0, 3, 2, 4)

    mask = jnp.tril(jnp.ones((CHUNK, CHUNK), dtype=bool))

    def step(state, inp):
        qi, ki, vi, gi = inp
        b = jnp.cumsum(gi, axis=-2)
        b_last = b[..., -1:, :]
        q_t = qi * jnp.exp(b)
        k_t = ki * jnp.exp(-b)
        att = jnp.where(mask, jnp.einsum('bhld,bhmd->bhlm', q_t, k_t), 0.0)
        o = jnp.einsum('bhld,bhde->bhle', q_t, state) + jnp.einsum('bhlm,bhme->bhle', att, vi)
        k_dec = ki * jnp.exp(b_last - b)
        state = state * jnp.exp(b_last)[..., 0, :, None] + jnp.einsum('bhld,bhle->bhde', k_dec, vi)
        return state, o

    s_final, o = lax.scan(step, s0, (to_chunks(q), to_chunks(k), to_chunks(v), to_chunks(g)))
    return o.transpose(1, 0, 3, 2, 4).reshape(bsz, n, h, dv), s_final

def gla_bidirectional(lat, ctx):
    ql, kl, vl, gfl, gbl = lat
    qc, kc, vc, gfc, gbc = ctx
    s0 = jnp.zeros((ql.shape[0], B_HEADS, B_DK, B_DV), jnp.float32)
    flip = lambda t: jnp.flip(t, axis=1)
    oc_f, sc_f = gla_scan(qc, kc, vc, gfc, s0)
    oc_b, sc_b = gla_scan(flip(qc), flip(kc), flip(vc), flip(gbc), s0)
    ol_f, _ = gla_scan(ql, kl, vl, gfl, sc_f)
    ol_b, _ = gla_scan(flip(ql), flip(kl), flip(vl), flip(gbl), sc_b)
    return ol_f + flip(ol_b), oc_f + flip(oc_b)

def even_mixer(h, hc, rope, w_in, q_norm, w_uq, kv_norm, w_ukv, q_gain, k_gain,
               gate_w, gate_b, gla_norm, w_out, update_ctx):
    lat = split_cols(jnp.dot(h, w_in), EVEN_SPLITS)
    cp = split_cols(jnp.dot(hc, w_in), EVEN_SPLITS)
    mla_p = (q_norm, w_uq, kv_norm, w_ukv, q_gain, k_gain)
    q_x, k_x, v_x = mla_heads(lat[0], lat[1], lat[2], *mla_p, rope)
    q_c, k_c, v_c = mla_heads(cp[0], cp[1], cp[2], *mla_p, None)
    scale = A_QK ** -0.5
    a_x = block_attention(q_x, jnp.concatenate([k_x, k_c], axis=1), jnp.concatenate([v_x, v_c], axis=1), scale)
    b_x, b_c = gla_bidirectional(gla_inputs(lat[4], lat[5], lat[6], lat[7], gate_w, gate_b),
                                 gla_inputs(cp[4], cp[5], cp[6], cp[7], gate_w, gate_b))
    gla_gain = gla_norm.reshape(B_HEADS, B_DV)

    def readout(a, b, za, zb):
        bsz, n = a.shape[:2]
        a = a.reshape(bsz, n, A_WIDTH) * jax.nn.silu(za)
        b = rms_norm(b, gla_gain).reshape(bsz, n, B_WIDTH).astype(zb.dtype) * jax.nn.silu(zb)
        return jnp.dot(jnp.concatenate([a, b], axis=-1), w_out)

    y = readout(a_x, b_x, lat[3], lat[8])
    yc = None
    if update_ctx:
        a_c = block_attention(q_c, k_c, v_c, scale)
        yc = readout(a_c, b_c, cp[3], cp[8])
    return y, yc

def neighborhood_attention(q, k, v, k_ctx, v_ctx, rpb):
    bsz, n, h, d = q.shape
    rows = n // GRID_W
    kr = min(WIN_ROWS, rows)
    kc = WIN_COLS
    scale = d ** -0.5
    kg = k.reshape(bsz, rows, GRID_W, h, d)
    vg = v.reshape(bsz, rows, GRID_W, h, d)
    qg = q.reshape(bsz, rows, GRID_W, h, d).transpose(1, 0, 2, 3, 4)
    col = jnp.arange(GRID_W)
    col_start = jnp.clip(col - kc // 2, 0, GRID_W - kc)
    col_mask = (col[None, :] >= col_start[:, None]) & (col[None, :] < col_start[:, None] + kc)
    col_idx = jnp.clip(col[None, :] - col[:, None] + WIN_COLS - 1, 0, 2 * WIN_COLS - 2)

    def one_row(args):
        qr, r = args
        r_start = jnp.clip(r - kr // 2, 0, rows - kr)
        kb = lax.dynamic_slice_in_dim(kg, r_start, kr, axis=1)
        vb = lax.dynamic_slice_in_dim(vg, r_start, kr, axis=1)
        row_idx = r_start + jnp.arange(kr) - r + WIN_ROWS - 1
        bias = rpb[:, row_idx][:, :, col_idx].transpose(0, 2, 1, 3)
        s_lat = jnp.einsum('bqhd,brkhd->bhqrk', qr, kb, preferred_element_type=jnp.float32) * scale
        s_lat = s_lat + bias.astype(jnp.float32)[None]
        s_lat = jnp.where(col_mask[None, None, :, None, :], s_lat, -jnp.inf).reshape(bsz, h, GRID_W, kr * GRID_W)
        s_ctx = jnp.einsum('bqhd,bchd->bhqc', qr, k_ctx, preferred_element_type=jnp.float32) * scale
        p = jax.nn.softmax(jnp.concatenate([s_lat, s_ctx], axis=-1), axis=-1).astype(v.dtype)
        o = jnp.einsum('bhqk,bkhd->bqhd', p[..., :kr * GRID_W], vb.reshape(bsz, kr * GRID_W, h, d))
        return o + jnp.einsum('bhqc,bchd->bqhd', p[..., kr * GRID_W:], v_ctx)

    o = lax.map(one_row, (qg, jnp.arange(rows)))
    return o.transpose(1, 0, 2, 3, 4).reshape(bsz, n, h, d)

def odd_mixer(h, hc, w_in, q_gain, k_gain, rpb, w_out, update_ctx):
    def heads(u):
        bsz, n, _ = u.shape
        q, k, v, z = jnp.split(u, 4, axis=-1)
        sh = lambda t: t.reshape(bsz, n, C_HEADS, C_HD)
        return rms_norm(sh(q), q_gain), rms_norm(sh(k), k_gain), sh(v), z

    q_x, k_x, v_x, z_x = heads(jnp.dot(h, w_in))
    q_c, k_c, v_c, z_c = heads(jnp.dot(hc, w_in))
    o = neighborhood_attention(q_x, k_x, v_x, k_c, v_c, rpb)
    y = jnp.dot(o.reshape(h.shape[0], h.shape[1], C_WIDTH) * jax.nn.silu(z_x), w_out)
    yc = None
    if update_ctx:
        o_c = block_attention(q_c, k_c, v_c, C_HD ** -0.5)
        yc = jnp.dot(o_c.reshape(hc.shape[0], hc.shape[1], C_WIDTH) * jax.nn.silu(z_c), w_out)
    return y, yc

def first_inputs(seed: int = 0) -> dict:
    key = jax.random.key(seed)
    ks = jax.random.split(key, 23)
    D = D_MODEL

    def normal(i, shape, s=1.0):
        return s * jax.random.normal(ks[i], shape, jnp.float32)

    def gain(i, shape):
        return 1.0 + normal(i, shape, 0.05)

    return {
        "x": normal(0, (BATCH, SEQ, D)),
        "c": normal(1, (BATCH, D)),
        "ctx": normal(2, (BATCH, CTX_LEN, D)),
        "c_ctx": normal(3, (D,)),
        "norm_g": gain(4, (DEPTH, D)),
        "ada_w": normal(5, (DEPTH, D, 3 * D), 0.5 * D ** -0.5),
        "ada_b": normal(6, (DEPTH, 3 * D), 0.02),
        "ev_w_in": normal(7, (N_EVEN, D, EVEN_IN), D ** -0.5),
        "ev_q_norm": gain(8, (N_EVEN, Q_LORA)),
        "ev_w_uq": normal(9, (N_EVEN, Q_LORA, A_HEADS * A_QK), Q_LORA ** -0.5),
        "ev_kv_norm": gain(10, (N_EVEN, KV_LORA)),
        "ev_w_ukv": normal(11, (N_EVEN, KV_LORA, A_HEADS * (A_NOPE + A_V)), KV_LORA ** -0.5),
        "ev_q_gain": gain(12, (N_EVEN, A_QK)),
        "ev_k_gain": gain(13, (N_EVEN, A_QK)),
        "ev_gate_w": normal(14, (N_EVEN, 2, GATE_RANK, B_KW), GATE_RANK ** -0.5),
        "ev_gate_b": normal(15, (N_EVEN, 2, B_KW), 0.1),
        "ev_gla_norm": gain(16, (N_EVEN, B_WIDTH)),
        "ev_w_out": normal(17, (N_EVEN, A_WIDTH + B_WIDTH, D), (A_WIDTH + B_WIDTH) ** -0.5),
        "od_w_in": normal(18, (N_ODD, D, ODD_IN), D ** -0.5),
        "od_q_gain": gain(19, (N_ODD, C_HD)),
        "od_k_gain": gain(20, (N_ODD, C_HD)),
        "od_rpb": normal(21, (N_ODD, C_HEADS, 2 * WIN_ROWS - 1, 2 * WIN_COLS - 1), 0.1),
        "od_w_out": normal(22, (N_ODD, C_WIDTH, D), C_WIDTH ** -0.5),
    }

def first_block(x, c, ctx, c_ctx, norm_g, ada_w, ada_b, ev_w_in, ev_q_norm, ev_w_uq, ev_kv_norm, ev_w_ukv,
              ev_q_gain, ev_k_gain, ev_gate_w, ev_gate_b, ev_gla_norm, ev_w_out,
              od_w_in, od_q_gain, od_k_gain, od_rpb, od_w_out):
    rope = axial_rope_tables(x.shape[1])
    cx = ctx
    for i in range(DEPTH):
        update_ctx = i < DEPTH - 1
        shift, scale, gate = modulation(c, ada_w[i], ada_b[i])
        c_shift, c_scale, c_gate = modulation(c_ctx, ada_w[i], ada_b[i])
        h = rms_norm(x, norm_g[i]) * (1 + scale) + shift
        hc = rms_norm(cx, norm_g[i]) * (1 + c_scale) + c_shift
        j = i // 2
        if i % 2 == 0:
            y, yc = even_mixer(h, hc, rope, ev_w_in[j], ev_q_norm[j], ev_w_uq[j], ev_kv_norm[j], ev_w_ukv[j],
                               ev_q_gain[j], ev_k_gain[j], ev_gate_w[j], ev_gate_b[j], ev_gla_norm[j],
                               ev_w_out[j], update_ctx)
        else:
            y, yc = odd_mixer(h, hc, od_w_in[j], od_q_gain[j], od_k_gain[j], od_rpb[j], od_w_out[j], update_ctx)
        x = x + gate * y
        if update_ctx:
            cx = cx + c_gate * yc
    return x


DEPTH_2 = 4

N_MIXERS = 3
D_INNER = D_MODEL
PLE_DIM = 256
CONV_WIDTH = 3
SSM_GROUP = 16
SSM_STATE = 64
SSM_GROUPS = D_INNER // SSM_GROUP
DT_MIN = 1e-3
DT_MAX = 1e-1
RWKV_HEAD = 64
RWKV_HEADS = D_INNER // RWKV_HEAD
DECAY_LORA = 64
ICLR_LORA = 64
RWKV_GN_EPS = 64e-5
LN_EPS = 1e-5
DN_ALPHA = (2 * DEPTH_2) ** 0.25
DN_BETA = (8 * DEPTH_2) ** -0.25
N_CONV = (DEPTH_2 + 2) // 3
N_SSM = (DEPTH_2 + 1) // 3
N_RWKV = DEPTH_2 // 3


def layer_norm(h, g, b, eps=LN_EPS):
    h32 = h.astype(jnp.float32)
    mu = h32.mean(-1, keepdims=True)
    var = jnp.square(h32 - mu).mean(-1, keepdims=True)
    return ((h32 - mu) * lax.rsqrt(var + eps) * g.astype(jnp.float32) + b.astype(jnp.float32)).astype(h.dtype)

def token_shift(x):
    return jnp.pad(x, ((0, 0), (1, 0), (0, 0)))[:, :-1]

def short_conv_mixer(x, w_in, conv_k, w_out):
    bg, cg, h, z = jnp.split(x @ w_in, 4, axis=-1)
    u = cg * h
    conv = lax.conv_general_dilated(
        u, conv_k[:, None, :].astype(u.dtype), window_strides=(1,),
        padding=[(CONV_WIDTH - 1, 0)], dimension_numbers=("NWC", "WIO", "NWC"),
        feature_group_count=D_INNER)
    return (bg * conv * jax.nn.silu(z)) @ w_out

def _ssm_combine(left, right):
    a_l, b_l = left
    a_r, b_r = right
    return a_r * a_l, a_r * b_l + b_r

def s5_mixer(x, w_in, lam_re, lam_im, log_dt, b_re, b_im, c_re, c_im, d_skip, w_glu, b_glu, w_out):
    f32 = jnp.float32
    u, z = jnp.split(x @ w_in, 2, axis=-1)
    bsz, seqlen, _ = u.shape
    ug = u.astype(f32).reshape(bsz, seqlen, SSM_GROUPS, SSM_GROUP)
    lam = lax.complex(lam_re.astype(f32), lam_im.astype(f32))
    dt = jnp.exp(log_dt.astype(f32))[:, None]
    a_bar = jnp.exp(lam * dt)
    b_mat = lax.complex(b_re.astype(f32), b_im.astype(f32))
    b_bar = ((a_bar - 1.0) / lam)[..., None] * b_mat
    c_mat = lax.complex(c_re.astype(f32), c_im.astype(f32))
    bu = jnp.einsum("blgh,gph->blgp", ug, b_bar)
    a_seq = jnp.broadcast_to(a_bar, bu.shape)
    states = lax.associative_scan(_ssm_combine, (a_seq, bu), axis=1)[1]
    y = jnp.einsum("blgp,ghp->blgh", states, c_mat).real + d_skip.astype(f32).reshape(SSM_GROUPS, SSM_GROUP) * ug
    y = jax.nn.gelu(y.reshape(bsz, seqlen, D_INNER).astype(x.dtype))
    y = y * jax.nn.sigmoid(y @ w_glu + b_glu)
    return (y * jax.nn.silu(z)) @ w_out

def _rwkv_step(state, inp):
    r_t, w_t, k_t, v_t, kk_t, a_t = inp
    sa = jnp.einsum("bhvk,bhk->bhv", state, -kk_t)
    state = (state * w_t[:, :, None, :] + sa[..., None] * (kk_t * a_t)[:, :, None, :]
             + v_t[..., None] * k_t[:, :, None, :])
    out = jnp.einsum("bhvk,bhk->bhv", state, r_t)
    return state, out

def rwkv7_mixer(x, mu, w_rkvz, w0, w1, w2, a0, a1, a2, k_k, k_a, r_k, lnx_g, lnx_b, w_out):
    f32 = jnp.float32
    bsz, seqlen, _ = x.shape
    dx = token_shift(x) - x
    xs = x[None] + dx[None] * mu[:, None, None, :]
    r, k, v, z = jnp.einsum("nbld,nde->nble", xs[:4], w_rkvz)
    xw, xa = xs[4], xs[5]
    w_log = -jax.nn.softplus(-(w0 + jnp.tanh(xw @ w1) @ w2)) - 0.5
    decay = jnp.exp(-jnp.exp(w_log.astype(f32)))
    a = jax.nn.sigmoid(a0 + (xa @ a1) @ a2).astype(f32)
    heads = lambda t: t.astype(f32).reshape(bsz, seqlen, RWKV_HEADS, RWKV_HEAD)
    kk = heads(k * k_k)
    kk = kk / jnp.maximum(jnp.linalg.norm(kk, axis=-1, keepdims=True), 1e-12)
    k = heads(k * (1.0 + (a.astype(k.dtype) - 1.0) * k_a))
    r, v, decay, a = heads(r), heads(v), heads(decay), heads(a)
    seq_first = lambda t: jnp.moveaxis(t, 1, 0)
    s0 = jnp.zeros((bsz, RWKV_HEADS, RWKV_HEAD, RWKV_HEAD), f32)
    _, out = lax.scan(_rwkv_step, s0, tuple(seq_first(t) for t in (r, decay, k, v, kk, a)))
    out = jnp.moveaxis(out, 0, 1)
    mu_o = out.mean(-1, keepdims=True)
    var_o = jnp.square(out - mu_o).mean(-1, keepdims=True)
    out = ((out - mu_o) * lax.rsqrt(var_o + RWKV_GN_EPS)).reshape(bsz, seqlen, D_INNER)
    out = out * lnx_g.astype(f32) + lnx_b.astype(f32)
    bonus = jnp.sum(r * k * r_k.astype(f32), axis=-1, keepdims=True) * v
    out = (out + bonus.reshape(bsz, seqlen, D_INNER)).astype(x.dtype)
    return (out * jax.nn.silu(z)) @ w_out

def second_inputs(seed: int = 0) -> dict:
    key = jax.random.key(seed)
    ks = iter(jax.random.split(key, 48))
    nrm = lambda shape, s: jax.random.normal(next(ks), shape, jnp.float32) * s
    D, E, G, P, H, N = D_MODEL, D_INNER, SSM_GROUPS, SSM_STATE, RWKV_HEADS, RWKV_HEAD
    ramp = jnp.linspace(0.0, 1.0, E, dtype=jnp.float32) ** 0.85
    inp = {}
    inp["x"] = nrm((BATCH, SEQ, D), 1.0)
    inp["p"] = nrm((DEPTH_2, BATCH, SEQ, PLE_DIM), 1.0)
    inp["conv_w_in"] = nrm((N_CONV, D, 4 * E), D ** -0.5)
    inp["conv_k"] = nrm((N_CONV, CONV_WIDTH, E), CONV_WIDTH ** -0.5)
    inp["conv_w_out"] = nrm((N_CONV, E, D), E ** -0.5 * DN_BETA)
    inp["ssm_w_in"] = nrm((N_SSM, D, 2 * E), D ** -0.5)
    inp["ssm_lam_re"] = -0.5 + nrm((N_SSM, G, P), 0.01)
    inp["ssm_lam_im"] = math.pi * jnp.arange(P, dtype=jnp.float32) + nrm((N_SSM, G, P), 0.01)
    inp["ssm_log_dt"] = jax.random.uniform(next(ks), (N_SSM, G), jnp.float32, math.log(DT_MIN), math.log(DT_MAX))
    inp["ssm_b_re"] = nrm((N_SSM, G, P, SSM_GROUP), (2 * SSM_GROUP) ** -0.5)
    inp["ssm_b_im"] = nrm((N_SSM, G, P, SSM_GROUP), (2 * SSM_GROUP) ** -0.5)
    inp["ssm_c_re"] = nrm((N_SSM, G, SSM_GROUP, P), (2 * P) ** -0.5)
    inp["ssm_c_im"] = nrm((N_SSM, G, SSM_GROUP, P), (2 * P) ** -0.5)
    inp["ssm_d"] = nrm((N_SSM, E), 1.0)
    inp["ssm_w_glu"] = nrm((N_SSM, E, E), E ** -0.5)
    inp["ssm_b_glu"] = nrm((N_SSM, E), 0.01)
    inp["ssm_w_out"] = nrm((N_SSM, E, D), E ** -0.5 * DN_BETA)
    inp["rwkv_mu"] = jax.random.uniform(next(ks), (N_RWKV, 6, D), jnp.float32)
    inp["rwkv_w_rkvz"] = nrm((N_RWKV, 4, D, E), D ** -0.5)
    inp["rwkv_w0"] = -6.0 + 5.0 * ramp + nrm((N_RWKV, E), 0.1)
    inp["rwkv_w1"] = nrm((N_RWKV, D, DECAY_LORA), D ** -0.5)
    inp["rwkv_w2"] = nrm((N_RWKV, DECAY_LORA, E), 0.1 * DECAY_LORA ** -0.5)
    inp["rwkv_a0"] = nrm((N_RWKV, E), 0.1)
    inp["rwkv_a1"] = nrm((N_RWKV, D, ICLR_LORA), D ** -0.5)
    inp["rwkv_a2"] = nrm((N_RWKV, ICLR_LORA, E), 0.1 * ICLR_LORA ** -0.5)
    inp["rwkv_k_k"] = 0.85 + nrm((N_RWKV, E), 0.05)
    inp["rwkv_k_a"] = 1.0 + nrm((N_RWKV, E), 0.05)
    inp["rwkv_r_k"] = nrm((N_RWKV, H, N), 0.1)
    inp["rwkv_lnx_g"] = 1.0 + nrm((N_RWKV, E), 0.05)
    inp["rwkv_lnx_b"] = nrm((N_RWKV, E), 0.01)
    inp["rwkv_w_out"] = nrm((N_RWKV, E, D), E ** -0.5 * DN_BETA)
    inp["ple_proj"] = nrm((DEPTH_2, PLE_DIM, D), PLE_DIM ** -0.5)
    inp["ple_gate"] = nrm((DEPTH_2, D, D), D ** -0.5)
    inp["ln_g"] = 1.0 + nrm((DEPTH_2, D), 0.05)
    inp["ln_b"] = nrm((DEPTH_2, D), 0.01)
    return inp

def second_block(x, p, conv_w_in, conv_k, conv_w_out,
              ssm_w_in, ssm_lam_re, ssm_lam_im, ssm_log_dt, ssm_b_re, ssm_b_im, ssm_c_re, ssm_c_im,
              ssm_d, ssm_w_glu, ssm_b_glu, ssm_w_out,
              rwkv_mu, rwkv_w_rkvz, rwkv_w0, rwkv_w1, rwkv_w2, rwkv_a0, rwkv_a1, rwkv_a2,
              rwkv_k_k, rwkv_k_a, rwkv_r_k, rwkv_lnx_g, rwkv_lnx_b, rwkv_w_out,
              ple_proj, ple_gate, ln_g, ln_b):
    for i in range(DEPTH_2):
        kind, j = i % N_MIXERS, i // N_MIXERS
        if kind == 0:
            y = short_conv_mixer(x, conv_w_in[j], conv_k[j], conv_w_out[j])
        elif kind == 1:
            y = s5_mixer(x, ssm_w_in[j], ssm_lam_re[j], ssm_lam_im[j], ssm_log_dt[j],
                         ssm_b_re[j], ssm_b_im[j], ssm_c_re[j], ssm_c_im[j], ssm_d[j],
                         ssm_w_glu[j], ssm_b_glu[j], ssm_w_out[j])
        else:
            y = rwkv7_mixer(x, rwkv_mu[j], rwkv_w_rkvz[j], rwkv_w0[j], rwkv_w1[j], rwkv_w2[j],
                            rwkv_a0[j], rwkv_a1[j], rwkv_a2[j], rwkv_k_k[j], rwkv_k_a[j],
                            rwkv_r_k[j], rwkv_lnx_g[j], rwkv_lnx_b[j], rwkv_w_out[j])
        r = DN_ALPHA * x + y
        r = r + (p[i] @ ple_proj[i]) * jax.nn.sigmoid(r @ ple_gate[i])
        x = layer_norm(r, ln_g[i], ln_b[i])
    return x


def setup_inputs(seed=0):
    out = dict(first_inputs(seed))
    for name, value in second_inputs(seed + 1).items():
        if name != "x":
            out[name + "_2"] = value
    return out


def reference(
    x, c, ctx, c_ctx, norm_g, ada_w, ada_b, ev_w_in, ev_q_norm, ev_w_uq, ev_kv_norm, ev_w_ukv,
    ev_q_gain, ev_k_gain, ev_gate_w, ev_gate_b, ev_gla_norm, ev_w_out, od_w_in, od_q_gain,
    od_k_gain, od_rpb, od_w_out, p_2, conv_w_in_2, conv_k_2, conv_w_out_2, ssm_w_in_2,
    ssm_lam_re_2, ssm_lam_im_2, ssm_log_dt_2, ssm_b_re_2, ssm_b_im_2, ssm_c_re_2, ssm_c_im_2,
    ssm_d_2, ssm_w_glu_2, ssm_b_glu_2, ssm_w_out_2, rwkv_mu_2, rwkv_w_rkvz_2, rwkv_w0_2,
    rwkv_w1_2, rwkv_w2_2, rwkv_a0_2, rwkv_a1_2, rwkv_a2_2, rwkv_k_k_2, rwkv_k_a_2, rwkv_r_k_2,
    rwkv_lnx_g_2, rwkv_lnx_b_2, rwkv_w_out_2, ple_proj_2, ple_gate_2, ln_g_2, ln_b_2,
):
    x = first_block(
        x, c, ctx, c_ctx, norm_g, ada_w, ada_b, ev_w_in, ev_q_norm, ev_w_uq, ev_kv_norm,
        ev_w_ukv, ev_q_gain, ev_k_gain, ev_gate_w, ev_gate_b, ev_gla_norm, ev_w_out, od_w_in,
        od_q_gain, od_k_gain, od_rpb, od_w_out,
    )
    return second_block(
        x, p_2, conv_w_in_2, conv_k_2, conv_w_out_2, ssm_w_in_2, ssm_lam_re_2, ssm_lam_im_2,
        ssm_log_dt_2, ssm_b_re_2, ssm_b_im_2, ssm_c_re_2, ssm_c_im_2, ssm_d_2, ssm_w_glu_2,
        ssm_b_glu_2, ssm_w_out_2, rwkv_mu_2, rwkv_w_rkvz_2, rwkv_w0_2, rwkv_w1_2, rwkv_w2_2,
        rwkv_a0_2, rwkv_a1_2, rwkv_a2_2, rwkv_k_k_2, rwkv_k_a_2, rwkv_r_k_2, rwkv_lnx_g_2,
        rwkv_lnx_b_2, rwkv_w_out_2, ple_proj_2, ple_gate_2, ln_g_2, ln_b_2,
    )


_drawn_inputs = setup_inputs


def setup_inputs(seed=0):
    import zlib

    import numpy as np

    out = dict(_drawn_inputs(seed))
    spreads = {}
    factors = {'norm_g': 4.378,
     'ada_b': 4.06,
     'ev_q_norm': 8.0,
     'ev_w_uq': 5.714,
     'ev_kv_norm': 8.0,
     'ev_q_gain': 8.0,
     'ev_k_gain': 8.0,
     'ev_gate_b': 8.0,
     'ev_gla_norm': 8.0,
     'od_q_gain': 8.0,
     'od_k_gain': 8.0,
     'od_rpb': 8.0,
     'ssm_lam_re_2': 64.0,
     'ssm_lam_im_2': 64.0,
     'ssm_log_dt_2': 64.0,
     'ssm_b_re_2': 64.0,
     'ssm_b_im_2': 64.0,
     'ssm_c_re_2': 64.0,
     'ssm_c_im_2': 64.0,
     'ssm_w_glu_2': 3.755,
     'ssm_b_glu_2': 200.0,
     'rwkv_w1_2': 8.0,
     'rwkv_w2_2': 8.0,
     'rwkv_a0_2': 8.0,
     'rwkv_a1_2': 8.0,
     'rwkv_a2_2': 8.0,
     'rwkv_k_k_2': 8.0,
     'rwkv_k_a_2': 8.0,
     'rwkv_lnx_g_2': 8.0,
     'rwkv_lnx_b_2': 64.0,
     'ln_b_2': 2.851}
    for name, (base, spread) in spreads.items():
        noise = np.random.default_rng([zlib.crc32(name.encode()), seed]).standard_normal(out[name].shape)
        drawn = base * np.exp(spread * noise) if base else spread * noise
        out[name] = jnp.asarray(drawn.astype(out[name].dtype))
    for name, factor in factors.items():
        out[name] = (out[name] * factor).astype(out[name].dtype)
    return out
```

```python
from contextlib import ExitStack

import concourse.bass as bass
from concourse import mybir

F32 = mybir.dt.float32
ALU = mybir.AluOpType
ACT = mybir.ActivationFunctionType
AX = mybir.AxisListType.X

P = 128
D = 1024
KT = D // P
SEQ, CTX = 512, 256
TOK = SEQ + CTX
LAT = (0, SEQ)
CTXG = (SEQ, CTX)
BANK = 512
RING = 2
SLOT = KT * 512
EPS = 1e-6
LN_EPS = 1e-5
GN_EPS = 64e-5
A_HEADS, A_NOPE, A_ROPE, A_V, A_QK = 8, 64, 32, 64, 96
Q_LORA, KV_LORA = 768, 256
B_HEADS, B_DK, B_DV, RANK, TAU = 4, 64, 128, 16, 16.0
CH = 64
NCH = TOK // CH
C_HEADS = 16
ALPHA = 8 ** 0.25
GROUPS, GRP, STATE = 64, 16, 64
HEADS = 16


class Count:

    def __init__(self, sem):
        self.sem, self.base = sem, 0

    def rise(self, n):
        self.base += n

    def next(self):
        self.base += 1
        return self.base


class Core:

    def __init__(self, nc, ctx):
        self.nc, self.ctx = nc, ctx
        self.psum = ctx.enter_context(nc.psum_tensor("psum", [P, 8, BANK], F32))
        self.ring = ctx.enter_context(nc.sbuf_tensor("ring", [P, RING, SLOT], F32))
        self.landed = [self.sem(f"weights_landed{i}") for i in range(RING)]
        self.counts = {}
        self.dve_step, self.act_step, self.pool_step = (Count(self.sem(n)) for n in ("vector_step", "scalar_step", "gpsimd_step"))
        self.weights, self.first, self.named = [], {}, 0

    def sem(self, name):
        return self.ctx.enter_context(self.nc.semaphore(name))

    def count(self, name):
        if name not in self.counts:
            self.counts[name] = Count(self.sem(name))
        return self.counts[name]

    def sb(self, ctx, name, shape):
        return ctx.enter_context(self.nc.sbuf_tensor(self.name(name), shape, F32))

    def name(self, what):
        self.named += 1
        return f"{what}_{self.named}"

    def plan(self, name, tiles):
        self.first[name] = len(self.weights)
        self.weights += tiles

    def send_weights(self, sp, n):
        if n >= len(self.weights):
            return
        dst, parts = self.ring[:, n % RING, :], self.weights[n]
        width = sum(a.shape[1] for a in parts)
        kt = parts[0].shape[0] // P
        view = dst[:, 0:kt * width].rearrange("p (k c) -> p k c", c=width)
        at = 0
        for a in parts:
            w = a.shape[1]
            sp.dma_start(view[:, :, at:at + w], a.rearrange("(k p) c -> p k c", p=P)).then_inc(self.landed[n % RING], 16)
            at += w

    def sent(self, n):
        return 16 * sum(len(self.weights[i]) for i in range(n % RING, n + 1, RING))

    def slot(self, n):
        parts = self.weights[n]
        width = sum(a.shape[1] for a in parts)
        kt = parts[0].shape[0] // P
        return self.ring[:, n % RING, 0:kt * width].rearrange("p (k c) -> p k c", c=width)


def products(K, name, units, beside=None):
    nc = K.nc
    base = K.first.get(name, 0)
    done, by_dve, by_act = K.count("product_done"), K.count("vector_freed"), K.count("scalar_freed")
    freed = {"vector": by_dve, "scalar": by_act}
    took, n_of = [], {"vector": 0, "scalar": 0}
    last_use = {}
    for i, u in enumerate(units):
        n_of[u[5]] += 1
        took.append(n_of[u[5]])
        if u[0] is not None:
            last_use[u[0]] = i + 1
    assert sorted(last_use) == list(range(len(last_use)))

    with nc.Block() as block:
        @block.tensor
        def _(pe):
            seen = set()
            for i, (tile, p0, m, n, operands, _, _) in enumerate(units):
                if i >= 8:
                    bank_free = freed[units[i - 8][5]]
                    pe.wait_ge(bank_free.sem, bank_free.base + took[i - 8])
                if tile is not None and tile not in seen:
                    seen.add(tile)
                    pe.wait_ge(K.landed[(base + tile) % RING], K.sent(base + tile))
                pairs = operands(K.slot(base + tile) if tile is not None else None)
                out = K.psum[p0:p0 + m, i % 8, 0:n]
                if pairs[0] == "T":
                    nc.tensor.transpose(out, pairs[1], pairs[2]).then_inc(done.sem, 1)
                    continue
                for j, (lhsT, rhs) in enumerate(pairs):
                    mm = nc.tensor.matmul(out, lhsT, rhs, start=j == 0, stop=j == len(pairs) - 1)
                mm.then_inc(done.sem, 1)

        @block.vector
        def _(dve):
            for i, (_, p0, m, n, _, engine, evacuate) in enumerate(units):
                if engine == "vector":
                    dve.wait_ge(done.sem, done.base + i + 1)
                    evacuate(dve, dve, K.psum[p0:p0 + m, i % 8, 0:n]).then_inc(by_dve.sem, 1)
            if beside:
                beside(dve)

        @block.scalar
        def _(act):
            for i, (_, p0, m, n, _, engine, evacuate) in enumerate(units):
                if engine == "scalar":
                    act.wait_ge(done.sem, done.base + i + 1)
                    evacuate(act, act, K.psum[p0:p0 + m, i % 8, 0:n]).then_inc(by_act.sem, 1)

        @block.sync
        def _(sp):
            for t in range(len(last_use)):
                sp.wait_ge(done.sem, done.base + last_use[t])
                K.send_weights(sp, base + t + RING)

    done.rise(len(units))
    by_dve.rise(n_of["vector"])
    by_act.rise(n_of["scalar"])


def norms(K, items, ones, scale, eps, apply, kind="rms", buffers=None):
    nc = K.nc
    sq_done, sq_used, root_done, root_used = (K.count(x) for x in (
        "square_done", "square_summed", "root_done", "root_used"))
    rows = items[0][0][0].shape[0]
    n_src = [len(s) for s, _ in items]
    upto = [sum(n_src[:i + 1]) for i in range(len(items))]
    with ExitStack() as ctx:
        if buffers:
            x, y = (b[:, :, :, :].rearrange("p e c t -> p e (c t)") for b in buffers)
            sq, root, rinv = x[:, 0:2, :], x[:, 2:4, :], y[:, 0:2, :]
        else:
            sq, root, rinv = (K.sb(ctx, n, [P, 2, BANK]) for n in ("squares", "roots", "rinv"))
        with nc.Block() as block:
            @block.scalar
            def _(act):
                def take_root(i):
                    n = items[i][0][0].shape[1]
                    act.wait_ge(sq_used.sem, sq_used.base + upto[i])
                    if i >= 2:
                        act.wait_ge(root_used.sem, root_used.base + i - 1)
                    if kind == "norm":
                        nc.scalar.activation(root[0:rows, i % 2, 0:n], K.psum[0:rows, i % 2, 0:n], ACT.Sqrt).then_inc(root_done.sem, 1)
                    else:
                        nc.scalar.activation(root[0:rows, i % 2, 0:n], K.psum[0:rows, i % 2, 0:n], ACT.Sqrt,
                                             bias=eps[0:rows, :], scale=scale).then_inc(root_done.sem, 1)
                j = 0
                for i, (srcs, _) in enumerate(items):
                    for s in srcs:
                        if j >= 2:
                            act.wait_ge(sq_used.sem, sq_used.base + j - 1)
                        nc.scalar.activation(sq[0:rows, j % 2, 0:s.shape[1]], s, ACT.Square).then_inc(sq_done.sem, 1)
                        j += 1
                    if i >= 1:
                        take_root(i - 1)
                take_root(len(items) - 1)

            @block.tensor
            def _(pe):
                j = 0
                for i, (srcs, _) in enumerate(items):
                    if i >= 2:
                        pe.wait_ge(root_done.sem, root_done.base + i - 1)
                    for k, s in enumerate(srcs):
                        pe.wait_ge(sq_done.sem, sq_done.base + j + 1)
                        n = s.shape[1]
                        mm = nc.tensor.matmul(K.psum[0:rows, i % 2, 0:n], ones, sq[0:rows, j % 2, 0:n],
                                              start=k == 0, stop=k == len(srcs) - 1)
                        mm.then_inc(sq_used.sem, 1)
                        j += 1

            @block.vector
            def _(dve):
                for i, (srcs, arg) in enumerate(items):
                    n = srcs[0].shape[1]
                    dve.wait_ge(root_done.sem, root_done.base + i + 1)
                    if i >= 2:
                        dve.wait_ge(root_used.sem, root_used.base + i - 1)
                    r = rinv[0:rows, i % 2, 0:n]
                    src = root[0:rows, i % 2, 0:n]
                    if kind == "norm":
                        dve.tensor_scalar(src, src, 1e-12, None, ALU.max).then_inc(K.dve_step.sem, 1)
                        dve.wait_ge(K.dve_step.sem, K.dve_step.next())
                    dve.reciprocal(r, src).then_inc(K.dve_step.sem, 1)
                    dve.wait_ge(K.dve_step.sem, K.dve_step.next())
                    apply(dve, r, arg).then_inc(root_used.sem, 1)
        sq_done.rise(upto[-1])
        sq_used.rise(upto[-1])
        for c in (root_done, root_used):
            c.rise(len(items))


def columns():
    sizes = [("cond", 2 * KT), ("norm_g", 2 * KT), ("ada_b", 48), ("q_norm", 6), ("kv_norm", 2), ("q_gain", 1), ("k_gain", 1),
             ("gate_b", 4), ("gla_norm", 4), ("od_q_gain", 1), ("od_k_gain", 1), ("conv_k", 48), ("lam_re", 32), ("lam_im", 32),
             ("log_dt", 32), ("d_skip", 8), ("b_glu", 8), ("mu", 48), ("w0", 8), ("a0", 8), ("k_k", 8), ("k_a", 8), ("r_k", 8),
             ("lnx_g", 8), ("lnx_b", 8), ("ln_g", 32), ("ln_b", 32)]
    at, out = 0, {}
    for name, n in sizes:
        out[name] = (at, n)
        at += n
    return out, at


def shape_constants():
    import numpy as np
    i = np.arange(P)
    same = lambda a, n: (a[:, None] // n) == (a[None, :] // n)
    t = np.arange(SEQ)
    inv = 10000.0 ** (-np.arange(0, 16, 2, dtype=np.float32) / 16)
    cos, sin = np.zeros((P, SEQ)), np.zeros((P, SEQ))
    swap = np.zeros((P, 96))
    for d in range(A_ROPE):
        ax, half, k = d // 16, d // 8 % 2, d % 8
        ang = ((t // 64 if ax == 0 else t % 64).astype(np.float32) * inv[k].astype(np.float32)).astype(np.float64)
        cos[64 + d] = np.cos(ang)
        sin[64 + d] = np.sin(ang) * (1 if half else -1)
        swap[64 + (d ^ 8), 64 + d] = 1
    s, u = i[:, None] % 64, np.arange(64)[None, :]
    blk = (s // 16) == (u // 16)
    c = np.arange(64)
    start = np.clip(c - 8, 0, 48)
    keep = (c[None, :] >= start[:, None]) & (c[None, :] < start[:, None] + 16)
    out = [("ident", np.eye(P)), ("ones", np.ones((P, P))), ("ones64", same(i, 64)),
           ("mask_f", same(i, 64) & (i[:, None] <= i[None, :])), ("mask_b", same(i, 64) & (i[:, None] >= i[None, :])),
           ("restart", np.tile(np.arange(TOK) % CH != 0, (P, 1))), 
           ("window", np.tile(np.where(keep, 0, -1e30), (2, 1))),
           ("before", s < u), ("upto", s <= u), ("before_in", (s < u) & blk), ("before_out", (s < u) & ~blk),
           ("after_in", (s > u) & blk), ("after_out", (s > u) & ~blk), ("eye64", s == u),
           ("eps", np.stack([np.full(P, EPS), np.full(P, LN_EPS), np.full(P, GN_EPS), np.full(P, 0.0), np.full(P, 1.0)], 1))]
    tables = np.concatenate([cos, sin, np.pad(swap, ((0, 0), (0, 32))), np.tile(np.arange(SEQ), (P, 1))], axis=1).astype(np.float32)
    at, where = 0, {}
    for name, a in out:
        where[name] = (at, a.shape[1])
        at += a.shape[1]
    return where, np.concatenate([a.astype(np.float32) for _, a in out], axis=1), tables


def plan_weights(K, A):
    def cut(w, a, b, n=512):
        return [[w[:, i:min(i + n, b)]] for i in range(a, b, n)]
    ev = A["ev_w_in"][0]
    K.plan("modulation0", cut(A["ada_w"][0], 0, 3 * D))
    K.plan("gla_in", cut(ev, 1568, 2592) + cut(ev, 2624, 3136) + cut(ev, 2592, 2624))
    K.plan("mla_in", cut(ev, 0, 1024) + cut(ev, 1024, 1056) + cut(ev, 1056, 1568))
    K.plan("q_up", cut(A["ev_w_uq"][0], 0, 768, 384))
    K.plan("kv_up", [[A["ev_w_ukv"][0]]])
    K.plan("ev_out", cut(A["ev_w_out"][0], 0, D))
    K.plan("modulation1", cut(A["ada_w"][1], 0, 3 * D))
    K.plan("od_in", cut(A["od_w_in"][0], 0, 4 * D))
    K.plan("od_out", cut(A["od_w_out"][0], 0, D))
    for layer in range(4):
        kind, j = layer % 3, layer // 3
        if kind == 0:
            w = A["conv_w_in_2"][j]
            K.plan(f"conv_in{layer}", [[w[:, s * D + e * P:s * D + (e + 1) * P] for s in (1, 2, 3, 0)] for e in range(KT)])
            K.plan(f"mix_out{layer}", cut(A["conv_w_out_2"][j], 0, D))
        elif kind == 1:
            K.plan("ssm_in", cut(A["ssm_w_in_2"][0], 0, 2 * D))
            K.plan("ssm_glu", cut(A["ssm_w_glu_2"][0], 0, D))
            K.plan(f"mix_out{layer}", cut(A["ssm_w_out_2"][0], 0, D))
        else:
            r = A["rwkv_w_rkvz_2"][0]
            K.plan("rwkv_w", [[A["rwkv_w1_2"][0]]])
            K.plan("rwkv_a", [[A["rwkv_a1_2"][0]]])
            K.plan("rwkv_z", cut(r[3], 0, D))
            for half in range(2):
                for n, m in enumerate("rkv"):
                    K.plan(f"rwkv_{m}{half}", [[r[n][:, half * 512:half * 512 + 512]]])
            K.plan(f"mix_out{layer}", cut(A["rwkv_w_out_2"][0], 0, D))
        K.plan(f"ple_p{layer}", [[A["ple_proj_2"][layer]]])
        K.plan(f"ple_g{layer}", cut(A["ple_gate_2"][layer], 0, D))


def span(g):
    return slice(g[0], g[0] + g[1])


def one_engine(K, engine, program):
    with K.nc.Block() as block:
        {"vector": block.vector, "scalar": block.scalar, "gpsimd": block.gpsimd}[engine](program)


def copy_to(dst):
    def f(eng, _, ps):
        return eng.tensor_copy(dst, ps)
    return f


def act_to(nc, dst, func):
    def f(eng, _, ps):
        return nc.scalar.activation(dst, ps, func)
    return f


def wide(src, kt, g):
    return [src[:, k, span(g)] for k in range(kt)]


def linear_units(tiles, kt, src, groups, finish, width=4):
    units = []
    for t in tiles:
        for e in range(width):
            for g in groups:
                engine, f = finish(t * width + e, g)
                units.append((t, 0, P, g[1],
                              lambda w, e=e, g=g: [(w[:, k, e * P:(e + 1) * P], src[:, k, span(g)]) for k in range(kt)], engine, f))
    return units


def modulation_units(K, nc, B, layer, tiles):
    units = []
    for t in range(tiles):
        for e in range(4):
            c = 4 * t + e
            def f(eng, _, ps, c=c):
                return eng.tensor_scalar(B.mod[:, layer, c, :], ps, B.col("ada_b")[:, 24 * layer + c:24 * layer + c + 1], None, ALU.add)
            units.append((t, 0, P, 2, lambda w, e=e: [(w[:, k, e * P:(e + 1) * P], B.scond[:, k, :]) for k in range(KT)], "vector", f))
    return units


class Buffers:
    pass


def setup(K, B, A):
    nc = K.nc
    loaded, ready = K.count("setup_loaded"), K.count("setup_ready")
    with nc.Block() as block:
        @block.sync
        def _(sp):
            sp.dma_start(B.cols[:, :], A["columns"]).then_inc(loaded.sem, 16)
            K.send_weights(sp, 0)
            sp.dma_start(B.consts[:, :], A["constants"]).then_inc(loaded.sem, 16)
            for n in range(1, RING):
                K.send_weights(sp, n)
            sp.dma_start(B.X[:, :, :], A["x"].rearrange("(k p) t -> p k t", p=P)).then_inc(loaded.sem, 16)
            sp.dma_start(B.XC[:, :, :], A["ctx"].rearrange("(k p) t -> p k t", p=P)).then_inc(loaded.sem, 16)
            sp.wait_ge(loaded.sem, loaded.base + 64)

        @block.scalar
        def _(act):
            act.wait_ge(loaded.sem, loaded.base + 64)
            nc.scalar.activation(B.scond.rearrange("p k c -> p (k c)"), B.col("cond"), ACT.Silu)
    loaded.rise(64)


def modulated_norm(K, B, layer, H):
    nc = K.nc

    def scales(dve):
        for c in range(2):
            i = dve.scalar_tensor_tensor(B.gain[:, :, c], B.mod[:, layer, 8:16, c], 1.0, B.col("norm_g")[:, 8 * layer:8 * layer + 8],
                                         ALU.add, ALU.mult)
        return i
    one_engine(K, "vector", scales)

    def apply(dve, r, arg):
        g, c = arg
        for k in range(KT):
            i = dve.scalar_tensor_tensor(H[:, k, span(g)], B.x(k, g), B.gain[:, k, c:c + 1], r, ALU.mult, ALU.mult)
        i.then_inc(K.dve_step.sem, 1)
        dve.wait_ge(K.dve_step.sem, K.dve_step.next())
        for k in range(KT):
            i = dve.tensor_scalar(H[:, k, span(g)], H[:, k, span(g)], B.mod[:, layer, k, c:c + 1], None, ALU.add)
        return i
    norms(K, [([B.x(k, g) for k in range(KT)], (g, c)) for c, g in enumerate((LAT, CTXG))], B.const("ones"), 1.0 / D, B.eps(0), apply)


def gla(K, B, ctx, H, A):
    nc = K.nc
    zb = K.sb(ctx, "gla_out", [P, B_HEADS, TOK])
    with ExitStack() as tmp:
        big = K.sb(tmp, "gla_state", [P, 8 * TOK])
        gq = big[:, 0:2 * TOK].rearrange("p (j t) -> p j t", j=2)
        gk = big[:, 2 * TOK:4 * TOK].rearrange("p (j t) -> p j t", j=2)
        bs = big[:, 4 * TOK:6 * TOK].rearrange("p (j t) -> p j t", j=2)
        ex = big[:, 6 * TOK:8 * TOK].rearrange("p (j t) -> p j t", j=2)
        st = big[:, :].rearrange("p (z j c e) -> p z j c e", z=2, j=2, c=NCH)
        gv = K.sb(tmp, "gla_v", [P, TOK // P, 512])
        lr = big[0:32, 4 * TOK:5 * TOK]
        gw = big[0:32, 5 * TOK:5 * TOK + 512].rearrange("p (z c) -> p z c", z=2)
        units = []
        for e in range(4):
            for g in (LAT, CTXG):
                dst = (gq if e < 2 else gk)[:, e % 2, span(g)]
                units.append((0, 0, P, g[1], lambda w, e=e, g=g: [(w[:, k, e * P:(e + 1) * P], H[:, k, span(g)]) for k in range(KT)],
                              "vector", copy_to(dst)))
        for t in range(TOK // P):
            units.append((1, 0, P, 512, lambda w, t=t: [(H[:, k, t * P:(t + 1) * P], w[:, k, :]) for k in range(KT)],
                          "vector", copy_to(gv[:, t, :])))
        units += [(2,) + u[1:] for u in linear_units([0], KT, H, (LAT, CTXG), lambda e, g: ("scalar", act_to(nc, zb[:, e, span(g)], ACT.Silu)))]
        for g in (LAT, CTXG):
            units.append((3, 0, 32, g[1], lambda w, g=g: [(w[:, k, :], H[:, k, span(g)]) for k in range(KT)], "vector", copy_to(lr[:, span(g)])))
        products(K, "gla_in", units)

        go = K.sb(tmp, "gla_kd", [P, 4, TOK])
        dirs = [[K.sb(tmp, f"gla_{n}{z}", [P, 2, TOK]) for n in ("qt", "kt")] + [go[:, 2 * z:2 * z + 2, :]] for z in range(2)]
        decay = K.sb(tmp, "gla_decay", [P, 2, 2, NCH])
        gl = K.sb(tmp, "gla_g", [P, 4, TOK])
        loaded, cleared = K.count("setup_loaded"), K.count("setup_ready")
        logits, lg_used, a1, v1 = (K.count(x) for x in ("product_done", "vector_freed", "scalar_part", "vector_part"))
        with nc.Block() as block:
            @block.gpsimd
            def _(pool):
                nc.gpsimd.memset(gw[:, :, :], 0.0).then_inc(cleared.sem, 1)

            @block.sync
            def _(sp):
                sp.wait_ge(cleared.sem, cleared.base + 1)
                for z in range(2):
                    sp.dma_start(gw[16 * z:16 * z + 16, z, :], A["ev_gate_w"][0, z]).then_inc(loaded.sem, 16)

            @block.tensor
            def _(pe):
                pe.wait_ge(loaded.sem, loaded.base + 32)
                for i in range(4):
                    z, j = i // 2, i % 2
                    for n, g in enumerate((LAT, CTXG)):
                        nc.tensor.matmul(K.psum[:, 2 * i + n, 0:g[1]], gw[:, z, j * P:(j + 1) * P], lr[:, span(g)], start=True,
                                         stop=True).then_inc(logits.sem, 1)

            @block.scalar
            def _(act):
                for i in range(4):
                    act.wait_ge(logits.sem, logits.base + 2 * i + 2)
                    ps = K.psum[:, 2 * i:2 * i + 2, :].rearrange("p b n -> p (b n)")[:, 0:TOK]
                    bias = B.col("gate_b")[:, i:i + 1]
                    nc.scalar.activation(gl[:, i, :], ps, ACT.Identity, bias=bias).then_inc(a1.sem, 1)
                    if i >= 1:
                        act.wait_ge(v1.sem, v1.base + i)
                    nc.scalar.activation(ex[:, 0, :], ps, ACT.Abs, bias=bias).then_inc(K.act_step.sem, 1)
                    act.wait_ge(K.act_step.sem, K.act_step.next())
                    nc.scalar.activation(ex[:, 0, :], ex[:, 0, :], ACT.Exp, scale=-1.0).then_inc(K.act_step.sem, 1)
                    act.wait_ge(K.act_step.sem, K.act_step.next())
                    nc.scalar.activation(ex[:, 1, :], ex[:, 0, :], ACT.Ln, bias=B.eps(4)).then_inc(a1.sem, 1)

            @block.vector
            def _(dve):
                for i in range(4):
                    dve.wait_ge(a1.sem, a1.base + 2 * i + 2)
                    dve.tensor_scalar(gl[:, i, :], gl[:, i, :], 0.0, None, ALU.min).then_inc(K.dve_step.sem, 1)
                    dve.wait_ge(K.dve_step.sem, K.dve_step.next())
                    dve.tensor_tensor(gl[:, i, :], gl[:, i, :], ex[:, 1, :], ALU.subtract).then_inc(v1.sem, 1)
        loaded.rise(32)
        cleared.rise(1)
        logits.rise(8)
        a1.rise(8)
        v1.rise(4)
        with nc.Block() as block:
            @block.vector
            def _(dve):
                for i in range(4):
                    z, j = i // 2, i % 2
                    g, b = gl[:, i, :], bs[:, i % 2, :]
                    qt, kt, kd = (x[:, j, :] for x in dirs[z])
                    if i >= 2:
                        dve.wait_ge(a1.sem, a1.base + 3 * i - 3)
                    dve.tensor_scalar(g, g, 1.0 / TAU, None, ALU.mult).then_inc(K.dve_step.sem, 1)
                    dve.wait_ge(K.dve_step.sem, K.dve_step.next())
                    dve.tensor_tensor_scan(b, B.const("restart"), g, 0.0, ALU.mult, ALU.add).then_inc(K.dve_step.sem, 1)
                    dve.wait_ge(K.dve_step.sem, K.dve_step.next())
                    bc = b.rearrange("p (c t) -> p c t", t=CH)
                    gc = g.rearrange("p (c t) -> p c t", t=CH)
                    dve.tensor_copy(decay[:, z, j, :], bc[:, :, CH - 1]).then_inc(K.dve_step.sem, 1)
                    dve.wait_ge(K.dve_step.sem, K.dve_step.next())
                    total = decay[:, z, j, :].unsqueeze(2).to_broadcast([P, NCH, CH])
                    if z == 1:
                        dve.tensor_tensor(bc, total, bc, ALU.subtract).then_inc(K.dve_step.sem, 1)
                        dve.wait_ge(K.dve_step.sem, K.dve_step.next())
                        dve.tensor_tensor(b, b, g, ALU.add).then_inc(K.dve_step.sem, 1)
                        dve.wait_ge(K.dve_step.sem, K.dve_step.next())
                    dve.tensor_tensor(gc, total, bc, ALU.subtract).then_inc(v1.sem, 1)
                    dve.wait_ge(a1.sem, a1.base + 3 * i + 3)
                    dve.scalar_tensor_tensor(qt, gq[:, j, :], float(B_DK) ** -0.5, qt, ALU.mult, ALU.mult)
                    dve.tensor_tensor(kt, gk[:, j, :], kt, ALU.mult)
                    dve.tensor_tensor(kd, gk[:, j, :], kd, ALU.mult)

            @block.scalar
            def _(act):
                for i in range(4):
                    z, j = i // 2, i % 2
                    qt, kt, kd = (x[:, j, :] for x in dirs[z])
                    act.wait_ge(v1.sem, v1.base + i + 1)
                    nc.scalar.activation(qt, bs[:, i % 2, :], ACT.Exp).then_inc(a1.sem, 1)
                    nc.scalar.activation(kt, bs[:, i % 2, :], ACT.Exp, scale=-1.0).then_inc(a1.sem, 1)
                    nc.scalar.activation(kd, gl[:, i, :], ACT.Exp).then_inc(a1.sem, 1)
                nc.scalar.activation(decay.rearrange("p z j c -> p (z j c)"), decay.rearrange("p z j c -> p (z j c)"), ACT.Exp)
        a1.rise(12)
        v1.rise(4)
        kdT = gl.rearrange("p a t -> p (a t)").rearrange("p (z t c) -> p z t c", z=2, c=256)
        units = []
        for z in range(2):
            for j in range(2):
                for t in range(TOK // P):
                    units.append((None, 0, P, P, lambda w, z=z, j=j, t=t: ("T", dirs[z][2][:, j, t * P:(t + 1) * P], B.const("ident")),
                                  ("vector", "scalar")[t % 2], (copy_to if t % 2 == 0 else lambda d: act_to(nc, d, ACT.Copy))(kdT[:, z, t, j * P:(j + 1) * P])))
        products(K, "", units)
        order = [[8, 9, 10, 11] + list(range(8)), [11, 10, 9, 8] + list(range(7, -1, -1))]
        sum_done, state_done = K.count("product_done"), K.count("vector_freed")
        work = [(n, z, j) for n in range(NCH - 1) for z in range(2) for j in range(2)]
        with nc.Block() as block:
            @block.tensor
            def _(pe):
                for i, (n, z, j) in enumerate(work):
                    if i >= 8:
                        pe.wait_ge(state_done.sem, state_done.base + i - 7)
                    c = order[z][n]
                    r = slice(CH * (c % 2), CH * (c % 2) + CH)
                    for h in range(2):
                        mm = nc.tensor.matmul(K.psum[CH * h:CH * h + CH, i % 8, 0:B_DV], kdT[r, z, c // 2, j * P + CH * h:j * P + CH * h + CH],
                                              gv[r, c // 2, (2 * j + h) * B_DV:(2 * j + h + 1) * B_DV], start=True, stop=True)
                    mm.then_inc(sum_done.sem, 1)

            @block.vector
            def _(dve):
                for z in range(2):
                    i = dve.memset(st[:, z, :, order[z][0], :], 0.0)
                i.then_inc(K.dve_step.sem, 1)
                dve.wait_ge(K.dve_step.sem, K.dve_step.next())
                for i, (n, z, j) in enumerate(work):
                    c, nxt = order[z][n], order[z][n + 1]
                    dve.wait_ge(sum_done.sem, sum_done.base + i + 1)
                    if i >= 4:
                        dve.wait_ge(state_done.sem, state_done.base + i - 3)
                    dve.scalar_tensor_tensor(st[:, z, j, nxt, :], st[:, z, j, c, :], decay[:, z, j, c:c + 1], K.psum[:, i % 8, 0:B_DV],
                                             ALU.mult, ALU.add).then_inc(state_done.sem, 1)
        sum_done.rise(len(work))
        state_done.rise(len(work))
        work = [(h, t) for h in range(B_HEADS) for t in range(TOK // P)]
        scores, masked, out_done, out_used = (K.count(x) for x in ("product_done", "vector_part", "sum_done", "scalar_freed"))
        att = K.sb(tmp, "gla_att", [P, 2, 2, P])
        with nc.Block() as block:
            @block.tensor
            def _(pe):
                def score(i):
                    h, t = work[i]
                    r, j = slice(CH * (h % 2), CH * (h % 2) + CH), h // 2
                    for z in range(2):
                        if i >= 2:
                            pe.wait_ge(masked.sem, masked.base + i - 1)
                        nc.tensor.matmul(K.psum[:, 2 * (i % 2) + z, 0:P], dirs[z][1][r, j, t * P:(t + 1) * P],
                                         dirs[z][0][r, j, t * P:(t + 1) * P], start=True, stop=True).then_inc(scores.sem, 1)
                score(0)
                for i, (h, t) in enumerate(work):
                    if i + 1 < len(work):
                        score(i + 1)
                    r, j = slice(CH * (h % 2), CH * (h % 2) + CH), h // 2
                    pe.wait_ge(masked.sem, masked.base + i + 1)
                    if i >= 2:
                        pe.wait_ge(out_used.sem, out_used.base + i - 1)
                    o = K.psum[:, 4 + i % 2, :]
                    nc.tensor.matmul(o[:, 0:P], gv[:, t, h * P:(h + 1) * P], att[:, i % 2, 0, :], start=True, stop=False)
                    for z in range(2):
                        for c in (2 * t, 2 * t + 1):
                            s = slice(c * CH, (c + 1) * CH)
                            mm = nc.tensor.matmul(o[:, (c % 2) * CH:(c % 2 + 1) * CH], st[r, z, j, c, :], dirs[z][0][r, j, s],
                                                  start=False, stop=z == 1 and c % 2 == 1)
                    mm.then_inc(out_done.sem, 1)

            @block.vector
            def _(dve):
                for i in range(len(work)):
                    dve.wait_ge(scores.sem, scores.base + 2 * i + 2)
                    if i >= 2:
                        dve.wait_ge(out_done.sem, out_done.base + i - 1)
                    dve.tensor_tensor(att[:, i % 2, 0, :], K.psum[:, 2 * (i % 2), 0:P], B.const("mask_f"), ALU.mult)
                    dve.tensor_tensor(att[:, i % 2, 1, :], K.psum[:, 2 * (i % 2) + 1, 0:P], B.const("mask_b"), ALU.mult).then_inc(K.dve_step.sem, 1)
                    dve.wait_ge(K.dve_step.sem, K.dve_step.next())
                    dve.tensor_tensor(att[:, i % 2, 0, :], att[:, i % 2, 0, :], att[:, i % 2, 1, :], ALU.add).then_inc(masked.sem, 1)

            @block.scalar
            def _(act):
                for i, (h, t) in enumerate(work):
                    act.wait_ge(out_done.sem, out_done.base + i + 1)
                    nc.scalar.activation(go[:, h, t * P:(t + 1) * P], K.psum[:, 4 + i % 2, 0:P], ACT.Copy).then_inc(out_used.sem, 1)
        scores.rise(2 * len(work))
        for c in (masked, out_done, out_used):
            c.rise(len(work))
        B.dump("gla", go[:, :, :])

        def apply(dve, r, arg):
            h, g = arg
            dve.scalar_tensor_tensor(go[:, h, span(g)], go[:, h, span(g)], B.col("gla_norm")[:, h:h + 1], r, ALU.mult, ALU.mult).then_inc(K.dve_step.sem, 1)
            dve.wait_ge(K.dve_step.sem, K.dve_step.next())
            return dve.tensor_tensor(zb[:, h, span(g)], zb[:, h, span(g)], go[:, h, span(g)], ALU.mult)
        norms(K, [([go[:, h, span(g)]], (h, g)) for h in range(B_HEADS) for g in (LAT, CTXG)], B.const("ones"), 1.0 / B_DV, B.eps(0), apply)
    return zb


def attention(K, B, ctx, name, n_heads, q_tiles, q_of, k_of, v_of, out_of, scale, scratch, table=None, table_src=None):
    nc = K.nc
    S, W, WT = (scratch[:, 2 * n:2 * n + 2, :] for n in range(3))
    m = K.sb(ctx, "att_max", [P, 2, 4])
    work = [(h, q) for h in range(n_heads) for q in q_tiles]
    nq = len(q_tiles)
    scores, maxed, exped, normed, turned, evac_v, evac_a, out_done, out_used = (K.count(x) for x in (
        "product_done", "vector_part", "scalar_part", "pool_part", "turned", "vector_freed", "scalar_freed", "sum_done", "root_used"))
    t_in = [K.count("table_loaded_even"), K.count("table_loaded_odd")]
    copied = K.count("ctx_scores_copied")
    ident = B.const("ident")
    with nc.Block() as block:
        @block.tensor
        def _(pe):
            def score(i):
                h, (q0, kt0, nk) = work[i]
                if i >= 2:
                    pe.wait_ge(exped.sem, exped.base + i - 1)
                k0 = kt0 * P
                first = min(nk * P, BANK)
                b = 2 * (i % 2)
                mm = nc.tensor.matmul(K.psum[:, b, 0:first], q_of(h)[:, q0:q0 + P], k_of(h)[:, k0:k0 + first], start=True, stop=True)
                if nk * P > BANK:
                    mm = nc.tensor.matmul(K.psum[:, b + 1, 0:nk * P - BANK], q_of(h)[:, q0:q0 + P], k_of(h)[:, k0 + BANK:k0 + nk * P],
                                          start=True, stop=True)
                mm.then_inc(scores.sem, 1)

            def turn(i):
                nk = work[i][1][2]
                pe.wait_ge(normed.sem, normed.base + i + 1)
                if i >= 1:
                    pe.wait_ge(evac_v.sem, evac_v.base + i)
                    pe.wait_ge(evac_a.sem, evac_a.base + i)
                for k in range(nk):
                    t = nc.tensor.transpose(K.psum[:, 4 + 2 * k // nk, k % (nk // 2) * P:(k % (nk // 2) + 1) * P], W[:, i % 2, k * P:(k + 1) * P], ident)
                t.then_inc(turned.sem, 1)

            def out(i):
                h, (q0, kt0, nk) = work[i]
                pe.wait_ge(evac_v.sem, evac_v.base + i + 1)
                pe.wait_ge(evac_a.sem, evac_a.base + i + 1)
                if i >= 2:
                    pe.wait_ge(out_used.sem, out_used.base + i - 1)
                o = K.psum[(h % 2) * 64:(h % 2) * 64 + 64, 6 + i % 2, 0:P]
                for k in range(nk):
                    mm = nc.tensor.matmul(o, v_of(h, kt0 + k), WT[:, i % 2, k * P:(k + 1) * P], start=k == 0, stop=k == nk - 1)
                mm.then_inc(out_done.sem, 1)

            score(0)
            for i in range(len(work)):
                if i + 1 < len(work):
                    score(i + 1)
                if i >= 1:
                    out(i - 1)
                turn(i)
            out(len(work) - 1)

        @block.vector
        def _(dve):
            def head(i):
                h, (q0, kt0, nk) = work[i]
                b = i % 2
                ps = K.psum[:, 2 * b:2 * b + 2, :].rearrange("p b n -> p (b n)")[:, 0:nk * P]
                if table is not None:
                    if i % nq == 0:
                        dve.wait_ge(t_in[h % 2].sem, t_in[h % 2].base + 16 * (h // 2 + 1))
                        dve.tensor_tensor(table[:, h % 2, :, :], table[:, h % 2, :, :],
                                                                B.const("window").unsqueeze(1).to_broadcast([P, 14, 64]), ALU.add).then_inc(K.dve_step.sem, 1)
                        dve.wait_ge(K.dve_step.sem, K.dve_step.next())
                    dve.wait_ge(scores.sem, scores.base + i + 1)
                    if i >= 2:
                        dve.wait_ge(exped.sem, exped.base + i - 1)
                    bias = table[:, h % 2, 6 - 2 * (q0 // P):14 - 2 * (q0 // P), :].rearrange("p m c -> p (m c)")
                    dve.scalar_tensor_tensor(S[:, b, 0:BANK], ps[:, 0:BANK], scale, bias, ALU.mult, ALU.add).then_inc(K.dve_step.sem, 1)
                    dve.wait_ge(K.dve_step.sem, K.dve_step.next())
                    dve.wait_ge(copied.sem, copied.base + i + 1)
                    src, f = S[:, b, 0:nk * P], -1.0
                else:
                    dve.wait_ge(scores.sem, scores.base + i + 1)
                    src, f = ps, -scale
                dve.tensor_reduce(m[:, b, 0:1], src, AX, ALU.max).then_inc(K.dve_step.sem, 1)
                dve.wait_ge(K.dve_step.sem, K.dve_step.next())
                dve.tensor_scalar(m[:, b, 1:2], m[:, b, 0:1], f, None, ALU.mult).then_inc(maxed.sem, 1)

            def probs(i):
                nk = work[i][1][2]
                b = i % 2
                dve.wait_ge(exped.sem, exped.base + i + 1)
                dve.reciprocal(m[:, b, 3:4], m[:, b, 2:3]).then_inc(K.dve_step.sem, 1)
                dve.wait_ge(K.dve_step.sem, K.dve_step.next())
                dve.tensor_scalar(W[:, b, 0:nk * P], W[:, b, 0:nk * P], m[:, b, 3:4], None, ALU.mult).then_inc(normed.sem, 1)

            def take(i):
                h, (q0, kt0, nk) = work[i]
                dve.wait_ge(turned.sem, turned.base + i + 1)
                if i >= 2:
                    dve.wait_ge(out_done.sem, out_done.base + i - 1)
                n = nk * P // 2
                dve.tensor_copy(WT[:, i % 2, 0:n], K.psum[:, 4, 0:n]).then_inc(evac_v.sem, 1)

            def finish(i):
                h, (q0, kt0, nk) = work[i]
                dve.wait_ge(out_done.sem, out_done.base + i + 1)
                o = out_of(h, slice(q0, q0 + P))
                dve.tensor_tensor(o, K.psum[(h % 2) * 64:(h % 2) * 64 + 64, 6 + i % 2, 0:P], o, ALU.mult).then_inc(out_used.sem, 1)

            head(0)
            for i in range(len(work)):
                probs(i)
                if i + 1 < len(work):
                    head(i + 1)
                take(i)
                if i >= 1:
                    finish(i - 1)
            finish(len(work) - 1)

        @block.scalar
        def _(act):
            def exp(i):
                nk = work[i][1][2]
                b = i % 2
                ps = K.psum[:, 2 * b:2 * b + 2, :].rearrange("p b n -> p (b n)")[:, 0:nk * P]
                if table is not None:
                    act.wait_ge(scores.sem, scores.base + i + 1)
                    nc.scalar.activation(S[:, b, BANK:TOK], ps[:, BANK:TOK], ACT.Copy, scale=scale).then_inc(copied.sem, 1)
                    src, f = S[:, b, 0:nk * P], 1.0
                else:
                    src, f = ps, scale
                act.wait_ge(maxed.sem, maxed.base + i + 1)
                if i >= 2:
                    act.wait_ge(turned.sem, turned.base + i - 1)
                nc.scalar.activation(W[:, b, 0:nk * P], src, ACT.Exp, bias=m[:, b, 1:2], scale=f, accum_out=m[:, b, 2:3]).then_inc(exped.sem, 1)

            def take(i):
                nk = work[i][1][2]
                act.wait_ge(turned.sem, turned.base + i + 1)
                if i >= 2:
                    act.wait_ge(out_done.sem, out_done.base + i - 1)
                n = nk * P // 2
                nc.scalar.activation(WT[:, i % 2, n:2 * n], K.psum[:, 5, 0:n], ACT.Copy).then_inc(evac_a.sem, 1)

            exp(0)
            for i in range(len(work)):
                if i + 1 < len(work):
                    exp(i + 1)
                take(i)

        if table is not None:
            @block.sync
            def _(sp):
                for h in range(n_heads):
                    if h >= 2:
                        sp.wait_ge(maxed.sem, maxed.base + (h - 1) * nq)
                    sp.dma_start(table[:, h % 2, :, :], table_src[h].rearrange("p (m c) -> p m c", c=64)).then_inc(t_in[h % 2].sem, 16)
    for c in (scores, maxed, exped, normed, turned, evac_v, evac_a, out_done, out_used):
        c.rise(len(work))
    if table is not None:
        copied.rise(len(work))
        for c in t_in:
            c.rise(8 * n_heads)


def mla(K, B, ctx, H, A):
    nc = K.nc
    za = K.sb(ctx, "mla_out", [P, 4, TOK])
    both = (LAT, CTXG)
    with ExitStack() as tmp:
        lat = K.sb(tmp, "mla_lat", [P, 8, TOK])
        kb = K.sb(tmp, "mla_k", [96, A_HEADS, TOK])
        krope = kb[64:96, 0, :]
        units = linear_units([0, 1], KT, H, both, lambda e, g: ("vector", copy_to(lat[:, e, span(g)])))
        for g in both:
            units.append((2, 64, 32, g[1], lambda w, g=g: [(w[:, k, :], H[:, k, span(g)]) for k in range(KT)], "vector",
                          copy_to(krope[:, span(g)])))
        units += [(3,) + u[1:] for u in linear_units([0], KT, H, both, lambda e, g: ("scalar", act_to(nc, za[:, e, span(g)], ACT.Silu)))]
        products(K, "mla_in", units)

        def apply(dve, r, arg):
            g, a, n, gain = arg
            for k in range(n):
                i = dve.scalar_tensor_tensor(lat[:, a + k, span(g)], lat[:, a + k, span(g)], B.col(gain)[:, k:k + 1], r, ALU.mult, ALU.mult)
            return i
        norms(K, [([lat[:, k, span(g)] for k in range(6)], (g, 0, 6, "q_norm")) for g in both], B.const("ones"), 1.0 / Q_LORA, B.eps(0), apply)
        norms(K, [([lat[:, 6 + k, span(g)] for k in range(2)], (g, 6, 2, "kv_norm")) for g in both], B.const("ones"), 1.0 / KV_LORA, B.eps(0), apply)

        qb = H
        v = K.sb(tmp, "mla_v", [P, TOK // P, 512])
        units = []
        for h in range(A_HEADS):
            for g in both:
                units.append((h // 4, 0, 96, g[1], lambda w, h=h, g=g: [(w[:, k, (h % 4) * 96:(h % 4 + 1) * 96], lat[:, k, span(g)]) for k in range(6)],
                              ("vector", "scalar")[h % 2], copy_to(qb[0:96, h, span(g)]) if h % 2 == 0 else act_to(nc, qb[0:96, h, span(g)], ACT.Copy)))
        products(K, "q_up", units)
        units = []
        for h in range(A_HEADS):
            for g in both:
                units.append((0, 0, 64, g[1], lambda w, h=h, g=g: [(w[:, k, h * 128:h * 128 + 64], lat[:, 6 + k, span(g)]) for k in range(2)],
                              ("vector", "scalar")[h % 2], copy_to(kb[0:64, h, span(g)]) if h % 2 == 0 else act_to(nc, kb[0:64, h, span(g)], ACT.Copy)))
        for t in range(TOK // P):
            units.append((0, 0, P, 512, lambda w, t=t: [(lat[:, 6 + k, t * P:(t + 1) * P],
                                                         w[:, k, :].rearrange("p (h c) -> p h c", c=128)[:, :, 64:128]) for k in range(2)],
                          "vector", copy_to(v[:, t, :])))
        products(K, "kv_up", units)

        def spread(pool):
            for h in range(1, A_HEADS):
                i = pool.tensor_copy(kb[64:96, h, :], krope)
        one_engine(K, "gpsimd", spread)

        def apply_head(dve, r, arg):
            x, gain = arg
            return dve.scalar_tensor_tensor(x, x, B.col(gain)[0:96, 0:1], r, ALU.mult, ALU.mult)
        norms(K, [([x[0:96, h, span(g)]], (x[0:96, h, span(g)], gain)) for x, gain in ((qb, "q_gain"), (kb, "k_gain")) for h in range(A_HEADS) for g in both],
              B.const("ones")[0:96, 0:96], 1.0 / A_QK, B.eps(0)[0:96, :], apply_head)

        rot = lat[0:96, 0:2, 0:SEQ]
        table = lat[:, 2:4, :].rearrange("p a t -> p (a t)")[:, 0:2 * SEQ + P]
        loaded = K.count("setup_loaded")
        with nc.Block() as block:
            @block.sync
            def _(sp):
                sp.dma_start(table, A["tables"][:, 0:2 * SEQ + P]).then_inc(loaded.sem, 16)
                sp.wait_ge(loaded.sem, loaded.base + 16)
        loaded.rise(16)
        units = []
        for n, (x, h) in enumerate([(x, h) for x in (qb, kb) for h in range(A_HEADS)]):
            def turn(eng, _, ps, x=x, h=h, n=n):
                t = x[64:96, h, 0:SEQ]
                eng.tensor_tensor(rot[64:96, n % 2, :], ps[64:96, :], table[64:96, SEQ:2 * SEQ], ALU.mult)
                eng.tensor_tensor(t, t, table[64:96, 0:SEQ], ALU.mult).then_inc(K.dve_step.sem, 1)
                eng.wait_ge(K.dve_step.sem, K.dve_step.next())
                return eng.tensor_tensor(t, t, rot[64:96, n % 2, :], ALU.add)
            units.append((None, 0, 96, SEQ, lambda w, x=x, h=h: [(table[0:96, 2 * SEQ:2 * SEQ + 96], x[0:96, h, 0:SEQ])], "vector", turn))
        products(K, "", units)
        with ExitStack() as att:
            tiles = [(q * P, 0, 6) for q in range(4)] + [(SEQ + q * P, 4, 2) for q in range(2)]
            attention(K, B, att, "mla", A_HEADS, tiles, lambda h: qb[0:96, h, :], lambda h: kb[0:96, h, :],
                      lambda h, t: v[:, t, h * 64:(h + 1) * 64],
                      lambda h, s: za[(h % 2) * 64:(h % 2) * 64 + 64, h // 2, s], float(A_QK) ** -0.5, K.sb(att, "attention", [P, 6, TOK]))
    return za


def residual_units(K, B, layer, tiles, kt, src_of, groups):
    units = []
    for t in tiles:
        for e in range(4):
            for c, g in groups:
                ch = 4 * t + e
                def f(eng, _, ps, ch=ch, c=c, g=g):
                    return eng.scalar_tensor_tensor(B.x(ch, g), ps, B.mod[:, layer, 16 + ch, c:c + 1], B.x(ch, g), ALU.mult, ALU.add)
                units.append((t, 0, P, g[1], lambda w, e=e, g=g: [(w[:, k, e * P:(e + 1) * P], src_of(k)[:, span(g)]) for k in range(kt)], "vector", f))
    return units


def odd_layer(K, B, A):
    nc = K.nc
    both = (LAT, CTXG)
    with ExitStack() as ctx:
        H = K.sb(ctx, "h", [P, KT, TOK])
        products(K, "modulation1", modulation_units(K, nc, B, 1, 6))
        modulated_norm(K, B, 1, H)
        q, k = K.sb(ctx, "od_q", [P, KT, SEQ]), K.sb(ctx, "od_k", [P, KT, TOK])
        v, z = K.sb(ctx, "od_v", [P, TOK // P, D]), K.sb(ctx, "od_z", [P, KT, SEQ])
        units = linear_units([0, 1], KT, H, (LAT,), lambda e, g: ("vector", copy_to(q[:, e, :])))
        units += linear_units([2, 3], KT, H, both, lambda e, g: ("vector", copy_to(k[:, e - 8, span(g)])))
        for c in range(2):
            for t in range(TOK // P):
                units.append((4 + c, 0, P, 512, lambda w, t=t: [(H[:, j, t * P:(t + 1) * P], w[:, j, :]) for j in range(KT)],
                              "vector", copy_to(v[:, t, c * 512:(c + 1) * 512])))
        units += linear_units([6, 7], KT, H, (LAT,), lambda e, g: ("scalar", act_to(nc, z[:, e - 24, :], ACT.Silu)))
        products(K, "od_in", units)

        def apply(dve, r, arg):
            x, gain = arg
            return dve.scalar_tensor_tensor(x, x, B.col(gain), r, ALU.mult, ALU.mult)
        norms(K, [([q[:, e, :]], (q[:, e, :], "od_q_gain")) for e in range(KT)] +
              [([k[:, e, span(g)]], (k[:, e, span(g)], "od_k_gain")) for e in range(KT) for g in both],
              B.const("ones64"), 1.0 / 64, B.eps(0), apply)
        table = K.sb(ctx, "bias_table", [P, 2, 14, 64])
        rows = lambda h: slice(64 * (h % 2), 64 * (h % 2) + 64)
        attention(K, B, ctx, "od", C_HEADS, [(i * P, 0, 6) for i in range(4)], lambda h: q[rows(h), h // 2, :], lambda h: k[rows(h), h // 2, :],
                  lambda h, t: v[:, t, h * 64:(h + 1) * 64], lambda h, s: z[rows(h), h // 2, s], 0.125, H, table, A["bias"])
        products(K, "od_out", residual_units(K, B, 1, [0, 1], KT, lambda j: z[:, j, :], [(0, LAT)]))


def conv_mixer(K, B, A, layer, G):
    nc = K.nc
    j = layer // 3
    dve_done, act_done = K.count("vector_freed"), K.count("scalar_freed")
    with ExitStack() as ctx:
        cg = K.sb(ctx, "conv_cg", [P, SEQ])
        u = K.sb(ctx, "conv_u", [P, SEQ + 2])
        acc = K.sb(ctx, "conv_sum", [P, SEQ])
        sz = K.sb(ctx, "conv_z", [P, 2, SEQ])
        one_engine(K, "vector", lambda dve: dve.memset(u[:, 0:2], 0.0))
        units = []
        for e in range(KT):
            tap = [B.col("conv_k")[:, 24 * j + 8 * i + e:24 * j + 8 * i + e + 1] for i in range(3)]

            def take_cg(eng, _, ps, e=e):
                if e:
                    eng.wait_ge(dve_done.sem, dve_done.base + 3 * e)
                return eng.tensor_copy(cg[:, :], ps)

            def take_h(eng, _, ps, e=e, tap=tap):
                eng.wait_ge(dve_done.sem, dve_done.base + 3 * e + 1)
                eng.tensor_tensor(u[:, 2:SEQ + 2], ps, cg[:, :], ALU.mult).then_inc(K.dve_step.sem, 1)
                eng.wait_ge(K.dve_step.sem, K.dve_step.next())
                eng.tensor_scalar(acc[:, :], u[:, 2:SEQ + 2], tap[2], None, ALU.mult).then_inc(K.dve_step.sem, 1)
                eng.wait_ge(K.dve_step.sem, K.dve_step.next())
                eng.scalar_tensor_tensor(acc[:, :], u[:, 1:SEQ + 1], tap[1], acc[:, :], ALU.mult, ALU.add).then_inc(K.dve_step.sem, 1)
                eng.wait_ge(K.dve_step.sem, K.dve_step.next())
                return eng.scalar_tensor_tensor(acc[:, :], u[:, 0:SEQ], tap[0], acc[:, :], ALU.mult, ALU.add)

            def take_z(eng, _, ps, e=e):
                if e >= 2:
                    eng.wait_ge(dve_done.sem, dve_done.base + 3 * (e - 1))
                return nc.scalar.activation(sz[:, e % 2, :], ps, ACT.Silu)

            def take_bg(eng, _, ps, e=e):
                eng.wait_ge(dve_done.sem, dve_done.base + 3 * e + 2)
                eng.tensor_tensor(acc[:, :], ps, acc[:, :], ALU.mult).then_inc(K.dve_step.sem, 1)
                eng.wait_ge(K.dve_step.sem, K.dve_step.next())
                eng.wait_ge(act_done.sem, act_done.base + e + 1)
                return eng.tensor_tensor(G[:, e, :], acc[:, :], sz[:, e % 2, :], ALU.mult)
            for s, (engine, f) in enumerate((("vector", take_cg), ("vector", take_h), ("scalar", take_z), ("vector", take_bg))):
                units.append((e, 0, P, SEQ, lambda w, s=s: [(w[:, k, s * P:(s + 1) * P], B.X[:, k, 0:SEQ]) for k in range(KT)], engine, f))
        products(K, f"conv_in{layer}", units)


def ssm_mixer(K, B, A, G):
    nc = K.nc
    PI2, MAGIC = 6.2831850, 12582912.0
    with ExitStack() as ctx:
        U = K.sb(ctx, "ssm_u", [P, KT, SEQ])
        Y = K.sb(ctx, "ssm_y", [P, KT, SEQ])
        units = linear_units([0, 1], KT, B.X, (LAT,), lambda e, g: ("vector", copy_to(U[:, e, :])))
        units += linear_units([2, 3], KT, B.X, (LAT,), lambda e, g: ("scalar", act_to(nc, G[:, e - 8, :], ACT.Silu)))
        products(K, "ssm_in", units)
        NP = GROUPS // 2
        with ExitStack() as tmp:
            time = K.sb(tmp, "time", [P, SEQ])
            bw = K.sb(tmp, "ssm_b", [P, 2, KT, P])
            cw = K.sb(tmp, "ssm_c", [P, 2, NP, 32])
            cs = K.sb(tmp, "ssm_c_scaled", [P, 3, NP, 32])
            s = K.sb(tmp, "ssm_scalars", [P, 14, NP])
            dt, mag, turn, sn, csn, ar, ai, inv, cr, ci, t0, t1, xr, rnd = (s[:, i, :] for i in range(14))
            loaded, a1, v1 = K.count("setup_loaded"), K.count("scalar_part"), K.count("vector_part")
            with nc.Block() as block:
                @block.sync
                def _(sp):
                    sp.dma_start(time[:, :], A["tables"][:, 2 * SEQ + P:3 * SEQ + P]).then_inc(loaded.sem, 16)
                    for i, n in enumerate(("ssm_b_re_2", "ssm_b_im_2")):
                        sp.dma_start(bw[:, i, :, :], A[n].rearrange("k p m -> p k m")).then_inc(loaded.sem, 16)
                    for i, n in enumerate(("ssm_c_re_2", "ssm_c_im_2")):
                        sp.dma_start(cw[:, i, :, :], A[n]).then_inc(loaded.sem, 16)
                    sp.wait_ge(loaded.sem, loaded.base + 80)

                @block.scalar
                def _(act):
                    nc.scalar.activation(dt, B.col("log_dt"), ACT.Exp).then_inc(a1.sem, 1)
                    act.wait_ge(v1.sem, v1.base + 1)
                    nc.scalar.activation(mag, xr, ACT.Exp).then_inc(a1.sem, 1)
                    act.wait_ge(v1.sem, v1.base + 2)
                    nc.scalar.activation(sn, turn, ACT.Sin, scale=PI2)
                    nc.scalar.activation(csn, t0, ACT.Sin, scale=PI2).then_inc(a1.sem, 1)

                @block.vector
                def _(dve):

                    def wrap(dst, x):
                        dve.tensor_scalar(rnd, x, MAGIC, MAGIC, ALU.add, ALU.subtract).then_inc(K.dve_step.sem, 1)
                        dve.wait_ge(K.dve_step.sem, K.dve_step.next())
                        dve.tensor_tensor(dst, x, rnd, ALU.subtract).then_inc(K.dve_step.sem, 1)
                        dve.wait_ge(K.dve_step.sem, K.dve_step.next())
                    dve.wait_ge(a1.sem, a1.base + 1)
                    dve.tensor_tensor(xr, B.col("lam_re"), dt, ALU.mult).then_inc(v1.sem, 1)
                    dve.tensor_tensor(t1, B.col("lam_im"), dt, ALU.mult).then_inc(K.dve_step.sem, 1)
                    dve.wait_ge(K.dve_step.sem, K.dve_step.next())
                    dve.tensor_scalar(t1, t1, 0.15915494309189535, None, ALU.mult).then_inc(K.dve_step.sem, 1)
                    dve.wait_ge(K.dve_step.sem, K.dve_step.next())
                    wrap(turn, t1)
                    dve.tensor_scalar(t1, turn, 0.25, None, ALU.add).then_inc(K.dve_step.sem, 1)
                    dve.wait_ge(K.dve_step.sem, K.dve_step.next())
                    dve.tensor_scalar(rnd, t1, MAGIC, MAGIC, ALU.add, ALU.subtract).then_inc(K.dve_step.sem, 1)
                    dve.wait_ge(K.dve_step.sem, K.dve_step.next())
                    dve.tensor_tensor(t0, t1, rnd, ALU.subtract).then_inc(v1.sem, 1)
                    dve.wait_ge(a1.sem, a1.base + 3)
                    dve.tensor_tensor(ar, mag, csn, ALU.mult).then_inc(K.dve_step.sem, 1)
                    dve.wait_ge(K.dve_step.sem, K.dve_step.next())
                    dve.tensor_tensor(ai, mag, sn, ALU.mult).then_inc(K.dve_step.sem, 1)
                    dve.wait_ge(K.dve_step.sem, K.dve_step.next())
                    dve.tensor_scalar(ar, ar, -1.0, None, ALU.add).then_inc(K.dve_step.sem, 1)
                    dve.wait_ge(K.dve_step.sem, K.dve_step.next())
                    lr, li = B.col("lam_re"), B.col("lam_im")
                    dve.tensor_tensor(t0, lr, lr, ALU.mult).then_inc(K.dve_step.sem, 1)
                    dve.wait_ge(K.dve_step.sem, K.dve_step.next())
                    dve.tensor_tensor(t1, li, li, ALU.mult).then_inc(K.dve_step.sem, 1)
                    dve.wait_ge(K.dve_step.sem, K.dve_step.next())
                    dve.tensor_tensor(t0, t0, t1, ALU.add).then_inc(K.dve_step.sem, 1)
                    dve.wait_ge(K.dve_step.sem, K.dve_step.next())
                    dve.reciprocal(inv, t0).then_inc(K.dve_step.sem, 1)
                    dve.wait_ge(K.dve_step.sem, K.dve_step.next())
                    dve.tensor_tensor(t0, ar, lr, ALU.mult).then_inc(K.dve_step.sem, 1)
                    dve.wait_ge(K.dve_step.sem, K.dve_step.next())
                    dve.tensor_tensor(t1, ai, li, ALU.mult).then_inc(K.dve_step.sem, 1)
                    dve.wait_ge(K.dve_step.sem, K.dve_step.next())
                    dve.tensor_tensor(t0, t0, t1, ALU.add).then_inc(K.dve_step.sem, 1)
                    dve.wait_ge(K.dve_step.sem, K.dve_step.next())
                    dve.tensor_tensor(cr, t0, inv, ALU.mult).then_inc(K.dve_step.sem, 1)
                    dve.wait_ge(K.dve_step.sem, K.dve_step.next())
                    dve.tensor_tensor(t0, ai, lr, ALU.mult).then_inc(K.dve_step.sem, 1)
                    dve.wait_ge(K.dve_step.sem, K.dve_step.next())
                    dve.tensor_tensor(t1, ar, li, ALU.mult).then_inc(K.dve_step.sem, 1)
                    dve.wait_ge(K.dve_step.sem, K.dve_step.next())
                    dve.tensor_tensor(t0, t0, t1, ALU.subtract).then_inc(K.dve_step.sem, 1)
                    dve.wait_ge(K.dve_step.sem, K.dve_step.next())
                    dve.tensor_tensor(ci, t0, inv, ALU.mult).then_inc(K.dve_step.sem, 1)
                    dve.wait_ge(K.dve_step.sem, K.dve_step.next())
                    dve.wait_ge(loaded.sem, loaded.base + 80)
                    crb, cib = (x.unsqueeze(2).to_broadcast([P, NP, 32]) for x in (cr, ci))
                    dve.tensor_tensor(cs[:, 0, :, :], cw[:, 0, :, :], crb, ALU.mult).then_inc(K.dve_step.sem, 1)
                    dve.wait_ge(K.dve_step.sem, K.dve_step.next())
                    dve.tensor_tensor(cs[:, 1, :, :], cw[:, 1, :, :], cib, ALU.mult).then_inc(K.dve_step.sem, 1)
                    dve.wait_ge(K.dve_step.sem, K.dve_step.next())
                    dve.tensor_tensor(cs[:, 0, :, :], cs[:, 0, :, :], cs[:, 1, :, :], ALU.subtract).then_inc(K.dve_step.sem, 1)
                    dve.wait_ge(K.dve_step.sem, K.dve_step.next())
                    dve.tensor_scalar(cs[:, 1, :, :], cs[:, 0, :, :], -1.0, None, ALU.mult).then_inc(K.dve_step.sem, 1)
                    dve.wait_ge(K.dve_step.sem, K.dve_step.next())
                    dve.tensor_tensor(cw[:, 0, :, :], cw[:, 0, :, :], cib, ALU.mult).then_inc(K.dve_step.sem, 1)
                    dve.wait_ge(K.dve_step.sem, K.dve_step.next())
                    dve.tensor_tensor(cw[:, 1, :, :], cw[:, 1, :, :], crb, ALU.mult).then_inc(K.dve_step.sem, 1)
                    dve.wait_ge(K.dve_step.sem, K.dve_step.next())
                    dve.tensor_tensor(cw[:, 0, :, :], cw[:, 0, :, :], cw[:, 1, :, :], ALU.add).then_inc(K.dve_step.sem, 1)
                    dve.wait_ge(K.dve_step.sem, K.dve_step.next())
                    dve.tensor_scalar(cs[:, 2, :, :], cw[:, 0, :, :], -1.0, None, ALU.mult).then_inc(K.dve_step.sem, 1)
                    dve.wait_ge(K.dve_step.sem, K.dve_step.next())
            loaded.rise(80)
            a1.rise(3)
            v1.rise(2)

            ph = K.sb(tmp, "ssm_phase", [P, 2, 3, SEQ])
            tb = K.sb(tmp, "ssm_table", [P, 2, 2, SEQ])
            bu = K.sb(tmp, "ssm_bu", [P, 2, 2, SEQ])
            w = K.sb(tmp, "ssm_turned", [P, 4, SEQ])
            zz = K.sb(tmp, "ssm_scan", [P, 2, 2, SEQ])
            mm = K.sb(tmp, "ssm_products", [P, 2, 4, SEQ])
            bu_done, bu_taken, tables, phases, scanned, prod_v, prod_p, y_done, y_taken = (K.count(x) for x in (
                "product_done", "scalar_freed", "scalar_part", "pool_part", "vector_part", "vector_freed", "pool_freed", "sum_done", "root_used"))
            turned = K.count("turned")
            with nc.Block() as block:
                @block.tensor
                def _(pe):
                    def bring(q):
                        r = slice(32 * (q % 4), 32 * (q % 4) + 32)
                        if q >= 2:
                            pe.wait_ge(bu_taken.sem, bu_taken.base + q - 1)
                        for i in range(2):
                            x = nc.tensor.matmul(K.psum[:, 2 * (q % 2) + i, :], bw[r, i, q // 4, :], U[r, q // 4, :], start=True, stop=True,
                                                 tile_position=(32 * (q % 4), 0))
                        x.then_inc(bu_done.sem, 1)
                    bring(0)
                    for q in range(NP):
                        if q + 1 < NP:
                            bring(q + 1)
                        if q % 4 == 0 and q >= 8:
                            pe.wait_ge(y_taken.sem, y_taken.base + q // 4 - 1)
                        pe.wait_ge(prod_v.sem, prod_v.base + q + 1)
                        pe.wait_ge(prod_p.sem, prod_p.base + q + 1)
                        o = K.psum[32 * (q % 4):32 * (q % 4) + 32, 4 + q // 4 % 2, :]
                        for n, c in enumerate((0, 1, 2, 2)):
                            x = nc.tensor.matmul(o, cs[:, c, q, :], mm[:, q % 2, n, :], start=n == 0, stop=n == 3, tile_position=(0, 32 * (q % 4)))
                        x.then_inc(y_done.sem, 1)

                @block.gpsimd
                def _(pool):

                    def phase(q):
                        a, c, t = (ph[:, q % 2, i, :] for i in range(3))
                        if q >= 2:
                            pool.wait_ge(tables.sem, tables.base + q - 1)
                        pool.tensor_scalar(a, time[:, :], turn[:, q:q + 1], None, ALU.mult).then_inc(K.pool_step.sem, 1)
                        pool.wait_ge(K.pool_step.sem, K.pool_step.next())
                        pool.tensor_scalar(t, a, MAGIC, MAGIC, ALU.add, ALU.subtract).then_inc(K.pool_step.sem, 1)
                        pool.wait_ge(K.pool_step.sem, K.pool_step.next())
                        pool.tensor_tensor(a, a, t, ALU.subtract).then_inc(K.pool_step.sem, 1)
                        pool.wait_ge(K.pool_step.sem, K.pool_step.next())
                        pool.tensor_scalar(c, a, 0.25, None, ALU.add).then_inc(K.pool_step.sem, 1)
                        pool.wait_ge(K.pool_step.sem, K.pool_step.next())
                        pool.tensor_scalar(t, c, MAGIC, MAGIC, ALU.add, ALU.subtract).then_inc(K.pool_step.sem, 1)
                        pool.wait_ge(K.pool_step.sem, K.pool_step.next())
                        pool.tensor_tensor(c, c, t, ALU.subtract).then_inc(phases.sem, 1)

                    def finish(q):
                        pool.wait_ge(scanned.sem, scanned.base + q + 1)
                        if q >= 2:
                            pool.wait_ge(y_done.sem, y_done.base + q - 1)
                        pool.tensor_tensor(mm[:, q % 2, 2, :], tb[:, q % 2, 0, :], zz[:, q % 2, 0, :], ALU.mult)
                        pool.tensor_tensor(mm[:, q % 2, 3, :], tb[:, q % 2, 1, :], zz[:, q % 2, 1, :], ALU.mult).then_inc(prod_p.sem, 1)
                    phase(0)
                    for q in range(NP):
                        if q + 1 < NP:
                            phase(q + 1)
                        finish(q)

                @block.scalar
                def _(act):
                    for q in range(NP):
                        if q >= 2:
                            act.wait_ge(prod_v.sem, prod_v.base + q - 1)
                            act.wait_ge(prod_p.sem, prod_p.base + q - 1)
                            act.wait_ge(turned.sem, turned.base + q - 1)
                        act.wait_ge(bu_done.sem, bu_done.base + q + 1)
                        for i in range(2):
                            x = nc.scalar.activation(bu[:, q % 2, i, :], K.psum[:, 2 * (q % 2) + i, :], ACT.Copy)
                        x.then_inc(bu_taken.sem, 1)
                        act.wait_ge(phases.sem, phases.base + q + 1)
                        nc.scalar.activation(tb[:, q % 2, 0, :], ph[:, q % 2, 0, :], ACT.Sin, scale=PI2)
                        nc.scalar.activation(tb[:, q % 2, 1, :], ph[:, q % 2, 1, :], ACT.Sin, scale=PI2).then_inc(tables.sem, 1)

                @block.vector
                def _(dve):
                    for q in range(NP):
                        re, im, sn_, cs_ = bu[:, q % 2, 0, :], bu[:, q % 2, 1, :], tb[:, q % 2, 0, :], tb[:, q % 2, 1, :]
                        dve.wait_ge(bu_taken.sem, bu_taken.base + q + 1)
                        dve.wait_ge(tables.sem, tables.base + q + 1)
                        dve.tensor_tensor(w[:, 0, :], re, cs_, ALU.mult)
                        dve.tensor_tensor(w[:, 1, :], im, sn_, ALU.mult)
                        dve.tensor_tensor(w[:, 2, :], im, cs_, ALU.mult)
                        dve.tensor_tensor(w[:, 3, :], re, sn_, ALU.mult).then_inc(turned.sem, 1)
                        dve.wait_ge(turned.sem, turned.base + q + 1)
                        dve.tensor_tensor(w[:, 0, :], w[:, 0, :], w[:, 1, :], ALU.add)
                        dve.tensor_tensor(w[:, 2, :], w[:, 2, :], w[:, 3, :], ALU.subtract).then_inc(K.dve_step.sem, 1)
                        dve.wait_ge(K.dve_step.sem, K.dve_step.next())
                        if q >= 2:
                            dve.wait_ge(prod_p.sem, prod_p.base + q - 1)
                            dve.wait_ge(prod_v.sem, prod_v.base + q - 1)
                            dve.wait_ge(y_done.sem, y_done.base + q - 1)
                        r = mag[:, q:q + 1].to_broadcast([P, SEQ])
                        dve.tensor_tensor_scan(zz[:, q % 2, 0, :], r, w[:, 0, :], 0.0, ALU.mult, ALU.add)
                        dve.tensor_tensor_scan(zz[:, q % 2, 1, :], r, w[:, 2, :], 0.0, ALU.mult, ALU.add).then_inc(scanned.sem, 1)
                        dve.wait_ge(scanned.sem, scanned.base + q + 1)
                        dve.tensor_tensor(mm[:, q % 2, 0, :], cs_, zz[:, q % 2, 0, :], ALU.mult)
                        dve.tensor_tensor(mm[:, q % 2, 1, :], sn_, zz[:, q % 2, 1, :], ALU.mult).then_inc(prod_v.sem, 1)
                        if q % 4 == 3:
                            j = q // 4
                            dve.wait_ge(y_done.sem, y_done.base + q + 1)
                            dve.scalar_tensor_tensor(Y[:, j, :], U[:, j, :], B.col("d_skip")[:, j:j + 1], K.psum[:, 4 + j % 2, :],
                                                     ALU.mult, ALU.add).then_inc(y_taken.sem, 1)
            for c in (bu_done, bu_taken, tables, phases, scanned, prod_v, prod_p, y_done, turned):
                c.rise(NP)
            y_taken.rise(KT)
        B.dump("ssm_y", Y[:, :, :])

        gelued = K.count("scalar_part")
        with nc.Block() as block:
            @block.scalar
            def _(act):
                for e in range(KT):
                    nc.scalar.activation(Y[:, e, :], Y[:, e, :], ACT.Gelu_apprx_tanh).then_inc(gelued.sem, 1)

            @block.vector
            def _(dve):
                for e in range(KT):
                    dve.wait_ge(gelued.sem, gelued.base + e + 1)
                    dve.tensor_tensor(G[:, e, :], G[:, e, :], Y[:, e, :], ALU.mult)
        gelued.rise(KT)
        taken = K.count("scalar_freed")

        def sigm(e, g):
            def f(eng, _, ps):
                return nc.scalar.activation(U[:, e, :], ps, ACT.Sigmoid, bias=B.col("b_glu")[:, e:e + 1])
            return "scalar", f

        def beside(dve):
            for e in range(KT):
                dve.wait_ge(taken.sem, taken.base + e + 1)
                dve.tensor_tensor(G[:, e, :], G[:, e, :], U[:, e, :], ALU.mult)
        products(K, "ssm_glu", linear_units([0, 1], KT, Y, (LAT,), sigm), beside)


def rwkv_mixer(K, B, A, G):
    nc = K.nc
    NC, HP = SEQ // CH, 4
    with ExitStack() as ctx:
        w2 = K.sb(ctx, "lora_w2", [64, 2, D])
        low = K.sb(ctx, "lora_low", [64, 2, SEQ])
        r, k, v, a, w = (K.sb(ctx, "rwkv_" + n, [P, HP, SEQ]) for n in "rkvaw")
        loaded = K.count("setup_loaded")
        taken = K.count("scalar_freed")

        def lerp(n, dx, xs, first=False):
            def f(dve):
                if first:
                    dve.tensor_scalar(dx[:, :, 0:1], B.X[:, :, 0:1], -1.0, None, ALU.mult).then_inc(K.dve_step.sem, 1)
                    dve.wait_ge(K.dve_step.sem, K.dve_step.next())
                    dve.tensor_tensor(dx[:, :, 1:SEQ], B.X[:, :, 0:SEQ - 1], B.X[:, :, 1:SEQ], ALU.subtract).then_inc(K.dve_step.sem, 1)
                    dve.wait_ge(K.dve_step.sem, K.dve_step.next())
                for e in range(KT):
                    c = 8 * n + e
                    dve.scalar_tensor_tensor(xs[:, e, :], dx[:, e, :], B.col("mu")[:, c:c + 1], B.X[:, e, 0:SEQ], ALU.mult, ALU.add)
            one_engine(K, "vector", f)

        def lora_in(name, n, xs, func):
            units = [(0, 0, 64, SEQ, lambda s: [(s[:, j, :], xs[:, j, :]) for j in range(KT)], "scalar", act_to(nc, low[:, n, :], func))]
            products(K, name, units)

        for half in range(2):
            tile0 = 4 * half
            with ExitStack() as pro:
                dx, xs = K.sb(pro, "dx", [P, KT, SEQ]), K.sb(pro, "xs", [P, KT, SEQ])
                if half == 0:
                    with nc.Block() as block:
                        @block.sync
                        def _(sp):
                            sp.dma_start(w2[:, 0, :], A["rwkv_w2_2"][0]).then_inc(loaded.sem, 16)
                            sp.dma_start(w2[:, 1, :], A["rwkv_a2_2"][0]).then_inc(loaded.sem, 16)
                            sp.wait_ge(loaded.sem, loaded.base + 32)
                    loaded.rise(32)
                    lerp(4, dx, xs, True)
                    lora_in("rwkv_w", 0, xs, ACT.Tanh)
                    lerp(5, dx, xs)
                    lora_in("rwkv_a", 1, xs, ACT.Copy)
                    lerp(3, dx, xs)
                    products(K, "rwkv_z", linear_units([0, 1], KT, xs, (LAT,), lambda e, g: ("scalar", act_to(nc, G[:, e, :], ACT.Silu))))
                for n, (m, dst) in enumerate(zip("rkv", (r, k, v))):
                    lerp(n, dx, xs, half == 1 and n == 0)
                    products(K, f"rwkv_{m}{half}", linear_units([0], KT, xs, (LAT,), lambda e, g, dst=dst: ("vector", copy_to(dst[:, e, :]))))
            units = []
            for n, (dst, bias) in enumerate(((w, "w0"), (a, "a0"))):
                for e in range(HP):
                    def f(eng, _, ps, dst=dst, bias=bias, e=e):
                        return nc.scalar.activation(dst[:, e, :], ps, ACT.Sigmoid, bias=B.col(bias)[:, tile0 + e:tile0 + e + 1])
                    c = (tile0 + e) * P
                    units.append((None, 0, P, SEQ, lambda s, n=n, c=c: [(w2[:, n, c:c + P], low[:, n, :])], "scalar", f))
            products(K, "", units)
            with ExitStack() as tmp:
                rwkv_chunks(K, B, tmp, half, r, k, v, a, w, G)


def rwkv_chunks(K, B, ctx, half, r, k, v, a, w, G):
    nc = K.nc
    NC, HP, tile0 = SEQ // CH, 4, 4 * half
    col = lambda n, e: B.col(n)[:, tile0 + e:tile0 + e + 1]
    O = K.sb(ctx, "rwkv_out", [P, HP, SEQ])
    kk = K.sb(ctx, "rwkv_kk", [P, HP, SEQ])
    pend = K.sb(ctx, "rwkv_end", [P, HP, NC])
    flat = lambda x: x.rearrange("p e t -> p (e t)")
    decay = -0.6065306597126334
    inner = ExitStack()
    ex = K.sb(inner, "rwkv_exp", [P, 3, HP, SEQ])

    def prepare(dve):
        for e in range(HP):
            dve.tensor_scalar(kk[:, e, :], k[:, e, :], col("k_k", e), None, ALU.mult).then_inc(K.dve_step.sem, 1)
            dve.wait_ge(K.dve_step.sem, K.dve_step.next())
            dve.tensor_scalar(ex[:, 0, e, :], a[:, e, :], -1.0, col("k_a", e), ALU.add, ALU.mult).then_inc(K.dve_step.sem, 1)
            dve.wait_ge(K.dve_step.sem, K.dve_step.next())
            dve.scalar_tensor_tensor(k[:, e, :], ex[:, 0, e, :], 1.0, k[:, e, :], ALU.add, ALU.mult).then_inc(K.dve_step.sem, 1)
            dve.wait_ge(K.dve_step.sem, K.dve_step.next())
            dve.scalar_tensor_tensor(O[:, e, :], r[:, e, :], col("r_k", e), k[:, e, :], ALU.mult, ALU.mult).then_inc(K.dve_step.sem, 1)
            dve.wait_ge(K.dve_step.sem, K.dve_step.next())
            dve.tensor_scalar(w[:, e, :], w[:, e, :], decay, None, ALU.mult).then_inc(K.dve_step.sem, 1)
            dve.wait_ge(K.dve_step.sem, K.dve_step.next())
            dve.tensor_tensor_scan(ex[:, 0, e, :], B.const("restart")[:, 0:SEQ], w[:, e, :], 0.0, ALU.mult, ALU.add).then_inc(K.dve_step.sem, 1)
            dve.wait_ge(K.dve_step.sem, K.dve_step.next())
        dve.tensor_copy(pend[:, :, :], ex[:, 0, :, :].rearrange("p e (c t) -> p e c t", t=CH)[:, :, :, CH - 1]).then_inc(K.dve_step.sem, 1)
        dve.wait_ge(K.dve_step.sem, K.dve_step.next())
        dve.tensor_tensor(flat(w[:, :, :]), flat(ex[:, 0, :, :]), flat(w[:, :, :]), ALU.subtract)
    one_engine(K, "vector", prepare)

    units = []
    for e in range(HP):
        def f(eng, _, ps, e=e):
            return eng.tensor_tensor(O[:, e, :], ps, v[:, e, :], ALU.mult)
        units.append((None, 0, P, SEQ, lambda s, e=e: [(B.const("ones64"), O[:, e, :])], "vector", f))
    products(K, "", units)

    def exps(act):
        cum = flat(ex[:, 0, :, :])
        nc.scalar.activation(flat(ex[:, 1, :, :]), cum, ACT.Exp)
        nc.scalar.activation(flat(ex[:, 2, :, :]), cum, ACT.Exp, scale=-1.0)
        nc.scalar.activation(flat(w[:, :, :]), flat(w[:, :, :]), ACT.Exp)
        nc.scalar.activation(pend.rearrange("p e c -> p (e c)"), pend.rearrange("p e c -> p (e c)"), ACT.Exp)
    one_engine(K, "scalar", exps)

    def apply(dve, rinv, e):
        dve.tensor_tensor(kk[:, e, :], kk[:, e, :], rinv, ALU.mult).then_inc(K.dve_step.sem, 1)
        dve.wait_ge(K.dve_step.sem, K.dve_step.next())
        dve.tensor_tensor(r[:, e, :], r[:, e, :], ex[:, 1, e, :], ALU.mult)
        dve.tensor_tensor(k[:, e, :], k[:, e, :], ex[:, 2, e, :], ALU.mult)
        dve.tensor_tensor(a[:, e, :], a[:, e, :], ex[:, 2, e, :], ALU.mult).then_inc(K.dve_step.sem, 1)
        dve.wait_ge(K.dve_step.sem, K.dve_step.next())
        dve.tensor_tensor(a[:, e, :], a[:, e, :], kk[:, e, :], ALU.mult)
        return dve.tensor_tensor(w[:, e, :], w[:, e, :], kk[:, e, :], ALU.mult)
    norms(K, [([kk[:, e, :]], e) for e in range(HP)], B.const("ones64"), 1.0, None, apply, "norm")
    inner.close()

    at, bt, kt, rt = w, a, k, r
    bT, RB, YT, XX, KV = (K.sb(ctx, "rwkv_" + n, [P, HP, NC, CH]) for n in ("bT", "rb", "yT", "x", "kv"))
    names = ("aT", "kT", "vT", "Bo", "AK", "RK", "Bi", "Ai", "B2", "A2", "GG")
    T = {n: K.sb(ctx, "rwkv_" + n, [P, NC, CH]) for n in names}
    T["R"], T["E"] = T["kT"], T["AK"]
    done, freed_v, freed_a = K.count("product_done"), K.count("vector_freed"), K.count("scalar_freed")
    chunk = lambda x, e: x[:, e, :].rearrange("p (c t) -> p c t", t=CH)
    eye = B.const("ident")

    def mask(n):
        return B.const(n).unsqueeze(1).to_broadcast([P, NC, CH])

    for e in range(HP):
        A_, B_, K_, R_, V_ = (chunk(x, e) for x in (at, bt, kt, rt, v))

        def masked(*pairs):
            def f(eng, ps):
                for n, (dst, m) in enumerate(pairs):
                    i = eng.tensor_tensor(dst, ps, mask(m), ALU.mult)
                return i
            return f
        keep = lambda dst: lambda eng, ps: eng.tensor_copy(dst, ps)
        plus = lambda dst, x: lambda eng, ps: eng.tensor_tensor(dst, ps, x, ALU.add)
        minus = lambda dst, x: lambda eng, ps: eng.scalar_tensor_tensor(dst, ps, -1.0, x, ALU.mult, ALU.add)
        t = {n: x[:, :, :] for n, x in T.items()}
        rounds = [
            [("I", A_, keep(t["aT"])), ("I", B_, keep(bT[:, e, :, :])), ("I", K_, keep(t["kT"])), ("I", V_, keep(t["vT"])),
             (B_, A_, masked((t["Bi"], "before_in"), (t["Bo"], "before_out"))), (A_, B_, masked((t["Ai"], "after_in"))),
             (K_, A_, masked((t["AK"], "before"))), (B_, R_, masked((RB[:, e, :, :], "upto")))],
            [(K_, R_, masked((t["RK"], "upto"))), (t["Ai"], t["Bi"], keep(t["B2"])), (t["Bi"], t["Ai"], keep(t["A2"])),
             (t["AK"], t["vT"], keep(t["GG"])), (t["kT"], t["vT"], keep(KV[:, e, :, :])), "start"],
            [(t["vT"], t["RK"], keep(chunk(kk, e))), (t["A2"], t["R"], plus(t["R"], t["R"])), (t["B2"], t["E"], plus(t["E"], t["E"])),
             (t["A2"], t["B2"], keep(t["Bi"])), (t["B2"], t["A2"], keep(t["Ai"]))],
            [(t["Ai"], t["R"], plus(t["R"], t["R"])), (t["Bi"], t["E"], plus(t["E"], t["E"])),
             (t["Ai"], t["Bi"], keep(t["B2"])), (t["Bi"], t["Ai"], keep(t["A2"]))],
            [(t["A2"], t["R"], plus(t["R"], t["R"])), (t["B2"], t["E"], plus(t["E"], t["E"]))],
            [(t["E"], t["Bo"], keep(t["Bi"])), (t["Bo"], t["E"], keep(t["Ai"]))],
            [(t["Bi"], t["Ai"], keep(t["A2"]))],
            [(t["A2"], t["R"], plus(t["R"], t["R"]))],
            [(t["Ai"], t["R"], minus(t["B2"], t["R"]))],
            [(t["B2"], t["GG"], keep(XX[:, e, :, :])), (t["aT"], t["B2"], keep(YT[:, e, :, :]))],
        ]
        for rnd in rounds:
            units = [u for u in rnd if u != "start"]
            with nc.Block() as block:
                @block.tensor
                def _(pe):
                    for i, (x, y, _) in enumerate(units):
                        for c in range(NC):
                            for h in range(2):
                                s = slice(64 * h, 64 * h + 64)
                                lhsT, rhs = (y[s, c, :], eye[s, s]) if isinstance(x, str) else (x[s, c, :], y[s, c, :])
                                mm = nc.tensor.matmul(K.psum[s, i, c * CH:(c + 1) * CH], lhsT, rhs, start=c == 0, stop=c == NC - 1,
                                                      skip_group_check=True)
                        mm.then_inc(done.sem, 1)

                @block.vector
                def _(dve):
                    for i, (_, _, take) in enumerate(units):
                        dve.wait_ge(done.sem, done.base + len(units))
                        take(dve, K.psum[:, i, :].rearrange("p (c t) -> p c t", t=CH))
                    if "start" in rnd:
                        dve.tensor_tensor(t["R"], mask("eye64"), t["Bi"], ALU.subtract)
                        dve.tensor_tensor(t["E"], mask("eye64"), t["Ai"], ALU.subtract)
            done.rise(len(units))

    two = lambda n: T[n][:, :, :].rearrange("p (a e) t -> p a e t", a=2)
    Hs, U, Hg = two("aT"), two("kT"), two("vT")[:, 0, :, :]
    uh, ud, od, hd, hs = (K.count(x) for x in ("product_done", "vector_part", "sum_done", "root_used", "vector_freed"))
    bank = lambda i: K.psum[:, i, 0:HP * CH].rearrange("p (e t) -> p e t", t=CH)
    with nc.Block() as block:
        @block.tensor
        def _(pe):
            def each(c, b, pairs, sem):
                for e in range(HP):
                    for h in range(2):
                        s = slice(64 * h, 64 * h + 64)
                        for n, (x, y) in enumerate(pairs):
                            mm = nc.tensor.matmul(bank(b)[s, e, :], x(s, e), y(s, e), start=n == 0 and e == 0, stop=n == len(pairs) - 1 and e == HP - 1,
                                                  skip_group_check=True)
                mm.then_inc(sem, 1)
            for c in range(NC):
                H, Uc = Hs[:, c % 2, :, :], U[:, c % 2, :, :]
                pe.wait_ge(hs.sem, hs.base + c + 1)
                if c >= 1:
                    pe.wait_ge(ud.sem, ud.base + c)
                each(c, 0, [(lambda s, e: YT[s, e, c, :], lambda s, e: H[s, e, :])], uh.sem)
                pe.wait_ge(ud.sem, ud.base + c + 1)
                if c >= 1:
                    pe.wait_ge(hd.sem, hd.base + c)
                each(c, 2, [(lambda s, e: bT[s, e, c, :], lambda s, e: Uc[s, e, :])], uh.sem)
                each(c, 4 + c % 2, [(lambda s, e: H[s, e, :], lambda s, e: chunk(rt, e)[s, c, :]),
                                    (lambda s, e: Uc[s, e, :], lambda s, e: RB[s, e, c, :])], od.sem)

        @block.vector
        def _(dve):
            dve.memset(Hs[:, 0, :, :], 0.0).then_inc(hs.sem, 1)
            for c in range(NC):
                H, Uc = Hs[:, c % 2, :, :], U[:, c % 2, :, :]
                dve.wait_ge(hs.sem, hs.base + c + 1)
                dve.tensor_tensor(Hg[:, :, :], H, KV[:, :, c, :], ALU.add)
                dve.wait_ge(uh.sem, uh.base + 2 * c + 1)
                dve.scalar_tensor_tensor(Uc, bank(0), -1.0, XX[:, :, c, :], ALU.mult, ALU.subtract).then_inc(ud.sem, 1)
                dve.wait_ge(ud.sem, ud.base + c + 1)
                dve.wait_ge(uh.sem, uh.base + 2 * c + 2)
                dve.tensor_tensor(Hg[:, :, :], bank(2), Hg[:, :, :], ALU.add).then_inc(K.dve_step.sem, 1)
                dve.wait_ge(K.dve_step.sem, K.dve_step.next())
                if c >= 1:
                    dve.wait_ge(od.sem, od.base + c)
                dve.tensor_tensor(Hs[:, (c + 1) % 2, :, :], Hg[:, :, :], pend[:, :, c].unsqueeze(2).to_broadcast([P, HP, CH]), ALU.mult).then_inc(hs.sem, 1)
                o = kk[:, :, c * CH:(c + 1) * CH]
                dve.wait_ge(od.sem, od.base + c + 1)
                dve.tensor_tensor(o, bank(4 + c % 2), o, ALU.add).then_inc(hd.sem, 1)
    uh.rise(2 * NC)
    ud.rise(NC)
    od.rise(NC)
    hd.rise(NC)
    hs.rise(NC + 1)

    center(K, B, [([kk[:, e, :]], [kk[:, e, :]]) for e in range(HP)], B.const("ones64"), 1.0 / CH, T["Bi"][:, :, :].rearrange("p c t -> p (c t)"))

    def readout(dve, rinv, e):
        x, g = kk[:, e, :], G[:, tile0 + e, :]
        dve.scalar_tensor_tensor(x, x, col("lnx_g", e), rinv, ALU.mult, ALU.mult).then_inc(K.dve_step.sem, 1)
        dve.wait_ge(K.dve_step.sem, K.dve_step.next())
        dve.scalar_tensor_tensor(x, x, col("lnx_b", e), O[:, e, :], ALU.add, ALU.add).then_inc(K.dve_step.sem, 1)
        dve.wait_ge(K.dve_step.sem, K.dve_step.next())
        return dve.tensor_tensor(g, g, x, ALU.mult)
    norms(K, [([kk[:, e, :]], e) for e in range(HP)], B.const("ones64"), 1.0 / CH, B.eps(2), readout, buffers=(YT, bT))


def center(K, B, items, ones, scale, mean):
    nc = K.nc
    units = []
    freed = K.count("vector_freed")
    for n, (srcs, dsts) in enumerate(items):
        def f(eng, _, ps, n=n, srcs=srcs, dsts=dsts):
            if n:
                eng.wait_ge(freed.sem, freed.base + n)
            eng.tensor_scalar(mean, ps, scale, None, ALU.mult).then_inc(K.dve_step.sem, 1)
            eng.wait_ge(K.dve_step.sem, K.dve_step.next())
            for x, y in zip(srcs, dsts):
                i = eng.tensor_tensor(y, x, mean, ALU.subtract)
            return i
        units.append((None, 0, P, SEQ, lambda w, srcs=srcs: [(ones, x) for x in srcs], "vector", f))
    products(K, "", units)


def second_layer(K, B, A, layer):
    nc = K.nc
    with ExitStack() as ctx:
        G = K.sb(ctx, "mixer_gated", [P, KT, SEQ])
        (conv_mixer, ssm_mixer, rwkv_mixer)[layer % 3](*((K, B, A, layer, G) if layer % 3 == 0 else (K, B, A, G)))
        B.dump(f"G{layer}", G[:, :, :])

        def add(e, g):
            def f(eng, _, ps):
                return eng.scalar_tensor_tensor(B.X[:, e, :], B.X[:, e, :], ALPHA, ps, ALU.mult, ALU.add)
            return "vector", f
        products(K, f"mix_out{layer}", linear_units([0, 1], KT, G, (LAT,), add))
        B.dump(f"rm{layer}", B.X[:, :, :])
        pT, pp = K.sb(ctx, "ple_in", [P, 2, SEQ]), K.sb(ctx, "ple", [P, KT, SEQ])
        loaded, taken = K.count("setup_loaded"), K.count("scalar_freed")
        with nc.Block() as block:
            @block.sync
            def _(sp):
                sp.dma_start(pT[:, :, :], A["p"][layer].rearrange("(k p) t -> p k t", p=P)).then_inc(loaded.sem, 16)
                sp.wait_ge(loaded.sem, loaded.base + 16)
        loaded.rise(16)
        products(K, f"ple_p{layer}", linear_units([0], 2, pT, (LAT,), lambda e, g: ("vector", copy_to(pp[:, e, :])), width=8))

        def sigm(e, g):
            return "scalar", act_to(nc, G[:, e, :], ACT.Sigmoid)

        def beside(dve):
            for e in range(KT):
                dve.wait_ge(taken.sem, taken.base + e + 1)
                dve.tensor_tensor(pp[:, e, :], pp[:, e, :], G[:, e, :], ALU.mult).then_inc(K.dve_step.sem, 1)
                dve.wait_ge(K.dve_step.sem, K.dve_step.next())
                dve.tensor_tensor(pp[:, e, :], pp[:, e, :], B.X[:, e, :], ALU.add)
        products(K, f"ple_g{layer}", linear_units([0, 1], KT, B.X, (LAT,), sigm), beside)
        B.dump(f"r{layer}", pp[:, :, :])
        center(K, B, [([pp[:, e, :] for e in range(KT)], [pp[:, e, :] for e in range(KT)])], B.const("ones"), 1.0 / D, pT[:, 0, :])

        def apply(dve, r, _):
            for e in range(KT):
                i = dve.scalar_tensor_tensor(B.X[:, e, :], pp[:, e, :], B.col("ln_g")[:, 8 * layer + e:8 * layer + e + 1], r, ALU.mult, ALU.mult)
            i.then_inc(K.dve_step.sem, 1)
            dve.wait_ge(K.dve_step.sem, K.dve_step.next())
            for e in range(KT):
                i = dve.tensor_scalar(B.X[:, e, :], B.X[:, e, :], B.col("ln_b")[:, 8 * layer + e:8 * layer + e + 1], None, ALU.add)
            return i
        norms(K, [([pp[:, e, :] for e in range(KT)], 0)], B.const("ones"), 1.0 / D, B.eps(1), apply)


def program(nc, A, out, stop=99, dumps=None):
    dumps = dumps or {}
    with ExitStack() as ctx:
        K, B = Core(nc, ctx), Buffers()
        where_c, n_c = columns()
        where_k, packed, _ = shape_constants()
        B.X = K.sb(ctx, "residual", [P, KT, SEQ])
        B.cols = K.sb(ctx, "columns", [P, n_c])
        B.consts = K.sb(ctx, "constants", [P, packed.shape[1]])
        B.col = lambda n: B.cols[:, where_c[n][0]:where_c[n][0] + where_c[n][1]]
        B.const = lambda n: B.consts[:, where_k[n][0]:where_k[n][0] + where_k[n][1]]
        B.eps = lambda i: B.const("eps")[:, i:i + 1]
        B.x = lambda k, g: B.X[:, k, :] if g == LAT else B.XC[:, k, :]
        stored = K.count("stored")

        def dump(name, ap):
            if name in dumps:
                with nc.Block() as block:
                    @block.sync
                    def _(sp):
                        sp.dma_start(dumps[name], ap).then_inc(stored.sem, 16)
                        sp.wait_ge(stored.sem, stored.base + 16)
                stored.rise(16)
        B.dump = dump
        plan_weights(K, A)
        with ExitStack() as first:
            B.XC = K.sb(first, "residual_ctx", [P, KT, CTX])
            B.scond = K.sb(first, "silu_cond", [P, KT, 2])
            B.mod = K.sb(first, "modulation", [P, 2, 24, 2])
            B.gain = K.sb(first, "norm_gain", [P, KT, 2])
            setup(K, B, A)
            products(K, "modulation0", modulation_units(K, nc, B, 0, 6))
            with ExitStack() as layer:
                H = K.sb(layer, "h", [P, KT, TOK])
                modulated_norm(K, B, 0, H)
                zb = gla(K, B, layer, H, A)
                za = mla(K, B, layer, H, A)
                products(K, "ev_out", residual_units(K, B, 0, [0, 1], 8, lambda k: za[:, k, :] if k < 4 else zb[:, k - 4, :],
                                                     [(0, LAT), (1, CTXG)]))
            dump("x1", B.X[:, :, :])
            odd_layer(K, B, A)
            dump("x2", B.X[:, :, :])
        for layer in range(4):
            if stop < layer + 3:
                return
            second_layer(K, B, A, layer)
            dump(f"ln{layer}", B.X[:, :, :])
        with nc.Block() as block:
            @block.sync
            def _(sp):
                sp.dma_start(out.rearrange("(k p) t -> p k t", p=P), B.X[:, :, :]).then_inc(stored.sem, 16)
                sp.wait_ge(stored.sem, stored.base + 16)
        stored.rise(16)


def host_layout(inputs):
    import numpy as np
    a = {n: np.asarray(v) for n, v in inputs.items()}
    col = lambda v: np.reshape(v, (-1, P)).T
    pad = lambda v: np.pad(np.reshape(v, (-1, 1)), ((0, P - v.size), (0, 0)))
    pairs = lambda v: np.reshape(v, (GROUPS // 2, P)).T
    where, n = columns()
    vectors = {
        "cond": np.stack([col(a["c"]), col(a["c_ctx"])], 2).reshape(P, 2 * KT), "norm_g": col(a["norm_g"]), "ada_b": col(a["ada_b"]),
        "q_norm": col(a["ev_q_norm"]), "kv_norm": col(a["ev_kv_norm"]), "q_gain": pad(a["ev_q_gain"]), "k_gain": pad(a["ev_k_gain"]),
        "gate_b": col(a["ev_gate_b"]), "gla_norm": col(a["ev_gla_norm"]), "od_q_gain": np.tile(a["od_q_gain"].reshape(-1, 1), (2, 1)),
        "od_k_gain": np.tile(a["od_k_gain"].reshape(-1, 1), (2, 1)), "conv_k": col(a["conv_k_2"]), "lam_re": pairs(a["ssm_lam_re_2"]),
        "lam_im": pairs(a["ssm_lam_im_2"]), "log_dt": pairs(np.repeat(a["ssm_log_dt_2"], STATE, axis=-1)), "d_skip": col(a["ssm_d_2"]),
        "b_glu": col(a["ssm_b_glu_2"]), "mu": col(a["rwkv_mu_2"]), "w0": col(a["rwkv_w0_2"]), "a0": col(a["rwkv_a0_2"]),
        "k_k": col(a["rwkv_k_k_2"]), "k_a": col(a["rwkv_k_a_2"]), "r_k": col(a["rwkv_r_k_2"]), "lnx_g": col(a["rwkv_lnx_g_2"]),
        "lnx_b": col(a["rwkv_lnx_b_2"]), "ln_g": col(a["ln_g_2"]), "ln_b": col(a["ln_b_2"])}
    out = {"columns": np.ascontiguousarray(np.concatenate([vectors[k] for k in where], axis=1)),
           "constants": shape_constants()[1], "tables": shape_constants()[2]}
    out["x"] = np.ascontiguousarray(a["x"][0].T)
    out["ctx"] = np.ascontiguousarray(a["ctx"][0].T)
    out["p"] = np.ascontiguousarray(a["p_2"][:, 0].transpose(0, 2, 1))
    c = np.arange(64)
    idx = np.clip(c[None, :] - c[:, None] + 15, 0, 30)
    r = a["od_rpb"][0]
    t = np.stack([r[:, 1 - e:15 - e][:, :, idx].transpose(0, 2, 1, 3) for e in (0, 1)], 1)
    out["bias"] = np.ascontiguousarray(t.reshape(C_HEADS, P, 14 * 64))
    for n in WEIGHTS:
        out[n] = np.ascontiguousarray(a[n])
    for n in ("ssm_b_re_2", "ssm_b_im_2"):
        z = np.zeros((GROUPS // 2, 2, GRP, 2, STATE), np.float32)
        for g in range(2):
            z[:, g, :, g, :] = a[n][0, g::2].transpose(0, 2, 1)
        out[n] = z.reshape(KT, P, P)
    for n in ("ssm_c_re_2", "ssm_c_im_2"):
        z = np.zeros((GROUPS // 2, 2, STATE, 2, GRP), np.float32)
        for g in range(2):
            z[:, g, :, g, :] = a[n][0, g::2].transpose(0, 2, 1)
        out[n] = np.ascontiguousarray(z.reshape(GROUPS // 2, P, 2 * GRP).transpose(1, 0, 2))
    return out


WEIGHTS = ("ada_w", "ev_w_in", "ev_w_uq", "ev_w_ukv", "ev_gate_w", "ev_w_out", "od_w_in", "od_w_out", "conv_w_in_2", "conv_w_out_2",
           "ssm_w_in_2", "ssm_w_glu_2", "ssm_w_out_2", "rwkv_w_rkvz_2", "rwkv_w1_2", "rwkv_w2_2", "rwkv_a1_2", "rwkv_a2_2", "rwkv_w_out_2",
           "ple_proj_2", "ple_gate_2")


def kernel(**inputs):
    import concourse.bacc as bacc
    from concourse.bass_utils import run_bass_kernel_spmd
    import numpy as np

    nc = bacc.Bacc("TRN2", target_bir_lowering=False, num_devices=1)
    host = host_layout(inputs)
    arrays = {f"{n}_dram": a for n, a in host.items()}
    A = {n: nc.dram_tensor(f"{n}_dram", a.shape, F32, kind="ExternalInput").ap() for n, a in host.items()}
    out = nc.dram_tensor("out_dram", (D, SEQ), F32, kind="ExternalOutput").ap()
    program(nc, A, out)
    got = run_bass_kernel_spmd(nc, [arrays], core_ids=[0])
    return np.ascontiguousarray(got.results[0]["out_dram"].T)[None]
```

```python
from contextlib import ExitStack

import concourse.bass as bass
from concourse import mybir

F32 = mybir.dt.float32
ALU = mybir.AluOpType
ACT = mybir.ActivationFunctionType
AX = mybir.AxisListType.X

P = 128
D = 1024
KT = D // P
SEQ, CTX = 512, 256
TOK = SEQ + CTX
LAT = (0, SEQ)
CTXG = (SEQ, CTX)
BANK = 512
RING = 2
SLOT = KT * 512
EPS = 1e-6
LN_EPS = 1e-5
GN_EPS = 64e-5
A_HEADS, A_NOPE, A_ROPE, A_V, A_QK = 8, 64, 32, 64, 96
Q_LORA, KV_LORA = 768, 256
B_HEADS, B_DK, B_DV, RANK, TAU = 4, 64, 128, 16, 16.0
CH = 64
NCH = TOK // CH
C_HEADS = 16
ALPHA = 8 ** 0.25
GROUPS, GRP, STATE = 64, 16, 64
HEADS = 16


class Count:

    def __init__(self, sem):
        self.sem, self.base = sem, 0

    def rise(self, n):
        self.base += n

    def next(self):
        self.base += 1
        return self.base


class Core:

    def __init__(self, nc, ctx):
        self.nc, self.ctx = nc, ctx
        self.psum = ctx.enter_context(nc.psum_tensor("psum", [P, 8, BANK], F32))
        self.ring = ctx.enter_context(nc.sbuf_tensor("ring", [P, RING, SLOT], F32))
        self.landed = [self.sem(f"weights_landed{i}") for i in range(RING)]
        self.counts = {}
        self.dve_step, self.act_step, self.pool_step = (Count(self.sem(n)) for n in ("vector_step", "scalar_step", "gpsimd_step"))
        self.weights, self.first, self.named = [], {}, 0

    def sem(self, name):
        return self.ctx.enter_context(self.nc.semaphore(name))

    def count(self, name):
        if name not in self.counts:
            self.counts[name] = Count(self.sem(name))
        return self.counts[name]

    def sb(self, ctx, name, shape):
        return ctx.enter_context(self.nc.sbuf_tensor(self.name(name), shape, F32))

    def name(self, what):
        self.named += 1
        return f"{what}_{self.named}"

    def plan(self, name, tiles):
        self.first[name] = len(self.weights)
        self.weights += tiles

    def send_weights(self, sp, n):
        if n >= len(self.weights):
            return
        dst, parts = self.ring[:, n % RING, :], self.weights[n]
        width = sum(a.shape[1] for a in parts)
        kt = parts[0].shape[0] // P
        view = dst[:, 0:kt * width].rearrange("p (k c) -> p k c", c=width)
        at = 0
        for a in parts:
            w = a.shape[1]
            sp.dma_start(view[:, :, at:at + w], a.rearrange("(k p) c -> p k c", p=P)).then_inc(self.landed[n % RING], 16)
            at += w

    def sent(self, n):
        return 16 * sum(len(self.weights[i]) for i in range(n % RING, n + 1, RING))

    def slot(self, n):
        parts = self.weights[n]
        width = sum(a.shape[1] for a in parts)
        kt = parts[0].shape[0] // P
        return self.ring[:, n % RING, 0:kt * width].rearrange("p (k c) -> p k c", c=width)


def products(K, name, units, beside=None, before=None, load=None):
    nc = K.nc
    base = K.first.get(name, 0)
    done, by_dve, by_act = K.count("product_done"), K.count("vector_freed"), K.count("scalar_freed")
    freed = {"vector": by_dve, "scalar": by_act}
    loaded = K.count("setup_loaded")
    took, n_of = [], {"vector": 0, "scalar": 0}
    last_use = {}
    for i, u in enumerate(units):
        n_of[u[5]] += 1
        took.append(n_of[u[5]])
        if u[0] is not None:
            last_use[u[0]] = i + 1
    assert sorted(last_use) == list(range(len(last_use)))

    with nc.Block() as block:
        @block.tensor
        def _(pe):
            seen = set()
            for i, (tile, p0, m, n, operands, _, _) in enumerate(units):
                if i >= 8:
                    bank_free = freed[units[i - 8][5]]
                    pe.wait_ge(bank_free.sem, bank_free.base + took[i - 8])
                if tile is not None and tile not in seen:
                    seen.add(tile)
                    pe.wait_ge(K.landed[(base + tile) % RING], K.sent(base + tile))
                pairs = operands(K.slot(base + tile) if tile is not None else None)
                out = K.psum[p0:p0 + m, i % 8, 0:n]
                if pairs[0] == "T":
                    nc.tensor.transpose(out, pairs[1], pairs[2]).then_inc(done.sem, 1)
                    continue
                for j, (lhsT, rhs) in enumerate(pairs):
                    mm = nc.tensor.matmul(out, lhsT, rhs, start=j == 0, stop=j == len(pairs) - 1)
                mm.then_inc(done.sem, 1)

        @block.vector
        def _(dve):
            if before:
                before(dve)
            for i, (_, p0, m, n, _, engine, evacuate) in enumerate(units):
                if engine == "vector":
                    dve.wait_ge(done.sem, done.base + i + 1)
                    evacuate(dve, dve, K.psum[p0:p0 + m, i % 8, 0:n]).then_inc(by_dve.sem, 1)
            if beside:
                beside(dve)

        @block.scalar
        def _(act):
            for i, (_, p0, m, n, _, engine, evacuate) in enumerate(units):
                if engine == "scalar":
                    act.wait_ge(done.sem, done.base + i + 1)
                    evacuate(act, act, K.psum[p0:p0 + m, i % 8, 0:n]).then_inc(by_act.sem, 1)

        @block.sync
        def _(sp):
            if load:
                sp.dma_start(*load).then_inc(loaded.sem, 16)
            for t in range(len(last_use)):
                sp.wait_ge(done.sem, done.base + last_use[t])
                K.send_weights(sp, base + t + RING)
            if load:
                sp.wait_ge(loaded.sem, loaded.base + 16)

    if load:
        loaded.rise(16)
    done.rise(len(units))
    by_dve.rise(n_of["vector"])
    by_act.rise(n_of["scalar"])


def dense(K, name, src, groups, n_out, finish, kt=KT, beside=None, load=None):
    nc = K.nc
    base = K.first[name]
    tok = max(g[0] + g[1] for g in groups)
    work = [(e, g) for e in range(n_out) for g in groups]
    fin = [finish(e, g) for e, g in work]
    n_g = len(groups)
    inputs = [(k, g) for k in range(kt) for g in groups]
    per_slot = sum(a.shape[1] for a in K.weights[base]) // P
    done, w_high, w_low, x_high, x_low, loaded = (K.count(n) for n in (
        "product_done", "weights_high", "weights_low", "input_high", "input_low", "setup_loaded"))
    freed = {"vector": K.count("vector_freed"), "scalar": K.count("scalar_freed")}
    took, n_of = [], {"vector": 0, "scalar": 0}
    for engine, _ in fin:
        n_of[engine] += 1
        took.append(n_of[engine])
    FR = mybir.dt.float32r
    with ExitStack() as ctx:
        xh, xl = (ctx.enter_context(nc.sbuf_tensor(K.name(n), [P, kt, tok], FR)) for n in ("input_high", "input_low"))
        wh, wl = (ctx.enter_context(nc.sbuf_tensor(K.name(n), [P, 2, kt, P], FR)) for n in ("weights_high", "weights_low"))

        def columns_of(e):
            c = e % per_slot * P
            return K.slot(base + e // per_slot)[:, :, c:c + P]

        with nc.Block() as block:
            @block.scalar
            def _(act):
                def weights(e):
                    if e % per_slot == 0:
                        act.wait_ge(K.landed[(base + e // per_slot) % RING], K.sent(base + e // per_slot))
                    if e >= 2:
                        act.wait_ge(done.sem, done.base + n_g * (e - 1))
                    nc.scalar.activation(wh[:, e % 2, :, :], columns_of(e), ACT.Copy).then_inc(w_high.sem, 1)
                weights(0)
                for k, g in inputs:
                    nc.scalar.activation(xh[:, k, span(g)], src(k, g), ACT.Copy).then_inc(x_high.sem, 1)
                for i, (e, g) in enumerate(work):
                    if i % n_g == 0 and e + 1 < n_out:
                        weights(e + 1)
                    if fin[i][0] == "scalar":
                        act.wait_ge(done.sem, done.base + i + 1)
                        fin[i][1](act, act, K.psum[:, i % 8, 0:g[1]]).then_inc(freed["scalar"].sem, 1)

            @block.vector
            def _(dve):
                def weights(e):
                    dve.wait_ge(w_high.sem, w_high.base + e + 1)
                    if e >= 2:
                        dve.wait_ge(done.sem, done.base + n_g * (e - 1))
                    dve.tensor_tensor(wl[:, e % 2, :, :], columns_of(e), wh[:, e % 2, :, :].bitcast(F32), ALU.subtract).then_inc(w_low.sem, 1)
                weights(0)
                for n, (k, g) in enumerate(inputs):
                    dve.wait_ge(x_high.sem, x_high.base + n + 1)
                    dve.tensor_tensor(xl[:, k, span(g)], src(k, g), xh[:, k, span(g)].bitcast(F32), ALU.subtract).then_inc(x_low.sem, 1)
                late = beside
                for i, (e, g) in enumerate(work):
                    if i % n_g == 0 and e + 1 < n_out:
                        weights(e + 1)
                    if late and n_of["vector"]:
                        dve.wait_ge(x_low.sem, x_low.base + len(inputs))
                        late(dve)
                        late = None
                    if fin[i][0] == "vector":
                        dve.wait_ge(done.sem, done.base + i + 1)
                        fin[i][1](dve, dve, K.psum[:, i % 8, 0:g[1]]).then_inc(freed["vector"].sem, 1)
                if late:
                    dve.wait_ge(x_low.sem, x_low.base + len(inputs))
                    late(dve)

            @block.tensor
            def _(pe):
                for i, (e, g) in enumerate(work):
                    if i >= 8:
                        bank_free = freed[fin[i - 8][0]]
                        pe.wait_ge(bank_free.sem, bank_free.base + took[i - 8])
                    pe.wait_ge(w_low.sem, w_low.base + e + 1)
                    out = K.psum[:, i % 8, 0:g[1]]
                    for k in range(kt):
                        if e == 0:
                            pe.wait_ge(x_low.sem, x_low.base + inputs.index((k, g)) + 1)
                        nc.tensor.matmul(out, wh[:, e % 2, k, :], xh[:, k, span(g)], start=k == 0, stop=False)
                        nc.tensor.matmul(out, wh[:, e % 2, k, :], xl[:, k, span(g)], start=False, stop=False)
                        mm = nc.tensor.matmul(out, wl[:, e % 2, k, :], xh[:, k, span(g)], start=False, stop=k == kt - 1)
                    mm.then_inc(done.sem, 1)

            @block.sync
            def _(sp):
                if load:
                    sp.dma_start(*load).then_inc(loaded.sem, 16)
                for t in range(n_out // per_slot):
                    sp.wait_ge(w_low.sem, w_low.base + per_slot * (t + 1))
                    K.send_weights(sp, base + t + RING)
                if load:
                    sp.wait_ge(loaded.sem, loaded.base + 16)
    if load:
        loaded.rise(16)
    done.rise(len(work))
    for c in (w_high, w_low):
        c.rise(n_out)
    for c in (x_high, x_low):
        c.rise(len(inputs))
    for n, c in freed.items():
        c.rise(n_of[n])


def norms(K, items, ones, scale, eps, apply, kind="rms", buffers=None):
    nc = K.nc
    sq_done, sq_used, root_done, root_used = (K.count(x) for x in (
        "square_done", "square_summed", "root_done", "root_used"))
    rows = items[0][0][0].shape[0]
    n_src = [len(s) for s, _ in items]
    upto = [sum(n_src[:i + 1]) for i in range(len(items))]
    with ExitStack() as ctx:
        if buffers:
            x, y = (b.rearrange("p e c t -> p e (c t)") for b in buffers)
            sq, root, rinv = x[:, 0:2, :], x[:, 2:4, :], y[:, 0:2, :]
        else:
            sq, root, rinv = (K.sb(ctx, n, [P, 2, BANK]) for n in ("squares", "roots", "rinv"))
        with nc.Block() as block:
            @block.scalar
            def _(act):
                def take_root(i):
                    n = items[i][0][0].shape[1]
                    act.wait_ge(sq_used.sem, sq_used.base + upto[i])
                    if i >= 2:
                        act.wait_ge(root_used.sem, root_used.base + i - 1)
                    if kind == "norm":
                        nc.scalar.activation(root[0:rows, i % 2, 0:n], K.psum[0:rows, i % 2, 0:n], ACT.Sqrt).then_inc(root_done.sem, 1)
                    else:
                        nc.scalar.activation(root[0:rows, i % 2, 0:n], K.psum[0:rows, i % 2, 0:n], ACT.Sqrt,
                                             bias=eps[0:rows, :], scale=scale).then_inc(root_done.sem, 1)
                j = 0
                for i, (srcs, _) in enumerate(items):
                    for s in srcs:
                        if j >= 2:
                            act.wait_ge(sq_used.sem, sq_used.base + j - 1)
                        nc.scalar.activation(sq[0:rows, j % 2, 0:s.shape[1]], s, ACT.Square).then_inc(sq_done.sem, 1)
                        j += 1
                    if i >= 1:
                        take_root(i - 1)
                take_root(len(items) - 1)

            @block.tensor
            def _(pe):
                j = 0
                for i, (srcs, _) in enumerate(items):
                    if i >= 2:
                        pe.wait_ge(root_done.sem, root_done.base + i - 1)
                    for k, s in enumerate(srcs):
                        pe.wait_ge(sq_done.sem, sq_done.base + j + 1)
                        n = s.shape[1]
                        mm = nc.tensor.matmul(K.psum[0:rows, i % 2, 0:n], ones, sq[0:rows, j % 2, 0:n],
                                              start=k == 0, stop=k == len(srcs) - 1)
                        mm.then_inc(sq_used.sem, 1)
                        j += 1

            @block.vector
            def _(dve):
                for i, (srcs, arg) in enumerate(items):
                    n = srcs[0].shape[1]
                    dve.wait_ge(root_done.sem, root_done.base + i + 1)
                    if i >= 2:
                        dve.wait_ge(root_used.sem, root_used.base + i - 1)
                    r = rinv[0:rows, i % 2, 0:n]
                    src = root[0:rows, i % 2, 0:n]
                    if kind == "norm":
                        dve.tensor_scalar(src, src, 1e-12, None, ALU.max).then_inc(K.dve_step.sem, 1)
                        dve.wait_ge(K.dve_step.sem, K.dve_step.next())
                    dve.reciprocal(r, src).then_inc(K.dve_step.sem, 1)
                    dve.wait_ge(K.dve_step.sem, K.dve_step.next())
                    apply(dve, r, arg).then_inc(root_used.sem, 1)
        sq_done.rise(upto[-1])
        sq_used.rise(upto[-1])
        for c in (root_done, root_used):
            c.rise(len(items))


def head_norms(K, B, items, rows, per, scale, eps, apply, kind="rms"):
    nc = K.nc
    sq_done, sq_used, root_done, root_used, spread_done, spread_used = (K.count(x) for x in (
        "square_done", "square_summed", "root_done", "root_used", "sum_done", "vector_freed"))
    groups = sorted({g for _, g, _, _ in items})
    order = [[it for it in items if it[1] == g] for g in groups]
    last = [sum(len(o) for o in order[:n + 1]) for n in range(len(order))]
    every = [it for o in order for it in o]
    select = "pick2" if per == 2 else "pick1"
    with ExitStack() as ctx:
        sq = K.sb(ctx, "squares", [P, 3, BANK])
        root = K.sb(ctx, "roots", [32, len(groups), BANK])
        top = max(it[0] for it in items) + per
        ones_of = K.sb(ctx, "spread_ones", [32, top, 64]) if per == 2 else None
        with nc.Block() as block:
            @block.scalar
            def _(act):
                for i, (_, g, x, _) in enumerate(every):
                    if i >= 3:
                        act.wait_ge(sq_used.sem, sq_used.base + i - 2)
                    nc.scalar.activation(sq[0:rows, i % 3, 0:g[1]], x, ACT.Square).then_inc(sq_done.sem, 1)
                for n, g in enumerate(groups):
                    act.wait_ge(sq_used.sem, sq_used.base + last[n])
                    if kind == "norm":
                        nc.scalar.activation(root[:, n, 0:g[1]], K.psum[0:32, n, 0:g[1]], ACT.Sqrt).then_inc(root_done.sem, 1)
                    else:
                        nc.scalar.activation(root[:, n, 0:g[1]], K.psum[0:32, n, 0:g[1]], ACT.Sqrt, bias=eps[0:32, :],
                                             scale=scale).then_inc(root_done.sem, 1)

            @block.tensor
            def _(pe):
                i = 0
                for n, o in enumerate(order):
                    for m, (base, g, _, _) in enumerate(o):
                        pe.wait_ge(sq_done.sem, sq_done.base + i + 1)
                        nc.tensor.matmul(K.psum[0:32, n, 0:g[1]], B.const(select)[0:rows, 32 - base:64 - base], sq[0:rows, i % 3, 0:g[1]],
                                         start=m == 0, stop=m == len(o) - 1).then_inc(sq_used.sem, 1)
                        i += 1
                i = 0
                for n, o in enumerate(order):
                    pe.wait_ge(root_used.sem, root_used.base + n + 1)
                    for base, g, _, _ in o:
                        if i >= 4:
                            pe.wait_ge(spread_used.sem, spread_used.base + i - 3)
                        lhsT = (ones_of[:, base:base + 2, :].rearrange("p h c -> p (h c)") if per == 2
                                else B.const("ident")[0:32, base:base + 1].to_broadcast([32, rows]))
                        nc.tensor.matmul(K.psum[0:rows, 4 + i % 4, 0:g[1]], lhsT, root[:, n, 0:g[1]], start=True,
                                         stop=True).then_inc(spread_done.sem, 1)
                        i += 1

            @block.vector
            def _(dve):
                if per == 2:
                    dve.tensor_copy(ones_of[:, :, :], B.const("ident")[0:32, 0:top].unsqueeze(2).to_broadcast([32, top, 64])).then_inc(K.dve_step.sem, 1)
                    dve.wait_ge(K.dve_step.sem, K.dve_step.next())
                for n, g in enumerate(groups):
                    x = root[:, n, 0:g[1]]
                    dve.wait_ge(root_done.sem, root_done.base + n + 1)
                    if kind == "norm":
                        dve.tensor_scalar(x, x, 1e-12, None, ALU.max).then_inc(K.dve_step.sem, 1)
                        dve.wait_ge(K.dve_step.sem, K.dve_step.next())
                    dve.reciprocal(x, x).then_inc(root_used.sem, 1)
                for i, (_, g, _, arg) in enumerate(every):
                    dve.wait_ge(spread_done.sem, spread_done.base + i + 1)
                    apply(dve, K.psum[0:rows, 4 + i % 4, 0:g[1]], arg).then_inc(spread_used.sem, 1)
        for c in (sq_done, sq_used, spread_done, spread_used):
            c.rise(len(every))
        for c in (root_done, root_used):
            c.rise(len(groups))


def columns():
    sizes = [("cond", 2 * KT), ("norm_g", 2 * KT), ("ada_b", 48), ("q_norm", 6), ("kv_norm", 2), ("q_gain", 1), ("k_gain", 1),
             ("gate_b", 4), ("gla_norm", 4), ("od_q_gain", 1), ("od_k_gain", 1), ("conv_k", 48), ("lam_re", 32), ("lam_im", 32),
             ("log_dt", 32), ("d_skip", 8), ("b_glu", 8), ("mu", 48), ("w0", 8), ("a0", 8), ("k_k", 8), ("k_a", 8), ("r_k", 8),
             ("lnx_g", 8), ("lnx_b", 8), ("ln_g", 32), ("ln_b", 32)]
    at, out = 0, {}
    for name, n in sizes:
        out[name] = (at, n)
        at += n
    return out, at


def shape_constants():
    import numpy as np
    i = np.arange(P)
    same = lambda a, n: (a[:, None] // n) == (a[None, :] // n)
    t = np.arange(SEQ)
    inv = 10000.0 ** (-np.arange(0, 16, 2, dtype=np.float32) / 16)
    cos, sin = np.zeros((P, SEQ)), np.zeros((P, SEQ))
    swap = np.zeros((P, 96))
    for d in range(A_ROPE):
        ax, half, k = d // 16, d // 8 % 2, d % 8
        ang = ((t // 64 if ax == 0 else t % 64).astype(np.float32) * inv[k].astype(np.float32)).astype(np.float64)
        cos[64 + d] = np.cos(ang)
        sin[64 + d] = np.sin(ang) * (1 if half else -1)
        swap[64 + (d ^ 8), 64 + d] = 1
    s, u = i[:, None] % 64, np.arange(64)[None, :]
    blk = (s // 16) == (u // 16)
    c = np.arange(64)
    start = np.clip(c - 8, 0, 48)
    keep = (c[None, :] >= start[:, None]) & (c[None, :] < start[:, None] + 16)
    out = [("ident", np.eye(P)), ("ones", np.ones((P, P))), ("ones64", same(i, 64)),
           ("pick1", np.tile(np.arange(64) == 32, (P, 1))), ("pick2", np.arange(64)[None, :] == 32 + (i[:, None] >= 64)),
           ("mask_f", same(i, 64) & (i[:, None] <= i[None, :])), ("mask_b", same(i, 64) & (i[:, None] >= i[None, :])),
           ("restart", np.tile(np.arange(TOK) % CH != 0, (P, 1))), 
           ("window", np.tile(np.where(keep, 0, -1e30), (2, 1))),
           ("before", s < u), ("upto", s <= u), ("before_in", (s < u) & blk), ("before_out", (s < u) & ~blk),
           ("after_in", (s > u) & blk), ("after_out", (s > u) & ~blk), ("eye64", s == u),
           ("eps", np.stack([np.full(P, EPS), np.full(P, LN_EPS), np.full(P, GN_EPS), np.full(P, 1.5707963), np.full(P, 1.0)], 1))]
    tables = np.concatenate([cos, sin, np.pad(swap, ((0, 0), (0, 32))), np.tile(np.arange(SEQ), (P, 1))], axis=1).astype(np.float32)
    at, where = 0, {}
    for name, a in out:
        where[name] = (at, a.shape[1])
        at += a.shape[1]
    return where, np.concatenate([a.astype(np.float32) for _, a in out], axis=1), tables


def plan_weights(K, A):
    def cut(w, a, b, n=512):
        return [[w[:, i:min(i + n, b)]] for i in range(a, b, n)]
    ev = A["ev_w_in"][0]
    K.plan("modulation0", cut(A["ada_w"][0], 0, 3 * D))
    K.plan("gla_in", cut(ev, 1568, 2592) + cut(ev, 2624, 3136) + cut(ev, 2592, 2624))
    K.plan("mla_in", cut(ev, 0, 1024) + cut(ev, 1024, 1056) + cut(ev, 1056, 1568))
    K.plan("q_up", cut(A["ev_w_uq"][0], 0, 768, 384))
    K.plan("kv_up", [[A["ev_w_ukv"][0]]])
    K.plan("ev_out", cut(A["ev_w_out"][0], 0, D))
    K.plan("modulation1", cut(A["ada_w"][1], 0, 3 * D))
    K.plan("od_in", cut(A["od_w_in"][0], 0, 4 * D))
    K.plan("od_out", cut(A["od_w_out"][0], 0, D))
    for layer in range(4):
        kind, j = layer % 3, layer // 3
        if kind == 0:
            w = A["conv_w_in_2"][j]
            K.plan(f"conv_in{layer}", [[w[:, s * D + e * P:s * D + (e + 1) * P] for s in (1, 2, 3, 0)] for e in range(KT)])
            K.plan(f"mix_out{layer}", cut(A["conv_w_out_2"][j], 0, D))
        elif kind == 1:
            K.plan("ssm_in", cut(A["ssm_w_in_2"][0], 0, 2 * D))
            K.plan("ssm_glu", cut(A["ssm_w_glu_2"][0], 0, D))
            K.plan(f"mix_out{layer}", cut(A["ssm_w_out_2"][0], 0, D))
        else:
            r = A["rwkv_w_rkvz_2"][0]
            K.plan("rwkv_w", [[A["rwkv_w1_2"][0]]])
            K.plan("rwkv_a", [[A["rwkv_a1_2"][0]]])
            K.plan("rwkv_z", cut(r[3], 0, D))
            for half in range(2):
                for n, m in enumerate("rkv"):
                    K.plan(f"rwkv_{m}{half}", [[r[n][:, half * 512:half * 512 + 512]]])
            K.plan(f"mix_out{layer}", cut(A["rwkv_w_out_2"][0], 0, D))
        K.plan(f"ple_p{layer}", [[A["ple_proj_2"][layer]]])
        K.plan(f"ple_g{layer}", cut(A["ple_gate_2"][layer], 0, D))


def span(g):
    return slice(g[0], g[0] + g[1])


def one_engine(K, engine, program):
    with K.nc.Block() as block:
        {"vector": block.vector, "scalar": block.scalar, "gpsimd": block.gpsimd}[engine](program)


def copy_to(dst):
    def f(eng, _, ps):
        return eng.tensor_copy(dst, ps)
    return f


def act_to(nc, dst, func):
    def f(eng, _, ps):
        return nc.scalar.activation(dst, ps, func)
    return f


def wide(src, kt, g):
    return [src[:, k, span(g)] for k in range(kt)]


def linear_units(tiles, kt, src, groups, finish, width=4):
    units = []
    for t in tiles:
        for e in range(width):
            for g in groups:
                engine, f = finish(t * width + e, g)
                units.append((t, 0, P, g[1],
                              lambda w, e=e, g=g: [(w[:, k, e * P:(e + 1) * P], src[:, k, span(g)]) for k in range(kt)], engine, f))
    return units


def modulation_units(K, nc, B, layer, tiles):
    units = []
    for t in range(tiles):
        for e in range(4):
            c = 4 * t + e
            def f(eng, _, ps, c=c):
                return eng.tensor_scalar(B.mod[:, layer, c, :], ps, B.col("ada_b")[:, 24 * layer + c:24 * layer + c + 1], None, ALU.add)
            units.append((t, 0, P, 2, lambda w, e=e: [(w[:, k, e * P:(e + 1) * P], B.scond[:, k, :]) for k in range(KT)], "vector", f))
    return units


class Buffers:
    pass


def setup(K, B, A):
    nc = K.nc
    loaded, x_in = K.count("setup_loaded"), K.count("activations_loaded")
    with nc.Block() as block:
        @block.sync
        def _(sp):
            sp.dma_start(B.cols[:, :], A["columns"]).then_inc(loaded.sem, 16)
            sp.dma_start(B.consts[:, :], A["constants"]).then_inc(loaded.sem, 16)
            sp.dma_start(B.X[:, :, :], A["x"].rearrange("(k p) t -> p k t", p=P)).then_inc(x_in.sem, 16)
            sp.dma_start(B.XC[:, :, :], A["ctx"].rearrange("(k p) t -> p k t", p=P)).then_inc(x_in.sem, 16)
            for n in range(RING):
                K.send_weights(sp, n)
            sp.wait_ge(loaded.sem, loaded.base + 32)
            sp.wait_ge(x_in.sem, x_in.base + 32)

        @block.scalar
        def _(act):
            act.wait_ge(loaded.sem, loaded.base + 32)
            nc.scalar.activation(B.scond.rearrange("p k c -> p (k c)"), B.col("cond"), ACT.Silu)
    loaded.rise(32)
    x_in.rise(32)


def normed(K, B, H):
    def apply(dve, r, g):
        for k in range(KT):
            i = dve.tensor_tensor(H[:, k, span(g)], B.x(k, g), r, ALU.mult)
        return i
    norms(K, [([B.x(k, g) for k in range(KT)], g) for g in (LAT, CTXG)], B.const("ones"), 1.0 / D, B.eps(0), apply)


def modulated(K, B, layer, H):
    nc = K.nc
    gains = K.count("vector_part")
    with nc.Block() as block:
        @block.vector
        def _(dve):
            for c in (1, 0):
                dve.scalar_tensor_tensor(B.gain[:, :, c], B.mod[:, layer, 8:16, c], 1.0, B.col("norm_g")[:, 8 * layer:8 * layer + 8],
                                         ALU.add, ALU.mult).then_inc(gains.sem, 1)
            dve.wait_ge(gains.sem, gains.base + 2)
            for k in range(KT):
                x = H[:, k, span(LAT)]
                dve.tensor_scalar(x, x, B.gain[:, k, 0:1], B.mod[:, layer, k, 0:1], ALU.mult, ALU.add)

        @block.scalar
        def _(act):
            act.wait_ge(gains.sem, gains.base + 1)
            for k in range(KT):
                x = H[:, k, span(CTXG)]
                nc.scalar.activation(x, x, ACT.Identity, scale=B.gain[:, k, 1:2], bias=B.mod[:, layer, k, 1:2])
    gains.rise(2)


def gla(K, B, ctx, H, A):
    nc = K.nc
    zb = K.sb(ctx, "gla_out", [P, B_HEADS, TOK])
    with ExitStack() as tmp:
        big = K.sb(tmp, "gla_state", [P, 8 * TOK])
        gq = big[:, 0:2 * TOK].rearrange("p (j t) -> p j t", j=2)
        gk = big[:, 2 * TOK:4 * TOK].rearrange("p (j t) -> p j t", j=2)
        bs = big[:, 4 * TOK:6 * TOK].rearrange("p (j t) -> p j t", j=2)
        ex = big[:, 6 * TOK:8 * TOK].rearrange("p (j t) -> p j t", j=2)
        st = big[:, :].rearrange("p (z j c e) -> p z j c e", z=2, j=2, c=NCH)
        gv = K.sb(tmp, "gla_v", [P, TOK // P, 512])
        lr = big[0:32, 4 * TOK:5 * TOK]
        gw = big[0:32, 5 * TOK:5 * TOK + 512].rearrange("p (z c) -> p z c", z=2)
        units = []
        for e in range(4):
            for g in (LAT, CTXG):
                dst = (gq if e < 2 else gk)[:, e % 2, span(g)]
                units.append((0, 0, P, g[1], lambda w, e=e, g=g: [(w[:, k, e * P:(e + 1) * P], H[:, k, span(g)]) for k in range(KT)],
                              "vector", copy_to(dst)))
        for t in range(TOK // P):
            units.append((1, 0, P, 512, lambda w, t=t: [(H[:, k, t * P:(t + 1) * P], w[:, k, :]) for k in range(KT)],
                          "vector", copy_to(gv[:, t, :])))
        units += [(2,) + u[1:] for u in linear_units([0], KT, H, (LAT, CTXG), lambda e, g: ("scalar", act_to(nc, zb[:, e, span(g)], ACT.Silu)))]
        for g in (LAT, CTXG):
            units.append((3, 0, 32, g[1], lambda w, g=g: [(w[:, k, :], H[:, k, span(g)]) for k in range(KT)], "vector", copy_to(lr[:, span(g)])))
        products(K, "gla_in", units)

        go = K.sb(tmp, "gla_kd", [P, 4, TOK])
        dirs = [[K.sb(tmp, f"gla_{n}{z}", [P, 2, TOK]) for n in ("qt", "kt")] + [go[:, 2 * z:2 * z + 2, :]] for z in range(2)]
        decay = K.sb(tmp, "gla_decay", [P, 2, 2, NCH])
        gl = K.sb(tmp, "gla_g", [P, 4, TOK])
        loaded, cleared = K.count("setup_loaded"), K.count("setup_ready")
        logits, lg_used, a1, v1 = (K.count(x) for x in ("product_done", "vector_freed", "scalar_part", "vector_part"))
        with nc.Block() as block:
            @block.gpsimd
            def _(pool):
                nc.gpsimd.memset(gw[:, :, :], 0.0).then_inc(cleared.sem, 1)

            @block.sync
            def _(sp):
                sp.wait_ge(cleared.sem, cleared.base + 1)
                for z in range(2):
                    sp.dma_start(gw[16 * z:16 * z + 16, z, :], A["ev_gate_w"][0, z]).then_inc(loaded.sem, 16)

            @block.tensor
            def _(pe):
                pe.wait_ge(loaded.sem, loaded.base + 32)
                for i in range(4):
                    z, j = i // 2, i % 2
                    for n, g in enumerate((LAT, CTXG)):
                        nc.tensor.matmul(K.psum[:, 2 * i + n, 0:g[1]], gw[:, z, j * P:(j + 1) * P], lr[:, span(g)], start=True,
                                         stop=True).then_inc(logits.sem, 1)

            @block.scalar
            def _(act):
                for i in range(4):
                    act.wait_ge(logits.sem, logits.base + 2 * i + 2)
                    ps = K.psum[:, 2 * i:2 * i + 2, :].rearrange("p b n -> p (b n)")[:, 0:TOK]
                    bias = B.col("gate_b")[:, i:i + 1]
                    nc.scalar.activation(gl[:, i, :], ps, ACT.Identity, bias=bias).then_inc(a1.sem, 1)
                    if i >= 1:
                        act.wait_ge(v1.sem, v1.base + i)
                    nc.scalar.activation(ex[:, 0, :], ps, ACT.Abs, bias=bias).then_inc(K.act_step.sem, 1)
                    act.wait_ge(K.act_step.sem, K.act_step.next())
                    nc.scalar.activation(ex[:, 0, :], ex[:, 0, :], ACT.Exp, scale=-1.0).then_inc(K.act_step.sem, 1)
                    act.wait_ge(K.act_step.sem, K.act_step.next())
                    nc.scalar.activation(ex[:, 1, :], ex[:, 0, :], ACT.Ln, bias=B.eps(4)).then_inc(a1.sem, 1)

            @block.vector
            def _(dve):
                for i in range(4):
                    dve.wait_ge(a1.sem, a1.base + 2 * i + 2)
                    dve.tensor_scalar(gl[:, i, :], gl[:, i, :], 0.0, None, ALU.min).then_inc(K.dve_step.sem, 1)
                    dve.wait_ge(K.dve_step.sem, K.dve_step.next())
                    dve.tensor_tensor(gl[:, i, :], gl[:, i, :], ex[:, 1, :], ALU.subtract).then_inc(v1.sem, 1)
        loaded.rise(32)
        cleared.rise(1)
        logits.rise(8)
        a1.rise(8)
        v1.rise(4)
        with nc.Block() as block:
            @block.vector
            def _(dve):
                for i in range(4):
                    z, j = i // 2, i % 2
                    g, b = gl[:, i, :], bs[:, i % 2, :]
                    qt, kt, kd = (x[:, j, :] for x in dirs[z])
                    if i >= 2:
                        dve.wait_ge(a1.sem, a1.base + 3 * i - 3)
                    dve.tensor_scalar(g, g, 1.0 / TAU, None, ALU.mult).then_inc(K.dve_step.sem, 1)
                    dve.wait_ge(K.dve_step.sem, K.dve_step.next())
                    dve.tensor_tensor_scan(b, B.const("restart"), g, 0.0, ALU.mult, ALU.add).then_inc(K.dve_step.sem, 1)
                    dve.wait_ge(K.dve_step.sem, K.dve_step.next())
                    bc = b.rearrange("p (c t) -> p c t", t=CH)
                    gc = g.rearrange("p (c t) -> p c t", t=CH)
                    dve.tensor_copy(decay[:, z, j, :], bc[:, :, CH - 1]).then_inc(K.dve_step.sem, 1)
                    dve.wait_ge(K.dve_step.sem, K.dve_step.next())
                    total = decay[:, z, j, :].unsqueeze(2).to_broadcast([P, NCH, CH])
                    if z == 1:
                        dve.tensor_tensor(bc, total, bc, ALU.subtract).then_inc(K.dve_step.sem, 1)
                        dve.wait_ge(K.dve_step.sem, K.dve_step.next())
                        dve.tensor_tensor(b, b, g, ALU.add).then_inc(K.dve_step.sem, 1)
                        dve.wait_ge(K.dve_step.sem, K.dve_step.next())
                    dve.tensor_tensor(gc, total, bc, ALU.subtract).then_inc(v1.sem, 1)
                    dve.wait_ge(a1.sem, a1.base + 3 * i + 3)
                    dve.scalar_tensor_tensor(qt, gq[:, j, :], float(B_DK) ** -0.5, qt, ALU.mult, ALU.mult)
                    dve.tensor_tensor(kt, gk[:, j, :], kt, ALU.mult)
                    dve.tensor_tensor(kd, gk[:, j, :], kd, ALU.mult)

            @block.scalar
            def _(act):
                for i in range(4):
                    z, j = i // 2, i % 2
                    qt, kt, kd = (x[:, j, :] for x in dirs[z])
                    act.wait_ge(v1.sem, v1.base + i + 1)
                    nc.scalar.activation(qt, bs[:, i % 2, :], ACT.Exp).then_inc(a1.sem, 1)
                    nc.scalar.activation(kt, bs[:, i % 2, :], ACT.Exp, scale=-1.0).then_inc(a1.sem, 1)
                    nc.scalar.activation(kd, gl[:, i, :], ACT.Exp).then_inc(a1.sem, 1)
                nc.scalar.activation(decay.rearrange("p z j c -> p (z j c)"), decay.rearrange("p z j c -> p (z j c)"), ACT.Exp)
        a1.rise(12)
        v1.rise(4)
        kdT = gl.rearrange("p a t -> p (a t)").rearrange("p (z t c) -> p z t c", z=2, c=256)
        units = []
        for z in range(2):
            for j in range(2):
                for t in range(TOK // P):
                    units.append((None, 0, P, P, lambda w, z=z, j=j, t=t: ("T", dirs[z][2][:, j, t * P:(t + 1) * P], B.const("ident")),
                                  ("vector", "scalar")[t % 2], (copy_to if t % 2 == 0 else lambda d: act_to(nc, d, ACT.Copy))(kdT[:, z, t, j * P:(j + 1) * P])))
        products(K, "", units)
        order = [[8, 9, 10, 11] + list(range(8)), [11, 10, 9, 8] + list(range(7, -1, -1))]
        sum_done, state_done = K.count("product_done"), K.count("vector_freed")
        work = [(n, z, j) for n in range(NCH - 1) for z in range(2) for j in range(2)]
        with nc.Block() as block:
            @block.tensor
            def _(pe):
                for i, (n, z, j) in enumerate(work):
                    if i >= 8:
                        pe.wait_ge(state_done.sem, state_done.base + i - 7)
                    c = order[z][n]
                    r = slice(CH * (c % 2), CH * (c % 2) + CH)
                    for h in range(2):
                        mm = nc.tensor.matmul(K.psum[CH * h:CH * h + CH, i % 8, 0:B_DV], kdT[r, z, c // 2, j * P + CH * h:j * P + CH * h + CH],
                                              gv[r, c // 2, (2 * j + h) * B_DV:(2 * j + h + 1) * B_DV], start=True, stop=True)
                    mm.then_inc(sum_done.sem, 1)

            @block.vector
            def _(dve):
                for z in range(2):
                    i = dve.memset(st[:, z, :, order[z][0], :], 0.0)
                i.then_inc(K.dve_step.sem, 1)
                dve.wait_ge(K.dve_step.sem, K.dve_step.next())
                for i, (n, z, j) in enumerate(work):
                    c, nxt = order[z][n], order[z][n + 1]
                    dve.wait_ge(sum_done.sem, sum_done.base + i + 1)
                    if i >= 4:
                        dve.wait_ge(state_done.sem, state_done.base + i - 3)
                    dve.scalar_tensor_tensor(st[:, z, j, nxt, :], st[:, z, j, c, :], decay[:, z, j, c:c + 1], K.psum[:, i % 8, 0:B_DV],
                                             ALU.mult, ALU.add).then_inc(state_done.sem, 1)
        sum_done.rise(len(work))
        state_done.rise(len(work))
        work = [(h, t) for h in range(B_HEADS) for t in range(TOK // P)]
        scores, masked, out_done, out_used = (K.count(x) for x in ("product_done", "vector_part", "sum_done", "scalar_freed"))
        att = K.sb(tmp, "gla_att", [P, 2, 2, P])
        with nc.Block() as block:
            @block.tensor
            def _(pe):
                def score(i):
                    h, t = work[i]
                    r, j = slice(CH * (h % 2), CH * (h % 2) + CH), h // 2
                    for z in range(2):
                        if i >= 2:
                            pe.wait_ge(masked.sem, masked.base + i - 1)
                        nc.tensor.matmul(K.psum[:, 2 * (i % 2) + z, 0:P], dirs[z][1][r, j, t * P:(t + 1) * P],
                                         dirs[z][0][r, j, t * P:(t + 1) * P], start=True, stop=True).then_inc(scores.sem, 1)
                score(0)
                for i, (h, t) in enumerate(work):
                    if i + 1 < len(work):
                        score(i + 1)
                    r, j = slice(CH * (h % 2), CH * (h % 2) + CH), h // 2
                    pe.wait_ge(masked.sem, masked.base + i + 1)
                    if i >= 2:
                        pe.wait_ge(out_used.sem, out_used.base + i - 1)
                    o = K.psum[:, 4 + i % 2, :]
                    nc.tensor.matmul(o[:, 0:P], gv[:, t, h * P:(h + 1) * P], att[:, i % 2, 0, :], start=True, stop=False)
                    for z in range(2):
                        for c in (2 * t, 2 * t + 1):
                            s = slice(c * CH, (c + 1) * CH)
                            mm = nc.tensor.matmul(o[:, (c % 2) * CH:(c % 2 + 1) * CH], st[r, z, j, c, :], dirs[z][0][r, j, s],
                                                  start=False, stop=z == 1 and c % 2 == 1)
                    mm.then_inc(out_done.sem, 1)

            @block.vector
            def _(dve):
                for i in range(len(work)):
                    dve.wait_ge(scores.sem, scores.base + 2 * i + 2)
                    if i >= 2:
                        dve.wait_ge(out_done.sem, out_done.base + i - 1)
                    dve.tensor_tensor(att[:, i % 2, 0, :], K.psum[:, 2 * (i % 2), 0:P], B.const("mask_f"), ALU.mult)
                    dve.tensor_tensor(att[:, i % 2, 1, :], K.psum[:, 2 * (i % 2) + 1, 0:P], B.const("mask_b"), ALU.mult).then_inc(K.dve_step.sem, 1)
                    dve.wait_ge(K.dve_step.sem, K.dve_step.next())
                    dve.tensor_tensor(att[:, i % 2, 0, :], att[:, i % 2, 0, :], att[:, i % 2, 1, :], ALU.add).then_inc(masked.sem, 1)

            @block.scalar
            def _(act):
                for i, (h, t) in enumerate(work):
                    act.wait_ge(out_done.sem, out_done.base + i + 1)
                    nc.scalar.activation(go[:, h, t * P:(t + 1) * P], K.psum[:, 4 + i % 2, 0:P], ACT.Copy).then_inc(out_used.sem, 1)
        scores.rise(2 * len(work))
        for c in (masked, out_done, out_used):
            c.rise(len(work))
        B.dump("gla", go[:, :, :])

        def apply(dve, r, arg):
            h, g = arg
            dve.scalar_tensor_tensor(go[:, h, span(g)], go[:, h, span(g)], B.col("gla_norm")[:, h:h + 1], r, ALU.mult, ALU.mult).then_inc(K.dve_step.sem, 1)
            dve.wait_ge(K.dve_step.sem, K.dve_step.next())
            return dve.tensor_tensor(zb[:, h, span(g)], zb[:, h, span(g)], go[:, h, span(g)], ALU.mult)
        head_norms(K, B, [(h, g, go[:, h, span(g)], (h, g)) for h in range(B_HEADS) for g in (LAT, CTXG)], P, 1, 1.0 / B_DV, B.eps(0), apply)
    return zb


def attention(K, B, ctx, name, n_heads, q_tiles, q_of, k_of, v_of, out_of, scale, scratch, table=None, table_src=None):
    nc = K.nc
    S, W, WT = (scratch[:, 2 * n:2 * n + 2, :] for n in range(3))
    m = K.sb(ctx, "att_max", [P, 2, 4])
    work = [(h, q) for h in range(n_heads) for q in q_tiles]
    nq = len(q_tiles)
    scores, maxed, exped, normed, turned, evac_v, evac_a, out_done, out_used = (K.count(x) for x in (
        "product_done", "vector_part", "scalar_part", "pool_part", "turned", "vector_freed", "scalar_freed", "sum_done", "root_used"))
    t_in = [K.count("table_loaded_even"), K.count("table_loaded_odd")]
    copied = K.count("ctx_scores_copied")
    ident = B.const("ident")
    with nc.Block() as block:
        @block.tensor
        def _(pe):
            def score(i):
                h, (q0, kt0, nk) = work[i]
                if i >= 2:
                    pe.wait_ge(exped.sem, exped.base + i - 1)
                k0 = kt0 * P
                first = min(nk * P, BANK)
                b = 2 * (i % 2)
                mm = nc.tensor.matmul(K.psum[:, b, 0:first], q_of(h)[:, q0:q0 + P], k_of(h)[:, k0:k0 + first], start=True, stop=True)
                if nk * P > BANK:
                    mm = nc.tensor.matmul(K.psum[:, b + 1, 0:nk * P - BANK], q_of(h)[:, q0:q0 + P], k_of(h)[:, k0 + BANK:k0 + nk * P],
                                          start=True, stop=True)
                mm.then_inc(scores.sem, 1)

            def turn(i):
                nk = work[i][1][2]
                pe.wait_ge(normed.sem, normed.base + i + 1)
                if i >= 1:
                    pe.wait_ge(evac_v.sem, evac_v.base + i)
                    pe.wait_ge(evac_a.sem, evac_a.base + i)
                for k in range(nk):
                    t = nc.tensor.transpose(K.psum[:, 4 + 2 * k // nk, k % (nk // 2) * P:(k % (nk // 2) + 1) * P], W[:, i % 2, k * P:(k + 1) * P], ident)
                t.then_inc(turned.sem, 1)

            def out(i):
                h, (q0, kt0, nk) = work[i]
                pe.wait_ge(evac_v.sem, evac_v.base + i + 1)
                pe.wait_ge(evac_a.sem, evac_a.base + i + 1)
                if i >= 2:
                    pe.wait_ge(out_used.sem, out_used.base + i - 1)
                o = K.psum[(h % 2) * 64:(h % 2) * 64 + 64, 6 + i % 2, 0:P]
                for k in range(nk):
                    mm = nc.tensor.matmul(o, v_of(h, kt0 + k), WT[:, i % 2, k * P:(k + 1) * P], start=k == 0, stop=k == nk - 1)
                mm.then_inc(out_done.sem, 1)

            score(0)
            for i in range(len(work)):
                if i + 1 < len(work):
                    score(i + 1)
                if i >= 1:
                    out(i - 1)
                turn(i)
            out(len(work) - 1)

        @block.vector
        def _(dve):
            def head(i):
                h, (q0, kt0, nk) = work[i]
                b = i % 2
                ps = K.psum[:, 2 * b:2 * b + 2, :].rearrange("p b n -> p (b n)")[:, 0:nk * P]
                if table is not None:
                    if i % nq == 0:
                        dve.wait_ge(t_in[h % 2].sem, t_in[h % 2].base + 16 * (h // 2 + 1))
                        dve.tensor_tensor(table[:, h % 2, :, :], table[:, h % 2, :, :],
                                                                B.const("window").unsqueeze(1).to_broadcast([P, 14, 64]), ALU.add).then_inc(K.dve_step.sem, 1)
                        dve.wait_ge(K.dve_step.sem, K.dve_step.next())
                    dve.wait_ge(scores.sem, scores.base + i + 1)
                    if i >= 2:
                        dve.wait_ge(exped.sem, exped.base + i - 1)
                    bias = table[:, h % 2, 6 - 2 * (q0 // P):14 - 2 * (q0 // P), :].rearrange("p m c -> p (m c)")
                    dve.scalar_tensor_tensor(S[:, b, 0:BANK], ps[:, 0:BANK], scale, bias, ALU.mult, ALU.add).then_inc(K.dve_step.sem, 1)
                    dve.wait_ge(K.dve_step.sem, K.dve_step.next())
                    dve.wait_ge(copied.sem, copied.base + i + 1)
                    src, f = S[:, b, 0:nk * P], -1.0
                else:
                    dve.wait_ge(scores.sem, scores.base + i + 1)
                    src, f = ps, -scale
                dve.tensor_reduce(m[:, b, 0:1], src, AX, ALU.max).then_inc(K.dve_step.sem, 1)
                dve.wait_ge(K.dve_step.sem, K.dve_step.next())
                dve.tensor_scalar(m[:, b, 1:2], m[:, b, 0:1], f, None, ALU.mult).then_inc(maxed.sem, 1)

            def probs(i):
                nk = work[i][1][2]
                b = i % 2
                dve.wait_ge(exped.sem, exped.base + i + 1)
                dve.reciprocal(m[:, b, 3:4], m[:, b, 2:3]).then_inc(K.dve_step.sem, 1)
                dve.wait_ge(K.dve_step.sem, K.dve_step.next())
                dve.tensor_scalar(W[:, b, 0:nk * P], W[:, b, 0:nk * P], m[:, b, 3:4], None, ALU.mult).then_inc(normed.sem, 1)

            def take(i):
                h, (q0, kt0, nk) = work[i]
                dve.wait_ge(turned.sem, turned.base + i + 1)
                if i >= 2:
                    dve.wait_ge(out_done.sem, out_done.base + i - 1)
                n = nk * P // 2
                dve.tensor_copy(WT[:, i % 2, 0:n], K.psum[:, 4, 0:n]).then_inc(evac_v.sem, 1)

            def finish(i):
                h, (q0, kt0, nk) = work[i]
                dve.wait_ge(out_done.sem, out_done.base + i + 1)
                o = out_of(h, slice(q0, q0 + P))
                dve.tensor_tensor(o, K.psum[(h % 2) * 64:(h % 2) * 64 + 64, 6 + i % 2, 0:P], o, ALU.mult).then_inc(out_used.sem, 1)

            head(0)
            for i in range(len(work)):
                probs(i)
                if i + 1 < len(work):
                    head(i + 1)
                take(i)
                if i >= 1:
                    finish(i - 1)
            finish(len(work) - 1)

        @block.scalar
        def _(act):
            def exp(i):
                nk = work[i][1][2]
                b = i % 2
                ps = K.psum[:, 2 * b:2 * b + 2, :].rearrange("p b n -> p (b n)")[:, 0:nk * P]
                if table is not None:
                    act.wait_ge(scores.sem, scores.base + i + 1)
                    nc.scalar.activation(S[:, b, BANK:TOK], ps[:, BANK:TOK], ACT.Copy, scale=scale).then_inc(copied.sem, 1)
                    src, f = S[:, b, 0:nk * P], 1.0
                else:
                    src, f = ps, scale
                act.wait_ge(maxed.sem, maxed.base + i + 1)
                if i >= 2:
                    act.wait_ge(turned.sem, turned.base + i - 1)
                nc.scalar.activation(W[:, b, 0:nk * P], src, ACT.Exp, bias=m[:, b, 1:2], scale=f, accum_out=m[:, b, 2:3]).then_inc(exped.sem, 1)

            def take(i):
                nk = work[i][1][2]
                act.wait_ge(turned.sem, turned.base + i + 1)
                if i >= 2:
                    act.wait_ge(out_done.sem, out_done.base + i - 1)
                n = nk * P // 2
                nc.scalar.activation(WT[:, i % 2, n:2 * n], K.psum[:, 5, 0:n], ACT.Copy).then_inc(evac_a.sem, 1)

            exp(0)
            for i in range(len(work)):
                if i + 1 < len(work):
                    exp(i + 1)
                take(i)

        if table is not None:
            @block.sync
            def _(sp):
                for h in range(n_heads):
                    if h >= 2:
                        sp.wait_ge(maxed.sem, maxed.base + (h - 1) * nq)
                    sp.dma_start(table[:, h % 2, :, :], table_src[h].rearrange("p (m c) -> p m c", c=64)).then_inc(t_in[h % 2].sem, 16)
    for c in (scores, maxed, exped, normed, turned, evac_v, evac_a, out_done, out_used):
        c.rise(len(work))
    if table is not None:
        copied.rise(len(work))
        for c in t_in:
            c.rise(8 * n_heads)


def mla(K, B, ctx, H, A):
    nc = K.nc
    za = K.sb(ctx, "mla_out", [P, 4, TOK])
    both = (LAT, CTXG)
    with ExitStack() as tmp:
        lat = K.sb(tmp, "mla_lat", [P, 8, TOK])
        kb = K.sb(tmp, "mla_k", [96, A_HEADS, TOK])
        krope = kb[64:96, 0, :]
        units = linear_units([0, 1], KT, H, both, lambda e, g: ("vector", copy_to(lat[:, e, span(g)])))
        for g in both:
            units.append((2, 64, 32, g[1], lambda w, g=g: [(w[:, k, :], H[:, k, span(g)]) for k in range(KT)], "vector",
                          copy_to(krope[:, span(g)])))
        units += [(3,) + u[1:] for u in linear_units([0], KT, H, both, lambda e, g: ("scalar", act_to(nc, za[:, e, span(g)], ACT.Silu)))]
        products(K, "mla_in", units)

        def apply(dve, r, arg):
            g, a, n, gain = arg
            for k in range(n):
                i = dve.scalar_tensor_tensor(lat[:, a + k, span(g)], lat[:, a + k, span(g)], B.col(gain)[:, k:k + 1], r, ALU.mult, ALU.mult)
            return i
        norms(K, [([lat[:, k, span(g)] for k in range(6)], (g, 0, 6, "q_norm")) for g in both], B.const("ones"), 1.0 / Q_LORA, B.eps(0), apply)
        norms(K, [([lat[:, 6 + k, span(g)] for k in range(2)], (g, 6, 2, "kv_norm")) for g in both], B.const("ones"), 1.0 / KV_LORA, B.eps(0), apply)

        qb = H
        v = K.sb(tmp, "mla_v", [P, TOK // P, 512])
        units = []
        for h in range(A_HEADS):
            for g in both:
                units.append((h // 4, 0, 96, g[1], lambda w, h=h, g=g: [(w[:, k, (h % 4) * 96:(h % 4 + 1) * 96], lat[:, k, span(g)]) for k in range(6)],
                              ("vector", "scalar")[h % 2], copy_to(qb[0:96, h, span(g)]) if h % 2 == 0 else act_to(nc, qb[0:96, h, span(g)], ACT.Copy)))
        products(K, "q_up", units)
        units = []
        for h in range(A_HEADS):
            for g in both:
                units.append((0, 0, 64, g[1], lambda w, h=h, g=g: [(w[:, k, h * 128:h * 128 + 64], lat[:, 6 + k, span(g)]) for k in range(2)],
                              ("vector", "scalar")[h % 2], copy_to(kb[0:64, h, span(g)]) if h % 2 == 0 else act_to(nc, kb[0:64, h, span(g)], ACT.Copy)))
        for t in range(TOK // P):
            units.append((0, 0, P, 512, lambda w, t=t: [(lat[:, 6 + k, t * P:(t + 1) * P],
                                                         w[:, k, :].rearrange("p (h c) -> p h c", c=128)[:, :, 64:128]) for k in range(2)],
                          "vector", copy_to(v[:, t, :])))

        def spread(dve):
            for h in range(1, A_HEADS):
                dve.tensor_copy(kb[64:96, h, :], krope)
        products(K, "kv_up", units, before=spread)

        def apply_head(dve, r, arg):
            x, gain = arg
            return dve.scalar_tensor_tensor(x, x, B.col(gain)[0:96, 0:1], r, ALU.mult, ALU.mult)
        head_norms(K, B, [(8 * n + h, g, x[0:96, h, span(g)], (x[0:96, h, span(g)], gain)) for n, (x, gain) in enumerate(((qb, "q_gain"), (kb, "k_gain")))
                          for h in range(A_HEADS) for g in both], 96, 1, 1.0 / A_QK, B.eps(0), apply_head)

        rot = lat[0:96, 0:2, 0:SEQ]
        table = lat[:, 2:4, :].rearrange("p a t -> p (a t)")[:, 0:2 * SEQ + P]
        loaded = K.count("setup_loaded")
        with nc.Block() as block:
            @block.sync
            def _(sp):
                sp.dma_start(table, A["tables"][:, 0:2 * SEQ + P]).then_inc(loaded.sem, 16)
                sp.wait_ge(loaded.sem, loaded.base + 16)
        loaded.rise(16)
        units = []
        for n, (x, h) in enumerate([(x, h) for x in (qb, kb) for h in range(A_HEADS)]):
            def turn(eng, _, ps, x=x, h=h, n=n):
                t = x[64:96, h, 0:SEQ]
                eng.tensor_tensor(rot[64:96, n % 2, :], ps[64:96, :], table[64:96, SEQ:2 * SEQ], ALU.mult)
                eng.tensor_tensor(t, t, table[64:96, 0:SEQ], ALU.mult).then_inc(K.dve_step.sem, 1)
                eng.wait_ge(K.dve_step.sem, K.dve_step.next())
                return eng.tensor_tensor(t, t, rot[64:96, n % 2, :], ALU.add)
            units.append((None, 0, 96, SEQ, lambda w, x=x, h=h: [(table[0:96, 2 * SEQ:2 * SEQ + 96], x[0:96, h, 0:SEQ])], "vector", turn))
        products(K, "", units)
        with ExitStack() as att:
            tiles = [(q * P, 0, 6) for q in range(4)] + [(SEQ + q * P, 4, 2) for q in range(2)]
            attention(K, B, att, "mla", A_HEADS, tiles, lambda h: qb[0:96, h, :], lambda h: kb[0:96, h, :],
                      lambda h, t: v[:, t, h * 64:(h + 1) * 64],
                      lambda h, s: za[(h % 2) * 64:(h % 2) * 64 + 64, h // 2, s], float(A_QK) ** -0.5, K.sb(att, "attention", [P, 6, TOK]))
    return za


def residual_units(K, B, layer, tiles, kt, src_of, groups):
    units = []
    for t in tiles:
        for e in range(4):
            for c, g in groups:
                ch = 4 * t + e
                def f(eng, _, ps, ch=ch, c=c, g=g):
                    return eng.scalar_tensor_tensor(B.x(ch, g), ps, B.mod[:, layer, 16 + ch, c:c + 1], B.x(ch, g), ALU.mult, ALU.add)
                units.append((t, 0, P, g[1], lambda w, e=e, g=g: [(w[:, k, e * P:(e + 1) * P], src_of(k)[:, span(g)]) for k in range(kt)], "vector", f))
    return units


def odd_layer(K, B, A):
    nc = K.nc
    both = (LAT, CTXG)
    with ExitStack() as ctx:
        H = K.sb(ctx, "h", [P, KT, TOK])
        normed(K, B, H)
        products(K, "modulation1", modulation_units(K, nc, B, 1, 6))
        modulated(K, B, 1, H)
        q, k = K.sb(ctx, "od_q", [P, KT, SEQ]), K.sb(ctx, "od_k", [P, KT, TOK])
        v, z = K.sb(ctx, "od_v", [P, TOK // P, D]), K.sb(ctx, "od_z", [P, KT, SEQ])
        units = linear_units([0, 1], KT, H, (LAT,), lambda e, g: ("vector", copy_to(q[:, e, :])))
        units += linear_units([2, 3], KT, H, both, lambda e, g: ("vector", copy_to(k[:, e - 8, span(g)])))
        for c in range(2):
            for t in range(TOK // P):
                units.append((4 + c, 0, P, 512, lambda w, t=t: [(H[:, j, t * P:(t + 1) * P], w[:, j, :]) for j in range(KT)],
                              "vector", copy_to(v[:, t, c * 512:(c + 1) * 512])))
        units += linear_units([6, 7], KT, H, (LAT,), lambda e, g: ("scalar", act_to(nc, z[:, e - 24, :], ACT.Silu)))
        products(K, "od_in", units)

        def apply(dve, r, arg):
            x, gain = arg
            return dve.scalar_tensor_tensor(x, x, B.col(gain), r, ALU.mult, ALU.mult)
        head_norms(K, B, [(2 * e, LAT, q[:, e, :], (q[:, e, :], "od_q_gain")) for e in range(KT)] +
                   [(16 + 2 * e, g, k[:, e, span(g)], (k[:, e, span(g)], "od_k_gain")) for e in range(KT) for g in both],
                   P, 2, 1.0 / 64, B.eps(0), apply)
        table = K.sb(ctx, "bias_table", [P, 2, 14, 64])
        rows = lambda h: slice(64 * (h % 2), 64 * (h % 2) + 64)
        attention(K, B, ctx, "od", C_HEADS, [(i * P, 0, 6) for i in range(4)], lambda h: q[rows(h), h // 2, :], lambda h: k[rows(h), h // 2, :],
                  lambda h, t: v[:, t, h * 64:(h + 1) * 64], lambda h, s: z[rows(h), h // 2, s], 0.125, H, table, A["bias"])
        products(K, "od_out", residual_units(K, B, 1, [0, 1], KT, lambda j: z[:, j, :], [(0, LAT)]))


def conv_mixer(K, B, A, layer, G):
    nc = K.nc
    j = layer // 3
    dve_done, act_done = K.count("vector_freed"), K.count("scalar_freed")
    with ExitStack() as ctx:
        cg = K.sb(ctx, "conv_cg", [P, SEQ])
        u = K.sb(ctx, "conv_u", [P, SEQ + 2])
        acc = K.sb(ctx, "conv_sum", [P, SEQ])
        sz = K.sb(ctx, "conv_z", [P, 2, SEQ])
        one_engine(K, "vector", lambda dve: dve.memset(u[:, 0:2], 0.0))
        units = []
        for e in range(KT):
            tap = [B.col("conv_k")[:, 24 * j + 8 * i + e:24 * j + 8 * i + e + 1] for i in range(3)]

            def take_cg(eng, _, ps, e=e):
                if e:
                    eng.wait_ge(dve_done.sem, dve_done.base + 3 * e)
                return eng.tensor_copy(cg[:, :], ps)

            def take_h(eng, _, ps, e=e, tap=tap):
                eng.wait_ge(dve_done.sem, dve_done.base + 3 * e + 1)
                eng.tensor_tensor(u[:, 2:SEQ + 2], ps, cg[:, :], ALU.mult).then_inc(K.dve_step.sem, 1)
                eng.wait_ge(K.dve_step.sem, K.dve_step.next())
                eng.tensor_scalar(acc[:, :], u[:, 2:SEQ + 2], tap[2], None, ALU.mult).then_inc(K.dve_step.sem, 1)
                eng.wait_ge(K.dve_step.sem, K.dve_step.next())
                eng.scalar_tensor_tensor(acc[:, :], u[:, 1:SEQ + 1], tap[1], acc[:, :], ALU.mult, ALU.add).then_inc(K.dve_step.sem, 1)
                eng.wait_ge(K.dve_step.sem, K.dve_step.next())
                return eng.scalar_tensor_tensor(acc[:, :], u[:, 0:SEQ], tap[0], acc[:, :], ALU.mult, ALU.add)

            def take_z(eng, _, ps, e=e):
                if e >= 2:
                    eng.wait_ge(dve_done.sem, dve_done.base + 3 * (e - 1))
                return nc.scalar.activation(sz[:, e % 2, :], ps, ACT.Silu)

            def take_bg(eng, _, ps, e=e):
                eng.wait_ge(dve_done.sem, dve_done.base + 3 * e + 2)
                eng.tensor_tensor(acc[:, :], ps, acc[:, :], ALU.mult).then_inc(K.dve_step.sem, 1)
                eng.wait_ge(K.dve_step.sem, K.dve_step.next())
                eng.wait_ge(act_done.sem, act_done.base + e + 1)
                return eng.tensor_tensor(G[:, e, :], acc[:, :], sz[:, e % 2, :], ALU.mult)
            units += [("vector", take_cg), ("vector", take_h), ("scalar", take_z), ("vector", take_bg)]
        dense(K, f"conv_in{layer}", lambda k, g: B.X[:, k, :], (LAT,), 4 * KT, lambda e, g: units[e])


def ssm_mixer(K, B, A, G):
    nc = K.nc
    PI2, MAGIC = 6.2831850, 12582912.0
    with ExitStack() as ctx:
        U = K.sb(ctx, "ssm_u", [P, KT, SEQ])
        Y = K.sb(ctx, "ssm_y", [P, KT, SEQ])
        dense(K, "ssm_in", lambda k, g: B.X[:, k, :], (LAT,), 16,
              lambda e, g: ("vector", copy_to(U[:, e, :])) if e < 8 else ("scalar", act_to(nc, G[:, e - 8, :], ACT.Silu)))
        NP = GROUPS // 2
        with ExitStack() as tmp:
            time = K.sb(tmp, "time", [P, SEQ])
            bw = K.sb(tmp, "ssm_b", [P, 2, KT, P])
            cw = K.sb(tmp, "ssm_c", [P, 2, NP, 32])
            cs = K.sb(tmp, "ssm_c_scaled", [P, 3, NP, 32])
            s = K.sb(tmp, "ssm_scalars", [P, 14, NP])
            dt, mag, turn, sn, csn, ar, ai, inv, cr, ci, t0, t1, xr, rnd = (s[:, i, :] for i in range(14))
            loaded, a1, v1 = K.count("setup_loaded"), K.count("scalar_part"), K.count("vector_part")
            with nc.Block() as block:
                @block.sync
                def _(sp):
                    sp.dma_start(time[:, :], A["tables"][:, 2 * SEQ + P:3 * SEQ + P]).then_inc(loaded.sem, 16)
                    for i, n in enumerate(("ssm_b_re_2", "ssm_b_im_2")):
                        sp.dma_start(bw[:, i, :, :], A[n].rearrange("k p m -> p k m")).then_inc(loaded.sem, 16)
                    for i, n in enumerate(("ssm_c_re_2", "ssm_c_im_2")):
                        sp.dma_start(cw[:, i, :, :], A[n]).then_inc(loaded.sem, 16)
                    sp.wait_ge(loaded.sem, loaded.base + 80)

                @block.scalar
                def _(act):
                    nc.scalar.activation(dt, B.col("log_dt"), ACT.Exp).then_inc(a1.sem, 1)
                    act.wait_ge(v1.sem, v1.base + 1)
                    nc.scalar.activation(mag, xr, ACT.Exp).then_inc(a1.sem, 1)
                    act.wait_ge(v1.sem, v1.base + 2)
                    nc.scalar.activation(sn, turn, ACT.Sin, scale=PI2)
                    nc.scalar.activation(csn, t0, ACT.Sin, scale=PI2).then_inc(a1.sem, 1)

                @block.vector
                def _(dve):

                    def wrap(dst, x):
                        dve.tensor_scalar(rnd, x, MAGIC, MAGIC, ALU.add, ALU.subtract).then_inc(K.dve_step.sem, 1)
                        dve.wait_ge(K.dve_step.sem, K.dve_step.next())
                        dve.tensor_tensor(dst, x, rnd, ALU.subtract).then_inc(K.dve_step.sem, 1)
                        dve.wait_ge(K.dve_step.sem, K.dve_step.next())
                    dve.wait_ge(a1.sem, a1.base + 1)
                    dve.tensor_tensor(xr, B.col("lam_re"), dt, ALU.mult).then_inc(v1.sem, 1)
                    dve.tensor_tensor(t1, B.col("lam_im"), dt, ALU.mult).then_inc(K.dve_step.sem, 1)
                    dve.wait_ge(K.dve_step.sem, K.dve_step.next())
                    dve.tensor_scalar(t1, t1, 0.15915494309189535, None, ALU.mult).then_inc(K.dve_step.sem, 1)
                    dve.wait_ge(K.dve_step.sem, K.dve_step.next())
                    wrap(turn, t1)
                    dve.tensor_scalar(t1, turn, 0.25, None, ALU.add).then_inc(K.dve_step.sem, 1)
                    dve.wait_ge(K.dve_step.sem, K.dve_step.next())
                    dve.tensor_scalar(rnd, t1, MAGIC, MAGIC, ALU.add, ALU.subtract).then_inc(K.dve_step.sem, 1)
                    dve.wait_ge(K.dve_step.sem, K.dve_step.next())
                    dve.tensor_tensor(t0, t1, rnd, ALU.subtract).then_inc(v1.sem, 1)
                    dve.wait_ge(a1.sem, a1.base + 3)
                    dve.tensor_tensor(ar, mag, csn, ALU.mult).then_inc(K.dve_step.sem, 1)
                    dve.wait_ge(K.dve_step.sem, K.dve_step.next())
                    dve.tensor_tensor(ai, mag, sn, ALU.mult).then_inc(K.dve_step.sem, 1)
                    dve.wait_ge(K.dve_step.sem, K.dve_step.next())
                    dve.tensor_scalar(ar, ar, -1.0, None, ALU.add).then_inc(K.dve_step.sem, 1)
                    dve.wait_ge(K.dve_step.sem, K.dve_step.next())
                    lr, li = B.col("lam_re"), B.col("lam_im")
                    dve.tensor_tensor(t0, lr, lr, ALU.mult).then_inc(K.dve_step.sem, 1)
                    dve.wait_ge(K.dve_step.sem, K.dve_step.next())
                    dve.tensor_tensor(t1, li, li, ALU.mult).then_inc(K.dve_step.sem, 1)
                    dve.wait_ge(K.dve_step.sem, K.dve_step.next())
                    dve.tensor_tensor(t0, t0, t1, ALU.add).then_inc(K.dve_step.sem, 1)
                    dve.wait_ge(K.dve_step.sem, K.dve_step.next())
                    dve.reciprocal(inv, t0).then_inc(K.dve_step.sem, 1)
                    dve.wait_ge(K.dve_step.sem, K.dve_step.next())
                    dve.tensor_tensor(t0, ar, lr, ALU.mult).then_inc(K.dve_step.sem, 1)
                    dve.wait_ge(K.dve_step.sem, K.dve_step.next())
                    dve.tensor_tensor(t1, ai, li, ALU.mult).then_inc(K.dve_step.sem, 1)
                    dve.wait_ge(K.dve_step.sem, K.dve_step.next())
                    dve.tensor_tensor(t0, t0, t1, ALU.add).then_inc(K.dve_step.sem, 1)
                    dve.wait_ge(K.dve_step.sem, K.dve_step.next())
                    dve.tensor_tensor(cr, t0, inv, ALU.mult).then_inc(K.dve_step.sem, 1)
                    dve.wait_ge(K.dve_step.sem, K.dve_step.next())
                    dve.tensor_tensor(t0, ai, lr, ALU.mult).then_inc(K.dve_step.sem, 1)
                    dve.wait_ge(K.dve_step.sem, K.dve_step.next())
                    dve.tensor_tensor(t1, ar, li, ALU.mult).then_inc(K.dve_step.sem, 1)
                    dve.wait_ge(K.dve_step.sem, K.dve_step.next())
                    dve.tensor_tensor(t0, t0, t1, ALU.subtract).then_inc(K.dve_step.sem, 1)
                    dve.wait_ge(K.dve_step.sem, K.dve_step.next())
                    dve.tensor_tensor(ci, t0, inv, ALU.mult).then_inc(K.dve_step.sem, 1)
                    dve.wait_ge(K.dve_step.sem, K.dve_step.next())
                    dve.wait_ge(loaded.sem, loaded.base + 80)
                    crb, cib = (x.unsqueeze(2).to_broadcast([P, NP, 32]) for x in (cr, ci))
                    dve.tensor_tensor(cs[:, 0, :, :], cw[:, 0, :, :], crb, ALU.mult).then_inc(K.dve_step.sem, 1)
                    dve.wait_ge(K.dve_step.sem, K.dve_step.next())
                    dve.tensor_tensor(cs[:, 1, :, :], cw[:, 1, :, :], cib, ALU.mult).then_inc(K.dve_step.sem, 1)
                    dve.wait_ge(K.dve_step.sem, K.dve_step.next())
                    dve.tensor_tensor(cs[:, 0, :, :], cs[:, 0, :, :], cs[:, 1, :, :], ALU.subtract).then_inc(K.dve_step.sem, 1)
                    dve.wait_ge(K.dve_step.sem, K.dve_step.next())
                    dve.tensor_scalar(cs[:, 1, :, :], cs[:, 0, :, :], -1.0, None, ALU.mult).then_inc(K.dve_step.sem, 1)
                    dve.wait_ge(K.dve_step.sem, K.dve_step.next())
                    dve.tensor_tensor(cw[:, 0, :, :], cw[:, 0, :, :], cib, ALU.mult).then_inc(K.dve_step.sem, 1)
                    dve.wait_ge(K.dve_step.sem, K.dve_step.next())
                    dve.tensor_tensor(cw[:, 1, :, :], cw[:, 1, :, :], crb, ALU.mult).then_inc(K.dve_step.sem, 1)
                    dve.wait_ge(K.dve_step.sem, K.dve_step.next())
                    dve.tensor_tensor(cw[:, 0, :, :], cw[:, 0, :, :], cw[:, 1, :, :], ALU.add).then_inc(K.dve_step.sem, 1)
                    dve.wait_ge(K.dve_step.sem, K.dve_step.next())
                    dve.tensor_scalar(cs[:, 2, :, :], cw[:, 0, :, :], -1.0, None, ALU.mult).then_inc(K.dve_step.sem, 1)
                    dve.wait_ge(K.dve_step.sem, K.dve_step.next())
            loaded.rise(80)
            a1.rise(3)
            v1.rise(2)

            ph = K.sb(tmp, "ssm_phase", [P, 2, 3, SEQ])
            tb = K.sb(tmp, "ssm_table", [P, 2, 2, SEQ])
            bu = K.sb(tmp, "ssm_bu", [P, 2, 2, SEQ])
            w = K.sb(tmp, "ssm_turned", [P, 4, SEQ])
            zz = K.sb(tmp, "ssm_scan", [P, 2, 2, SEQ])
            mm = K.sb(tmp, "ssm_products", [P, 2, 4, SEQ])
            bu_done, bu_taken, tables, phases, scanned, prod_v, prod_p, y_done, y_taken = (K.count(x) for x in (
                "product_done", "scalar_freed", "scalar_part", "pool_part", "vector_part", "vector_freed", "pool_freed", "sum_done", "root_used"))
            turned, turns_made, rounded = K.count("turned"), K.count("turns_made"), K.count("turns_rounded")
            rd = K.sb(tmp, "ssm_whole_turns", [P, 2, SEQ])
            with nc.Block() as block:
                @block.tensor
                def _(pe):
                    def bring(q):
                        r = slice(32 * (q % 4), 32 * (q % 4) + 32)
                        if q >= 2:
                            pe.wait_ge(bu_taken.sem, bu_taken.base + q - 1)
                        for i in range(2):
                            x = nc.tensor.matmul(K.psum[:, 2 * (q % 2) + i, :], bw[r, i, q // 4, :], U[r, q // 4, :], start=True, stop=True,
                                                 tile_position=(32 * (q % 4), 0))
                        x.then_inc(bu_done.sem, 1)
                    bring(0)
                    for q in range(NP):
                        if q + 1 < NP:
                            bring(q + 1)
                        if q % 4 == 0 and q >= 8:
                            pe.wait_ge(y_taken.sem, y_taken.base + q // 4 - 1)
                        pe.wait_ge(prod_v.sem, prod_v.base + q + 1)
                        pe.wait_ge(prod_p.sem, prod_p.base + q + 1)
                        o = K.psum[32 * (q % 4):32 * (q % 4) + 32, 4 + q // 4 % 2, :]
                        for n, c in enumerate((0, 1, 2, 2)):
                            x = nc.tensor.matmul(o, cs[:, c, q, :], mm[:, q % 2, n, :], start=n == 0, stop=n == 3, tile_position=(0, 32 * (q % 4)))
                        x.then_inc(y_done.sem, 1)

                @block.gpsimd
                def _(pool):
                    def fraction(q):
                        pool.wait_ge(rounded.sem, rounded.base + q + 1)
                        if q >= 2:
                            pool.wait_ge(tables.sem, tables.base + q - 1)
                        pool.tensor_tensor(ph[:, q % 2, 1, :], ph[:, q % 2, 0, :], rd[:, q % 2, :], ALU.subtract).then_inc(phases.sem, 1)

                    def finish(q):
                        pool.wait_ge(scanned.sem, scanned.base + q + 1)
                        if q >= 2:
                            pool.wait_ge(y_done.sem, y_done.base + q - 1)
                        pool.tensor_tensor(mm[:, q % 2, 2, :], tb[:, q % 2, 0, :], zz[:, q % 2, 0, :], ALU.mult)
                        pool.tensor_tensor(mm[:, q % 2, 3, :], tb[:, q % 2, 1, :], zz[:, q % 2, 1, :], ALU.mult).then_inc(prod_p.sem, 1)
                    fraction(0)
                    for q in range(NP):
                        if q + 1 < NP:
                            fraction(q + 1)
                        finish(q)

                @block.scalar
                def _(act):
                    def turns(q):
                        if q >= 2:
                            act.wait_ge(phases.sem, phases.base + q - 1)
                        nc.scalar.activation(ph[:, q % 2, 0, :], time[:, :], ACT.Copy, scale=turn[:, q:q + 1]).then_inc(turns_made.sem, 1)
                    turns(0)
                    for q in range(NP):
                        if q + 1 < NP:
                            turns(q + 1)
                        if q >= 2:
                            act.wait_ge(prod_v.sem, prod_v.base + q - 1)
                            act.wait_ge(prod_p.sem, prod_p.base + q - 1)
                        act.wait_ge(bu_done.sem, bu_done.base + q + 1)
                        for i in range(2):
                            x = nc.scalar.activation(bu[:, q % 2, i, :], K.psum[:, 2 * (q % 2) + i, :], ACT.Copy)
                        x.then_inc(bu_taken.sem, 1)
                        act.wait_ge(phases.sem, phases.base + q + 1)
                        nc.scalar.activation(ph[:, q % 2, 2, :], ph[:, q % 2, 1, :], ACT.Abs).then_inc(K.act_step.sem, 1)
                        nc.scalar.activation(tb[:, q % 2, 0, :], ph[:, q % 2, 1, :], ACT.Sin, scale=PI2)
                        act.wait_ge(K.act_step.sem, K.act_step.next())
                        nc.scalar.activation(tb[:, q % 2, 1, :], ph[:, q % 2, 2, :], ACT.Sin, scale=-PI2, bias=B.eps(3)).then_inc(tables.sem, 1)

                @block.vector
                def _(dve):
                    def whole(q):
                        dve.wait_ge(turns_made.sem, turns_made.base + q + 1)
                        if q >= 2:
                            dve.wait_ge(phases.sem, phases.base + q - 1)
                        dve.tensor_scalar(rd[:, q % 2, :], ph[:, q % 2, 0, :], MAGIC, MAGIC, ALU.add, ALU.subtract).then_inc(rounded.sem, 1)
                    whole(0)
                    for q in range(NP):
                        re, im, sn_, cs_ = bu[:, q % 2, 0, :], bu[:, q % 2, 1, :], tb[:, q % 2, 0, :], tb[:, q % 2, 1, :]
                        if q + 1 < NP:
                            whole(q + 1)
                        dve.wait_ge(bu_taken.sem, bu_taken.base + q + 1)
                        dve.wait_ge(tables.sem, tables.base + q + 1)
                        dve.tensor_tensor(w[:, 0, :], re, cs_, ALU.mult)
                        dve.tensor_tensor(w[:, 1, :], im, sn_, ALU.mult)
                        dve.tensor_tensor(w[:, 2, :], im, cs_, ALU.mult)
                        dve.tensor_tensor(w[:, 3, :], re, sn_, ALU.mult).then_inc(turned.sem, 1)
                        dve.wait_ge(turned.sem, turned.base + q + 1)
                        dve.tensor_tensor(w[:, 0, :], w[:, 0, :], w[:, 1, :], ALU.add)
                        dve.tensor_tensor(w[:, 2, :], w[:, 2, :], w[:, 3, :], ALU.subtract).then_inc(K.dve_step.sem, 1)
                        dve.wait_ge(K.dve_step.sem, K.dve_step.next())
                        if q >= 2:
                            dve.wait_ge(prod_p.sem, prod_p.base + q - 1)
                            dve.wait_ge(prod_v.sem, prod_v.base + q - 1)
                            dve.wait_ge(y_done.sem, y_done.base + q - 1)
                        r = mag[:, q:q + 1].to_broadcast([P, SEQ])
                        dve.tensor_tensor_scan(zz[:, q % 2, 0, :], r, w[:, 0, :], 0.0, ALU.mult, ALU.add)
                        dve.tensor_tensor_scan(zz[:, q % 2, 1, :], r, w[:, 2, :], 0.0, ALU.mult, ALU.add).then_inc(scanned.sem, 1)
                        dve.wait_ge(scanned.sem, scanned.base + q + 1)
                        dve.tensor_tensor(mm[:, q % 2, 0, :], cs_, zz[:, q % 2, 0, :], ALU.mult)
                        dve.tensor_tensor(mm[:, q % 2, 1, :], sn_, zz[:, q % 2, 1, :], ALU.mult).then_inc(prod_v.sem, 1)
                        if q % 4 == 3:
                            j = q // 4
                            dve.wait_ge(y_done.sem, y_done.base + q + 1)
                            dve.scalar_tensor_tensor(Y[:, j, :], U[:, j, :], B.col("d_skip")[:, j:j + 1], K.psum[:, 4 + j % 2, :],
                                                     ALU.mult, ALU.add).then_inc(y_taken.sem, 1)
            for c in (bu_done, bu_taken, tables, phases, scanned, prod_v, prod_p, y_done, turned, turns_made, rounded):
                c.rise(NP)
            y_taken.rise(KT)
        B.dump("ssm_y", Y[:, :, :])

        gelued = K.count("scalar_part")
        with nc.Block() as block:
            @block.scalar
            def _(act):
                for e in range(KT):
                    nc.scalar.activation(Y[:, e, :], Y[:, e, :], ACT.Gelu_apprx_tanh).then_inc(gelued.sem, 1)

            @block.vector
            def _(dve):
                for e in range(KT):
                    dve.wait_ge(gelued.sem, gelued.base + e + 1)
                    dve.tensor_tensor(G[:, e, :], G[:, e, :], Y[:, e, :], ALU.mult)
        gelued.rise(KT)
        taken = K.count("scalar_freed")

        def sigm(e, g):
            def f(eng, _, ps):
                return nc.scalar.activation(U[:, e, :], ps, ACT.Sigmoid, bias=B.col("b_glu")[:, e:e + 1])
            return "scalar", f

        def beside(dve):
            for e in range(KT):
                dve.wait_ge(taken.sem, taken.base + e + 1)
                dve.tensor_tensor(G[:, e, :], G[:, e, :], U[:, e, :], ALU.mult)
        dense(K, "ssm_glu", lambda k, g: Y[:, k, :], (LAT,), 8, sigm, beside=beside)


def rwkv_mixer(K, B, A, G):
    nc = K.nc
    NC, HP = SEQ // CH, 4
    with ExitStack() as ctx:
        w2 = K.sb(ctx, "lora_w2", [64, 2, D])
        low = K.sb(ctx, "lora_low", [64, 2, SEQ])
        r, k, v = (K.sb(ctx, "rwkv_" + n, [P, HP, SEQ]) for n in "rkv")
        aw = K.sb(ctx, "rwkv_aw", [P, 2 * HP, SEQ])
        a, w = aw[:, 0:HP, :], aw[:, HP:2 * HP, :]

        def lerp(n, dx, xs, first=False):
            def f(dve):
                if first:
                    dve.tensor_scalar(dx[:, :, 0:1], B.X[:, :, 0:1], -1.0, None, ALU.mult).then_inc(K.dve_step.sem, 1)
                    dve.wait_ge(K.dve_step.sem, K.dve_step.next())
                    dve.tensor_tensor(dx[:, :, 1:SEQ], B.X[:, :, 0:SEQ - 1], B.X[:, :, 1:SEQ], ALU.subtract).then_inc(K.dve_step.sem, 1)
                    dve.wait_ge(K.dve_step.sem, K.dve_step.next())
                for e in range(KT):
                    c = 8 * n + e
                    dve.scalar_tensor_tensor(xs[:, e, :], dx[:, e, :], B.col("mu")[:, c:c + 1], B.X[:, e, 0:SEQ], ALU.mult, ALU.add)
            return f

        for half in range(2):
            tile0 = 4 * half
            with ExitStack() as pro:
                dx, xs = aw, K.sb(pro, "xs", [P, KT, SEQ])
                order = [4, 5, 3, 0, 1, 2] if half == 0 else [0, 1, 2]
                one_engine(K, "vector", lerp(order[0], dx, xs, True))
                for i, n in enumerate(order):
                    x = lambda k, g: xs[:, k, :]
                    nxt = lerp(order[i + 1], dx, xs) if i + 1 < len(order) else None
                    if n >= 4:
                        j, name, func = n - 4, ("rwkv_w", "rwkv_a")[n - 4], (ACT.Tanh, ACT.Copy)[n - 4]
                        products(K, name, [(0, 0, 64, SEQ, lambda s: [(s[:, c, :], xs[:, c, :]) for c in range(KT)], "scalar",
                                            act_to(nc, low[:, j, :], func))], load=(w2[:, j, :], A[("rwkv_w2_2", "rwkv_a2_2")[j]][0]))
                        one_engine(K, "vector", nxt)
                    elif n == 3:
                        dense(K, "rwkv_z", x, (LAT,), 8, lambda e, g: ("scalar", act_to(nc, G[:, e, :], ACT.Silu)), beside=nxt)
                    else:
                        dst = (r, k, v)[n]
                        dense(K, f"rwkv_{'rkv'[n]}{half}", x, (LAT,), 4, lambda e, g, dst=dst: ("vector", copy_to(dst[:, e, :])), beside=nxt)
            units = []
            for n, (dst, bias) in enumerate(((w, "w0"), (a, "a0"))):
                for e in range(HP):
                    def f(eng, _, ps, dst=dst, bias=bias, e=e):
                        return nc.scalar.activation(dst[:, e, :], ps, ACT.Sigmoid, bias=B.col(bias)[:, tile0 + e:tile0 + e + 1])
                    c = (tile0 + e) * P
                    units.append((None, 0, P, SEQ, lambda s, n=n, c=c: [(w2[:, n, c:c + P], low[:, n, :])], "scalar", f))
            products(K, "", units)
            with ExitStack() as tmp:
                rwkv_chunks(K, B, tmp, half, r, k, v, a, w, G)


def rwkv_chunks(K, B, ctx, half, r, k, v, a, w, G):
    nc = K.nc
    NC, HP, tile0 = SEQ // CH, 4, 4 * half
    col = lambda n, e: B.col(n)[:, tile0 + e:tile0 + e + 1]
    O = K.sb(ctx, "rwkv_out", [P, HP, SEQ])
    kk = K.sb(ctx, "rwkv_kk", [P, HP, SEQ])
    pend = K.sb(ctx, "rwkv_end", [P, HP, NC])
    flat = lambda x: x.rearrange("p e t -> p (e t)")
    decay = -0.6065306597126334
    inner = ExitStack()
    ex = K.sb(inner, "rwkv_exp", [P, 3, HP, SEQ])

    def prepare(dve):
        for e in range(HP):
            dve.tensor_scalar(kk[:, e, :], k[:, e, :], col("k_k", e), None, ALU.mult).then_inc(K.dve_step.sem, 1)
            dve.wait_ge(K.dve_step.sem, K.dve_step.next())
            dve.tensor_scalar(ex[:, 0, e, :], a[:, e, :], -1.0, col("k_a", e), ALU.add, ALU.mult).then_inc(K.dve_step.sem, 1)
            dve.wait_ge(K.dve_step.sem, K.dve_step.next())
            dve.scalar_tensor_tensor(k[:, e, :], ex[:, 0, e, :], 1.0, k[:, e, :], ALU.add, ALU.mult).then_inc(K.dve_step.sem, 1)
            dve.wait_ge(K.dve_step.sem, K.dve_step.next())
            dve.scalar_tensor_tensor(O[:, e, :], r[:, e, :], col("r_k", e), k[:, e, :], ALU.mult, ALU.mult).then_inc(K.dve_step.sem, 1)
            dve.wait_ge(K.dve_step.sem, K.dve_step.next())
            dve.tensor_scalar(w[:, e, :], w[:, e, :], decay, None, ALU.mult).then_inc(K.dve_step.sem, 1)
            dve.wait_ge(K.dve_step.sem, K.dve_step.next())
            dve.tensor_tensor_scan(ex[:, 0, e, :], B.const("restart")[:, 0:SEQ], w[:, e, :], 0.0, ALU.mult, ALU.add).then_inc(K.dve_step.sem, 1)
            dve.wait_ge(K.dve_step.sem, K.dve_step.next())
        dve.tensor_copy(pend[:, :, :], ex[:, 0, :, :].rearrange("p e (c t) -> p e c t", t=CH)[:, :, :, CH - 1]).then_inc(K.dve_step.sem, 1)
        dve.wait_ge(K.dve_step.sem, K.dve_step.next())
        dve.tensor_tensor(flat(w[:, :, :]), flat(ex[:, 0, :, :]), flat(w[:, :, :]), ALU.subtract)
    one_engine(K, "vector", prepare)

    units = []
    for e in range(HP):
        def f(eng, _, ps, e=e):
            return eng.tensor_tensor(O[:, e, :], ps, v[:, e, :], ALU.mult)
        units.append((None, 0, P, SEQ, lambda s, e=e: [(B.const("ones64"), O[:, e, :])], "vector", f))
    products(K, "", units)

    def exps(act):
        cum = flat(ex[:, 0, :, :])
        nc.scalar.activation(flat(ex[:, 1, :, :]), cum, ACT.Exp)
        nc.scalar.activation(flat(ex[:, 2, :, :]), cum, ACT.Exp, scale=-1.0)
        nc.scalar.activation(flat(w[:, :, :]), flat(w[:, :, :]), ACT.Exp)
        nc.scalar.activation(pend.rearrange("p e c -> p (e c)"), pend.rearrange("p e c -> p (e c)"), ACT.Exp)
    one_engine(K, "scalar", exps)

    def apply(dve, rinv, e):
        dve.tensor_tensor(kk[:, e, :], kk[:, e, :], rinv, ALU.mult).then_inc(K.dve_step.sem, 1)
        dve.wait_ge(K.dve_step.sem, K.dve_step.next())
        dve.tensor_tensor(r[:, e, :], r[:, e, :], ex[:, 1, e, :], ALU.mult)
        dve.tensor_tensor(k[:, e, :], k[:, e, :], ex[:, 2, e, :], ALU.mult)
        dve.tensor_tensor(a[:, e, :], a[:, e, :], ex[:, 2, e, :], ALU.mult).then_inc(K.dve_step.sem, 1)
        dve.wait_ge(K.dve_step.sem, K.dve_step.next())
        dve.tensor_tensor(a[:, e, :], a[:, e, :], kk[:, e, :], ALU.mult)
        return dve.tensor_tensor(w[:, e, :], w[:, e, :], kk[:, e, :], ALU.mult)
    head_norms(K, B, [(2 * e, LAT, kk[:, e, :], e) for e in range(HP)], P, 2, 1.0, None, apply, "norm")
    inner.close()

    at, bt, kt, rt = w, a, k, r
    by_chunk = lambda x: x[:, :, :].rearrange("p e (c t) -> p e c t", t=CH)
    bT, RB, YT, XX = by_chunk(a), by_chunk(w), by_chunk(k), by_chunk(v)
    KV = K.sb(ctx, "rwkv_kv", [P, HP, NC, CH])
    names = ("aT", "kT", "vT", "Bo", "AK", "RK", "Bi", "Ai", "B2", "A2", "R")
    T = {n: K.sb(ctx, "rwkv_" + n, [P, 2, NC, CH]) for n in names}
    T["E"], T["GG"] = T["AK"], T["kT"]
    done, taken = K.count("product_done"), K.count("vector_freed")
    chunk = lambda x, e: x[:, e, :].rearrange("p (c t) -> p c t", t=CH)
    eye = B.const("ident")

    def mask(n):
        return B.const(n).unsqueeze(1).to_broadcast([P, NC, CH])

    def masked(dve, ps, pairs):
        for dst, m in pairs:
            i = dve.tensor_tensor(dst, ps, mask(m), ALU.mult)
        return i

    def rounds(e):
        A_, B_, K_, R_, V_ = (chunk(x, e) for x in (at, bt, kt, rt, v))
        t = {n: x[:, e % 2, :, :] for n, x in T.items()}
        keep = lambda dst: lambda dve, ps: dve.tensor_copy(dst, ps)
        cut = lambda *pairs: lambda dve, ps: masked(dve, ps, pairs)
        plus = lambda dst: lambda dve, ps: dve.tensor_tensor(dst, ps, dst, ALU.add)
        minus = lambda dst, x: lambda dve, ps: dve.scalar_tensor_tensor(dst, ps, -1.0, x, ALU.mult, ALU.add)
        turn = None
        return [
            [(B_, A_, cut((t["Bi"], "before_in"), (t["Bo"], "before_out"))), (A_, B_, cut((t["Ai"], "after_in"))),
             (K_, A_, cut((t["AK"], "before"))), (A_, turn, keep(t["aT"]))],
            [(B_, R_, cut((RB[:, e, :, :], "upto"))), (B_, turn, keep(bT[:, e, :, :])),
             (K_, R_, cut((t["RK"], "upto"))), (K_, turn, keep(t["kT"]))],
            [(V_, turn, keep(t["vT"])), (t["Ai"], t["Bi"], keep(t["B2"])), (t["Bi"], t["Ai"], keep(t["A2"])),
             lambda dve: dve.tensor_tensor(t["R"], mask("eye64"), t["Bi"], ALU.subtract)],
            [(t["AK"], t["vT"], keep(t["GG"])), (t["kT"], t["vT"], keep(KV[:, e, :, :])), (t["vT"], t["RK"], keep(chunk(kk, e))),
             (t["A2"], t["R"], plus(t["R"]))],
            [(t["A2"], t["B2"], keep(t["Bi"])), (t["B2"], t["A2"], keep(t["Ai"]))],
            [(t["Ai"], t["R"], plus(t["R"])), (t["Bi"], t["Ai"], keep(t["A2"]))],
            [(t["A2"], t["R"], plus(t["R"]))],
            [(t["R"], turn, keep(t["E"]))],
            [(t["E"], t["Bo"], keep(t["Bi"])), (t["Bo"], t["E"], keep(t["Ai"]))],
            [(t["Bi"], t["Ai"], keep(t["A2"]))],
            [(t["A2"], t["R"], plus(t["R"]))],
            [(t["Ai"], t["R"], minus(t["B2"], t["R"]))],
            [(t["B2"], t["GG"], keep(XX[:, e, :, :])), (t["aT"], t["B2"], keep(YT[:, e, :, :]))],
        ]

    of = [rounds(e) for e in range(HP)]
    turns = [(2 * g + p, of[2 * g + p][n]) for g in range(HP // 2) for n in range(len(of[0])) for p in range(2)]
    upto = [0]
    for _, units in turns:
        upto.append(upto[-1] + len(units))
    n_done = [0]
    for _, units in turns:
        n_done.append(n_done[-1] + sum(isinstance(u, tuple) for u in units))
    with nc.Block() as block:
        @block.tensor
        def _(pe):
            for n, (e, units) in enumerate(turns):
                if n >= 2:
                    pe.wait_ge(taken.sem, taken.base + upto[n - 1])
                for i, u in enumerate(x for x in units if isinstance(x, tuple)):
                    for c in range(NC):
                        for h in range(2):
                            s = slice(64 * h, 64 * h + 64)
                            rhs = eye[s, s] if u[1] is None else u[1][s, c, :]
                            mm = nc.tensor.matmul(K.psum[s, 4 * (e % 2) + i, c * CH:(c + 1) * CH], u[0][s, c, :], rhs, start=c == 0,
                                                  stop=c == NC - 1, skip_group_check=True)
                    mm.then_inc(done.sem, 1)

        @block.vector
        def _(dve):
            for n, (e, units) in enumerate(turns):
                dve.wait_ge(done.sem, done.base + n_done[n + 1])
                if n >= 2:
                    dve.wait_ge(taken.sem, taken.base + upto[n - 1])
                for i, u in enumerate(units):
                    if isinstance(u, tuple):
                        u[2](dve, K.psum[:, 4 * (e % 2) + i, :].rearrange("p (c t) -> p c t", t=CH)).then_inc(taken.sem, 1)
                    else:
                        u(dve).then_inc(taken.sem, 1)
    done.rise(n_done[-1])
    taken.rise(upto[-1])

    two = lambda n: T[n][:, 0, :, :].rearrange("p (a e) t -> p a e t", a=2)
    Hs, U, Hg = two("aT"), two("kT"), two("vT")[:, 0, :, :]
    uh, ud, od, hd, hs = (K.count(x) for x in ("product_done", "vector_part", "sum_done", "root_used", "vector_freed"))
    bank = lambda i: K.psum[:, i, 0:HP * CH].rearrange("p (e t) -> p e t", t=CH)
    with nc.Block() as block:
        @block.tensor
        def _(pe):
            def each(c, b, pairs, sem):
                for e in range(HP):
                    for h in range(2):
                        s = slice(64 * h, 64 * h + 64)
                        for n, (x, y) in enumerate(pairs):
                            mm = nc.tensor.matmul(bank(b)[s, e, :], x(s, e), y(s, e), start=n == 0 and e == 0, stop=n == len(pairs) - 1 and e == HP - 1,
                                                  skip_group_check=True)
                mm.then_inc(sem, 1)
            for c in range(NC):
                H, Uc = Hs[:, c % 2, :, :], U[:, c % 2, :, :]
                pe.wait_ge(hs.sem, hs.base + c + 1)
                if c >= 1:
                    pe.wait_ge(ud.sem, ud.base + c)
                each(c, 0, [(lambda s, e: YT[s, e, c, :], lambda s, e: H[s, e, :])], uh.sem)
                pe.wait_ge(ud.sem, ud.base + c + 1)
                if c >= 1:
                    pe.wait_ge(hd.sem, hd.base + c)
                each(c, 2, [(lambda s, e: bT[s, e, c, :], lambda s, e: Uc[s, e, :])], uh.sem)
                each(c, 4 + c % 2, [(lambda s, e: H[s, e, :], lambda s, e: chunk(rt, e)[s, c, :]),
                                    (lambda s, e: Uc[s, e, :], lambda s, e: RB[s, e, c, :])], od.sem)

        @block.vector
        def _(dve):
            dve.memset(Hs[:, 0, :, :], 0.0).then_inc(hs.sem, 1)
            for c in range(NC):
                H, Uc = Hs[:, c % 2, :, :], U[:, c % 2, :, :]
                dve.wait_ge(hs.sem, hs.base + c + 1)
                dve.tensor_tensor(Hg[:, :, :], H, KV[:, :, c, :], ALU.add)
                dve.wait_ge(uh.sem, uh.base + 2 * c + 1)
                dve.scalar_tensor_tensor(Uc, bank(0), -1.0, XX[:, :, c, :], ALU.mult, ALU.subtract).then_inc(ud.sem, 1)
                dve.wait_ge(ud.sem, ud.base + c + 1)
                dve.wait_ge(uh.sem, uh.base + 2 * c + 2)
                dve.tensor_tensor(Hg[:, :, :], bank(2), Hg[:, :, :], ALU.add).then_inc(K.dve_step.sem, 1)
                dve.wait_ge(K.dve_step.sem, K.dve_step.next())
                if c >= 1:
                    dve.wait_ge(od.sem, od.base + c)
                dve.tensor_tensor(Hs[:, (c + 1) % 2, :, :], Hg[:, :, :], pend[:, :, c].unsqueeze(2).to_broadcast([P, HP, CH]), ALU.mult).then_inc(hs.sem, 1)
                o = kk[:, :, c * CH:(c + 1) * CH]
                dve.wait_ge(od.sem, od.base + c + 1)
                dve.tensor_tensor(o, bank(4 + c % 2), o, ALU.add).then_inc(hd.sem, 1)
    uh.rise(2 * NC)
    ud.rise(NC)
    od.rise(NC)
    hd.rise(NC)
    hs.rise(NC + 1)

    center(K, B, [([kk[:, e, :]], [kk[:, e, :]]) for e in range(HP)], B.const("ones64"), 1.0 / CH, T["Bi"][:, 0, :, :].rearrange("p c t -> p (c t)"))

    def readout(dve, rinv, e):
        x, g = kk[:, e, :], G[:, tile0 + e, :]
        dve.scalar_tensor_tensor(x, x, col("lnx_g", e), rinv, ALU.mult, ALU.mult).then_inc(K.dve_step.sem, 1)
        dve.wait_ge(K.dve_step.sem, K.dve_step.next())
        dve.scalar_tensor_tensor(x, x, col("lnx_b", e), O[:, e, :], ALU.add, ALU.add).then_inc(K.dve_step.sem, 1)
        dve.wait_ge(K.dve_step.sem, K.dve_step.next())
        return dve.tensor_tensor(g, g, x, ALU.mult)
    head_norms(K, B, [(2 * e, LAT, kk[:, e, :], e) for e in range(HP)], P, 2, 1.0 / CH, B.eps(2), readout)


def center(K, B, items, ones, scale, mean):
    nc = K.nc
    units = []
    freed = K.count("vector_freed")
    for n, (srcs, dsts) in enumerate(items):
        def f(eng, _, ps, n=n, srcs=srcs, dsts=dsts):
            if n:
                eng.wait_ge(freed.sem, freed.base + n)
            eng.tensor_scalar(mean, ps, scale, None, ALU.mult).then_inc(K.dve_step.sem, 1)
            eng.wait_ge(K.dve_step.sem, K.dve_step.next())
            for x, y in zip(srcs, dsts):
                i = eng.tensor_tensor(y, x, mean, ALU.subtract)
            return i
        units.append((None, 0, P, SEQ, lambda w, srcs=srcs: [(ones, x) for x in srcs], "vector", f))
    products(K, "", units)


def second_layer(K, B, A, layer):
    nc = K.nc
    with ExitStack() as ctx:
        G = K.sb(ctx, "mixer_gated", [P, KT, SEQ])
        (conv_mixer, ssm_mixer, rwkv_mixer)[layer % 3](*((K, B, A, layer, G) if layer % 3 == 0 else (K, B, A, G)))
        B.dump(f"G{layer}", G[:, :, :])

        def add(e, g):
            def f(eng, _, ps):
                return eng.scalar_tensor_tensor(B.X[:, e, :], B.X[:, e, :], ALPHA, ps, ALU.mult, ALU.add)
            return "vector", f
        pT, pp = K.sb(ctx, "ple_in", [P, 2, SEQ]), K.sb(ctx, "ple", [P, KT, SEQ])
        dense(K, f"mix_out{layer}", lambda k, g: G[:, k, :], (LAT,), 8, add,
              load=(pT[:, :, :], A["p"][layer].rearrange("(k p) t -> p k t", p=P)))
        B.dump(f"rm{layer}", B.X[:, :, :])
        taken = K.count("scalar_freed")
        products(K, f"ple_p{layer}", linear_units([0], 2, pT, (LAT,), lambda e, g: ("vector", copy_to(pp[:, e, :])), width=8))

        def sigm(e, g):
            return "scalar", act_to(nc, G[:, e, :], ACT.Sigmoid)

        def beside(dve):
            for e in range(KT):
                dve.wait_ge(taken.sem, taken.base + e + 1)
                dve.tensor_tensor(pp[:, e, :], pp[:, e, :], G[:, e, :], ALU.mult).then_inc(K.dve_step.sem, 1)
                dve.wait_ge(K.dve_step.sem, K.dve_step.next())
                dve.tensor_tensor(pp[:, e, :], pp[:, e, :], B.X[:, e, :], ALU.add)
        dense(K, f"ple_g{layer}", lambda k, g: B.X[:, k, :], (LAT,), 8, sigm, beside=beside)
        B.dump(f"r{layer}", pp[:, :, :])
        center(K, B, [([pp[:, e, :] for e in range(KT)], [pp[:, e, :] for e in range(KT)])], B.const("ones"), 1.0 / D, pT[:, 0, :])

        def apply(dve, r, _):
            for e in range(KT):
                i = dve.scalar_tensor_tensor(B.X[:, e, :], pp[:, e, :], B.col("ln_g")[:, 8 * layer + e:8 * layer + e + 1], r, ALU.mult, ALU.mult)
            i.then_inc(K.dve_step.sem, 1)
            dve.wait_ge(K.dve_step.sem, K.dve_step.next())
            for e in range(KT):
                i = dve.tensor_scalar(B.X[:, e, :], B.X[:, e, :], B.col("ln_b")[:, 8 * layer + e:8 * layer + e + 1], None, ALU.add)
            return i
        norms(K, [([pp[:, e, :] for e in range(KT)], 0)], B.const("ones"), 1.0 / D, B.eps(1), apply)


def program(nc, A, out, stop=99, dumps=None):
    dumps = dumps or {}
    with ExitStack() as ctx:
        K, B = Core(nc, ctx), Buffers()
        where_c, n_c = columns()
        where_k, packed, _ = shape_constants()
        B.X = K.sb(ctx, "residual", [P, KT, SEQ])
        B.cols = K.sb(ctx, "columns", [P, n_c])
        B.consts = K.sb(ctx, "constants", [P, packed.shape[1]])
        B.col = lambda n: B.cols[:, where_c[n][0]:where_c[n][0] + where_c[n][1]]
        B.const = lambda n: B.consts[:, where_k[n][0]:where_k[n][0] + where_k[n][1]]
        B.eps = lambda i: B.const("eps")[:, i:i + 1]
        B.x = lambda k, g: B.X[:, k, :] if g == LAT else B.XC[:, k, :]
        stored = K.count("stored")

        def dump(name, ap):
            if name in dumps:
                with nc.Block() as block:
                    @block.sync
                    def _(sp):
                        sp.dma_start(dumps[name], ap).then_inc(stored.sem, 16)
                        sp.wait_ge(stored.sem, stored.base + 16)
                stored.rise(16)
        B.dump = dump
        plan_weights(K, A)
        with ExitStack() as first:
            B.XC = K.sb(first, "residual_ctx", [P, KT, CTX])
            B.scond = K.sb(first, "silu_cond", [P, KT, 2])
            B.mod = K.sb(first, "modulation", [P, 2, 24, 2])
            B.gain = K.sb(first, "norm_gain", [P, KT, 2])
            setup(K, B, A)
            with ExitStack() as layer:
                H = K.sb(layer, "h", [P, KT, TOK])
                normed(K, B, H)
                products(K, "modulation0", modulation_units(K, nc, B, 0, 6))
                modulated(K, B, 0, H)
                zb = gla(K, B, layer, H, A)
                za = mla(K, B, layer, H, A)
                products(K, "ev_out", residual_units(K, B, 0, [0, 1], 8, lambda k: za[:, k, :] if k < 4 else zb[:, k - 4, :],
                                                     [(0, LAT), (1, CTXG)]))
            dump("x1", B.X[:, :, :])
            odd_layer(K, B, A)
            dump("x2", B.X[:, :, :])
        for layer in range(4):
            if stop < layer + 3:
                return
            second_layer(K, B, A, layer)
            dump(f"ln{layer}", B.X[:, :, :])
        with nc.Block() as block:
            @block.sync
            def _(sp):
                sp.dma_start(out.rearrange("(k p) t -> p k t", p=P), B.X[:, :, :]).then_inc(stored.sem, 16)
                sp.wait_ge(stored.sem, stored.base + 16)
        stored.rise(16)


def host_layout(inputs):
    import numpy as np
    a = {n: np.asarray(v) for n, v in inputs.items()}
    col = lambda v: np.reshape(v, (-1, P)).T
    pad = lambda v: np.pad(np.reshape(v, (-1, 1)), ((0, P - v.size), (0, 0)))
    pairs = lambda v: np.reshape(v, (GROUPS // 2, P)).T
    where, n = columns()
    vectors = {
        "cond": np.stack([col(a["c"]), col(a["c_ctx"])], 2).reshape(P, 2 * KT), "norm_g": col(a["norm_g"]), "ada_b": col(a["ada_b"]),
        "q_norm": col(a["ev_q_norm"]), "kv_norm": col(a["ev_kv_norm"]), "q_gain": pad(a["ev_q_gain"]), "k_gain": pad(a["ev_k_gain"]),
        "gate_b": col(a["ev_gate_b"]), "gla_norm": col(a["ev_gla_norm"]), "od_q_gain": np.tile(a["od_q_gain"].reshape(-1, 1), (2, 1)),
        "od_k_gain": np.tile(a["od_k_gain"].reshape(-1, 1), (2, 1)), "conv_k": col(a["conv_k_2"]), "lam_re": pairs(a["ssm_lam_re_2"]),
        "lam_im": pairs(a["ssm_lam_im_2"]), "log_dt": pairs(np.repeat(a["ssm_log_dt_2"], STATE, axis=-1)), "d_skip": col(a["ssm_d_2"]),
        "b_glu": col(a["ssm_b_glu_2"]), "mu": col(a["rwkv_mu_2"]), "w0": col(a["rwkv_w0_2"]), "a0": col(a["rwkv_a0_2"]),
        "k_k": col(a["rwkv_k_k_2"]), "k_a": col(a["rwkv_k_a_2"]), "r_k": col(a["rwkv_r_k_2"]), "lnx_g": col(a["rwkv_lnx_g_2"]),
        "lnx_b": col(a["rwkv_lnx_b_2"]), "ln_g": col(a["ln_g_2"]), "ln_b": col(a["ln_b_2"])}
    out = {"columns": np.ascontiguousarray(np.concatenate([vectors[k] for k in where], axis=1)),
           "constants": shape_constants()[1], "tables": shape_constants()[2]}
    out["x"] = np.ascontiguousarray(a["x"][0].T)
    out["ctx"] = np.ascontiguousarray(a["ctx"][0].T)
    out["p"] = np.ascontiguousarray(a["p_2"][:, 0].transpose(0, 2, 1))
    c = np.arange(64)
    idx = np.clip(c[None, :] - c[:, None] + 15, 0, 30)
    r = a["od_rpb"][0]
    t = np.stack([r[:, 1 - e:15 - e][:, :, idx].transpose(0, 2, 1, 3) for e in (0, 1)], 1)
    out["bias"] = np.ascontiguousarray(t.reshape(C_HEADS, P, 14 * 64))
    for n in WEIGHTS:
        out[n] = np.ascontiguousarray(a[n])
    for n in ("ssm_b_re_2", "ssm_b_im_2"):
        z = np.zeros((GROUPS // 2, 2, GRP, 2, STATE), np.float32)
        for g in range(2):
            z[:, g, :, g, :] = a[n][0, g::2].transpose(0, 2, 1)
        out[n] = z.reshape(KT, P, P)
    for n in ("ssm_c_re_2", "ssm_c_im_2"):
        z = np.zeros((GROUPS // 2, 2, STATE, 2, GRP), np.float32)
        for g in range(2):
            z[:, g, :, g, :] = a[n][0, g::2].transpose(0, 2, 1)
        out[n] = np.ascontiguousarray(z.reshape(GROUPS // 2, P, 2 * GRP).transpose(1, 0, 2))
    return out


WEIGHTS = ("ada_w", "ev_w_in", "ev_w_uq", "ev_w_ukv", "ev_gate_w", "ev_w_out", "od_w_in", "od_w_out", "conv_w_in_2", "conv_w_out_2",
           "ssm_w_in_2", "ssm_w_glu_2", "ssm_w_out_2", "rwkv_w_rkvz_2", "rwkv_w1_2", "rwkv_w2_2", "rwkv_a1_2", "rwkv_a2_2", "rwkv_w_out_2",
           "ple_proj_2", "ple_gate_2")


def kernel(**inputs):
    import concourse.bacc as bacc
    from concourse.bass_utils import run_bass_kernel_spmd
    import numpy as np

    nc = bacc.Bacc("TRN2", target_bir_lowering=False, num_devices=1)
    host = host_layout(inputs)
    arrays = {f"{n}_dram": a for n, a in host.items()}
    A = {n: nc.dram_tensor(f"{n}_dram", a.shape, F32, kind="ExternalInput").ap() for n, a in host.items()}
    out = nc.dram_tensor("out_dram", (D, SEQ), F32, kind="ExternalOutput").ap()
    program(nc, A, out)
    got = run_bass_kernel_spmd(nc, [arrays], core_ids=[0])
    return np.ascontiguousarray(got.results[0]["out_dram"].T)[None]
```

```python
from contextlib import ExitStack

import concourse.bass as bass
from concourse import mybir

F32 = mybir.dt.float32
FR = mybir.dt.float32r
ALU = mybir.AluOpType
ACT = mybir.ActivationFunctionType
AX = mybir.AxisListType.X

P = 128
D = 1024
KT = D // P
SEQ, CTX = 512, 256
TOK = SEQ + CTX
LAT = (0, SEQ)
CTXG = (SEQ, CTX)
BANK = 512
RING = 2
SLOT = KT * 512
EPS = 1e-6
LN_EPS = 1e-5
GN_EPS = 64e-5
A_HEADS, A_NOPE, A_ROPE, A_V, A_QK = 8, 64, 32, 64, 96
Q_LORA, KV_LORA = 768, 256
B_HEADS, B_DK, B_DV, RANK, TAU = 4, 64, 128, 16, 16.0
CH = 64
NCH = TOK // CH
C_HEADS = 16
ALPHA = 8 ** 0.25
GROUPS, GRP, STATE = 64, 16, 64
HEADS = 16


class Count:

    def __init__(self, sem):
        self.sem, self.base = sem, 0

    def rise(self, n):
        self.base += n

    def next(self):
        self.base += 1
        return self.base


class Core:

    def __init__(self, nc, ctx):
        self.nc, self.ctx = nc, ctx
        self.psum = ctx.enter_context(nc.psum_tensor("psum", [P, 8, BANK], F32))
        self.ring = ctx.enter_context(nc.sbuf_tensor("ring", [P, RING, SLOT], F32))
        self.landed = [self.sem(f"weights_landed{i}") for i in range(RING)]
        self.counts = {}
        self.dve_step, self.act_step, self.pool_step = (Count(self.sem(n)) for n in ("vector_step", "scalar_step", "gpsimd_step"))
        self.weights, self.first, self.named = [], {}, 0

    def sem(self, name):
        return self.ctx.enter_context(self.nc.semaphore(name))

    def count(self, name):
        if name not in self.counts:
            self.counts[name] = Count(self.sem(name))
        return self.counts[name]

    def sb(self, ctx, name, shape, dtype=F32):
        return ctx.enter_context(self.nc.sbuf_tensor(self.name(name), shape, dtype))

    def name(self, what):
        self.named += 1
        return f"{what}_{self.named}"

    def plan(self, name, tiles):
        self.first[name] = len(self.weights)
        self.weights += tiles

    def send_weights(self, sp, n):
        if n >= len(self.weights):
            return
        dst, parts = self.ring[:, n % RING, :], self.weights[n]
        width = sum(a.shape[1] for a in parts)
        kt = parts[0].shape[0] // P
        view = dst[:, 0:kt * width].rearrange("p (k c) -> p k c", c=width)
        at = 0
        for a in parts:
            w = a.shape[1]
            sp.dma_start(view[:, :, at:at + w], a.rearrange("(k p) c -> p k c", p=P)).then_inc(self.landed[n % RING], 16)
            at += w

    def sent(self, n):
        return 16 * sum(len(self.weights[i]) for i in range(n % RING, n + 1, RING))

    def slot(self, n):
        parts = self.weights[n]
        width = sum(a.shape[1] for a in parts)
        kt = parts[0].shape[0] // P
        return self.ring[:, n % RING, 0:kt * width].rearrange("p (k c) -> p k c", c=width)


def products(K, name, units, beside=None, before=None, load=None):
    nc = K.nc
    base = K.first.get(name, 0)
    done, by_dve, by_act = K.count("product_done"), K.count("vector_freed"), K.count("scalar_freed")
    freed = {"vector": by_dve, "scalar": by_act}
    loaded = K.count("setup_loaded")
    took, n_of = [], {"vector": 0, "scalar": 0}
    last_use = {}
    for i, u in enumerate(units):
        n_of[u[5]] += 1
        took.append(n_of[u[5]])
        if u[0] is not None:
            last_use[u[0]] = i + 1
    assert sorted(last_use) == list(range(len(last_use)))

    with nc.Block() as block:
        @block.tensor
        def _(pe):
            seen = set()
            for i, (tile, p0, m, n, operands, _, _) in enumerate(units):
                if i >= 8:
                    bank_free = freed[units[i - 8][5]]
                    pe.wait_ge(bank_free.sem, bank_free.base + took[i - 8])
                if tile is not None and tile not in seen:
                    seen.add(tile)
                    pe.wait_ge(K.landed[(base + tile) % RING], K.sent(base + tile))
                pairs = operands(K.slot(base + tile) if tile is not None else None)
                out = K.psum[p0:p0 + m, i % 8, 0:n]
                if pairs[0] == "T":
                    nc.tensor.transpose(out, pairs[1], pairs[2]).then_inc(done.sem, 1)
                    continue
                for j, (lhsT, rhs) in enumerate(pairs):
                    mm = nc.tensor.matmul(out, lhsT, rhs, start=j == 0, stop=j == len(pairs) - 1)
                mm.then_inc(done.sem, 1)

        @block.vector
        def _(dve):
            if before:
                before(dve)
            for i, (_, p0, m, n, _, engine, evacuate) in enumerate(units):
                if engine == "vector":
                    dve.wait_ge(done.sem, done.base + i + 1)
                    evacuate(dve, dve, K.psum[p0:p0 + m, i % 8, 0:n]).then_inc(by_dve.sem, 1)
            if beside:
                beside(dve)

        @block.scalar
        def _(act):
            for i, (_, p0, m, n, _, engine, evacuate) in enumerate(units):
                if engine == "scalar":
                    act.wait_ge(done.sem, done.base + i + 1)
                    evacuate(act, act, K.psum[p0:p0 + m, i % 8, 0:n]).then_inc(by_act.sem, 1)

        @block.sync
        def _(sp):
            if load:
                sp.dma_start(*load).then_inc(loaded.sem, 16)
            for t in range(len(last_use)):
                sp.wait_ge(done.sem, done.base + last_use[t])
                K.send_weights(sp, base + t + RING)
            if load:
                sp.wait_ge(loaded.sem, loaded.base + 16)

    if load:
        loaded.rise(16)
    done.rise(len(units))
    by_dve.rise(n_of["vector"])
    by_act.rise(n_of["scalar"])


def dense(K, name, src, groups, n_out, finish, kt=KT, m=P, beside=None, load=None, on_pool=None):
    nc = K.nc
    base = K.first[name]
    of = groups if isinstance(groups, list) else [groups] * n_out
    tok = max(g[0] + g[1] for g in of[0])
    work = [(e, g) for e in range(n_out) for g in of[e]]
    fin = [finish(e, g) for e, g in work]
    through = [sum(len(x) for x in of[:e]) for e in range(n_out)]
    inputs = [(k, g) for k in range(kt) for g in of[0]]
    per_slot = sum(a.shape[1] for a in K.weights[base]) // m
    done, w_high, w_low, x_high, x_low, loaded = (K.count(n) for n in (
        "product_done", "weights_high", "weights_low", "input_high", "input_low", "setup_loaded"))
    freed = {"vector": K.count("vector_freed"), "scalar": K.count("scalar_freed")}
    took, n_of = [], {"vector": 0, "scalar": 0}
    for engine, _ in fin:
        n_of[engine] += 1
        took.append(n_of[engine])
    with ExitStack() as ctx:
        xh, xl = (K.sb(ctx, n, [P, kt, tok], FR) for n in ("input_high", "input_low"))
        wh, wl = (K.sb(ctx, n, [P, 2, kt, m], FR) for n in ("weights_high", "weights_low"))

        def columns_of(e):
            c = e % per_slot * m
            return K.slot(base + e // per_slot)[:, :, c:c + m]

        with nc.Block() as block:
            @block.scalar
            def _(act):
                def weights(e):
                    if e % per_slot == 0:
                        act.wait_ge(K.landed[(base + e // per_slot) % RING], K.sent(base + e // per_slot))
                    if e >= 2:
                        act.wait_ge(done.sem, done.base + through[e - 1])
                    nc.scalar.activation(wh[:, e % 2, :, :], columns_of(e), ACT.Copy).then_inc(w_high.sem, 1)
                weights(0)
                for k, g in inputs:
                    nc.scalar.activation(xh[:, k, span(g)], src(k, g), ACT.Copy).then_inc(x_high.sem, 1)
                for i, (e, g) in enumerate(work):
                    if i == through[e] and e + 1 < n_out:
                        weights(e + 1)
                    if fin[i][0] == "scalar":
                        act.wait_ge(done.sem, done.base + i + 1)
                        fin[i][1](act, act, K.psum[0:m, i % 8, 0:g[1]]).then_inc(freed["scalar"].sem, 1)

            @block.vector
            def _(dve):
                def weights(e):
                    dve.wait_ge(w_high.sem, w_high.base + e + 1)
                    if e >= 2:
                        dve.wait_ge(done.sem, done.base + through[e - 1])
                    dve.tensor_tensor(wl[:, e % 2, :, :], columns_of(e), wh[:, e % 2, :, :].bitcast(F32), ALU.subtract).then_inc(w_low.sem, 1)
                weights(0)
                for n, (k, g) in enumerate(inputs):
                    dve.wait_ge(x_high.sem, x_high.base + n + 1)
                    dve.tensor_tensor(xl[:, k, span(g)], src(k, g), xh[:, k, span(g)].bitcast(F32), ALU.subtract).then_inc(x_low.sem, 1)
                late = beside
                for i, (e, g) in enumerate(work):
                    if i == through[e] and e + 1 < n_out:
                        weights(e + 1)
                    if late and n_of["vector"]:
                        dve.wait_ge(x_low.sem, x_low.base + len(inputs))
                        late(dve)
                        late = None
                    if fin[i][0] == "vector":
                        dve.wait_ge(done.sem, done.base + i + 1)
                        fin[i][1](dve, dve, K.psum[0:m, i % 8, 0:g[1]]).then_inc(freed["vector"].sem, 1)
                if late:
                    dve.wait_ge(x_low.sem, x_low.base + len(inputs))
                    late(dve)

            if on_pool:
                block.gpsimd(on_pool)

            @block.tensor
            def _(pe):
                for i, (e, g) in enumerate(work):
                    if i >= 8:
                        bank_free = freed[fin[i - 8][0]]
                        pe.wait_ge(bank_free.sem, bank_free.base + took[i - 8])
                    pe.wait_ge(w_low.sem, w_low.base + e + 1)
                    out = K.psum[0:m, i % 8, 0:g[1]]
                    for k in range(kt):
                        if e == 0:
                            pe.wait_ge(x_low.sem, x_low.base + inputs.index((k, g)) + 1)
                        nc.tensor.matmul(out, wh[:, e % 2, k, :], xh[:, k, span(g)], start=k == 0, stop=False)
                        nc.tensor.matmul(out, wh[:, e % 2, k, :], xl[:, k, span(g)], start=False, stop=False)
                        mm = nc.tensor.matmul(out, wl[:, e % 2, k, :], xh[:, k, span(g)], start=False, stop=k == kt - 1)
                    mm.then_inc(done.sem, 1)

            @block.sync
            def _(sp):
                if load:
                    sp.dma_start(*load).then_inc(loaded.sem, 16)
                for t in range(n_out // per_slot):
                    sp.wait_ge(w_low.sem, w_low.base + per_slot * (t + 1))
                    K.send_weights(sp, base + t + RING)
                if load:
                    sp.wait_ge(loaded.sem, loaded.base + 16)
    if load:
        loaded.rise(16)
    done.rise(len(work))
    for c in (w_high, w_low):
        c.rise(n_out)
    for c in (x_high, x_low):
        c.rise(len(inputs))
    for n, c in freed.items():
        c.rise(n_of[n])


def norms(K, items, ones, scale, eps, apply, kind="rms"):
    nc = K.nc
    sq_done, sq_used, root_done, root_used = (K.count(x) for x in (
        "square_done", "square_summed", "root_done", "root_used"))
    rows = items[0][0][0].shape[0]
    n_src = [len(s) for s, _ in items]
    upto = [sum(n_src[:i + 1]) for i in range(len(items))]
    with ExitStack() as ctx:
        sq, root, rinv = (K.sb(ctx, n, [P, 2, BANK]) for n in ("squares", "roots", "rinv"))
        with nc.Block() as block:
            @block.scalar
            def _(act):
                def take_root(i):
                    n = items[i][0][0].shape[1]
                    act.wait_ge(sq_used.sem, sq_used.base + upto[i])
                    if i >= 2:
                        act.wait_ge(root_used.sem, root_used.base + i - 1)
                    if kind == "norm":
                        nc.scalar.activation(root[0:rows, i % 2, 0:n], K.psum[0:rows, i % 2, 0:n], ACT.Sqrt).then_inc(root_done.sem, 1)
                    else:
                        nc.scalar.activation(root[0:rows, i % 2, 0:n], K.psum[0:rows, i % 2, 0:n], ACT.Sqrt,
                                             bias=eps[0:rows, :], scale=scale).then_inc(root_done.sem, 1)
                j = 0
                for i, (srcs, _) in enumerate(items):
                    for s in srcs:
                        if j >= 2:
                            act.wait_ge(sq_used.sem, sq_used.base + j - 1)
                        nc.scalar.activation(sq[0:rows, j % 2, 0:s.shape[1]], s, ACT.Square).then_inc(sq_done.sem, 1)
                        j += 1
                    if i >= 1:
                        take_root(i - 1)
                take_root(len(items) - 1)

            @block.tensor
            def _(pe):
                j = 0
                for i, (srcs, _) in enumerate(items):
                    if i >= 2:
                        pe.wait_ge(root_done.sem, root_done.base + i - 1)
                    for k, s in enumerate(srcs):
                        pe.wait_ge(sq_done.sem, sq_done.base + j + 1)
                        n = s.shape[1]
                        mm = nc.tensor.matmul(K.psum[0:rows, i % 2, 0:n], ones, sq[0:rows, j % 2, 0:n],
                                              start=k == 0, stop=k == len(srcs) - 1)
                        mm.then_inc(sq_used.sem, 1)
                        j += 1

            @block.vector
            def _(dve):
                for i, (srcs, arg) in enumerate(items):
                    n = srcs[0].shape[1]
                    dve.wait_ge(root_done.sem, root_done.base + i + 1)
                    if i >= 2:
                        dve.wait_ge(root_used.sem, root_used.base + i - 1)
                    r = rinv[0:rows, i % 2, 0:n]
                    src = root[0:rows, i % 2, 0:n]
                    if kind == "norm":
                        dve.tensor_scalar(src, src, 1e-12, None, ALU.max).then_inc(K.dve_step.sem, 1)
                        dve.wait_ge(K.dve_step.sem, K.dve_step.next())
                    dve.reciprocal(r, src).then_inc(K.dve_step.sem, 1)
                    dve.wait_ge(K.dve_step.sem, K.dve_step.next())
                    apply(dve, r, arg).then_inc(root_used.sem, 1)
        sq_done.rise(upto[-1])
        sq_used.rise(upto[-1])
        for c in (root_done, root_used):
            c.rise(len(items))


def head_norms(K, B, items, rows, per, scale, eps, apply, kind="rms", before=None):
    nc = K.nc
    sq_done, sq_used, root_done, root_used, spread_done, spread_used = (K.count(x) for x in (
        "square_done", "square_summed", "root_done", "root_used", "sum_done", "vector_freed"))
    groups = sorted({g for _, g, _, _ in items})
    order = [[it for it in items if it[1] == g] for g in groups]
    last = [sum(len(o) for o in order[:n + 1]) for n in range(len(order))]
    every = [it for o in order for it in o]
    select = "pick2" if per == 2 else "pick1"
    with ExitStack() as ctx:
        sq = K.sb(ctx, "squares", [P, 3, BANK])
        root = K.sb(ctx, "roots", [32, len(groups), BANK])
        top = max(it[0] for it in items) + per
        width = 64 if per == 2 else 1
        ones_of = K.sb(ctx, "spread_ones", [64, top, width], FR)
        split = K.sb(ctx, "roots_split", [64, len(groups), BANK], FR)
        with nc.Block() as block:
            @block.scalar
            def _(act):
                for i, (_, g, x, _) in enumerate(every):
                    if i >= 3:
                        act.wait_ge(sq_used.sem, sq_used.base + i - 2)
                    nc.scalar.activation(sq[0:rows, i % 3, 0:g[1]], x, ACT.Square).then_inc(sq_done.sem, 1)
                for n, g in enumerate(groups):
                    act.wait_ge(sq_used.sem, sq_used.base + last[n])
                    if kind == "norm":
                        nc.scalar.activation(root[:, n, 0:g[1]], K.psum[0:32, n, 0:g[1]], ACT.Sqrt).then_inc(root_done.sem, 1)
                    else:
                        nc.scalar.activation(root[:, n, 0:g[1]], K.psum[0:32, n, 0:g[1]], ACT.Sqrt, bias=eps[0:32, :],
                                             scale=scale).then_inc(root_done.sem, 1)

            @block.tensor
            def _(pe):
                i = 0
                for n, o in enumerate(order):
                    for m, (base, g, _, _) in enumerate(o):
                        pe.wait_ge(sq_done.sem, sq_done.base + i + 1)
                        nc.tensor.matmul(K.psum[0:32, n, 0:g[1]], B.const(select)[0:rows, 32 - base:64 - base], sq[0:rows, i % 3, 0:g[1]],
                                         start=m == 0, stop=m == len(o) - 1).then_inc(sq_used.sem, 1)
                        i += 1
                i = 0
                for n, o in enumerate(order):
                    pe.wait_ge(root_used.sem, root_used.base + n + 1)
                    for base, g, _, _ in o:
                        if i >= 4:
                            pe.wait_ge(spread_used.sem, spread_used.base + i - 3)
                        lhsT = ones_of[:, base:base + per, :].rearrange("p h c -> p (h c)")
                        if per == 1:
                            lhsT = lhsT.to_broadcast([64, rows])
                        nc.tensor.matmul(K.psum[0:rows, 4 + i % 4, 0:g[1]], lhsT, split[:, n, 0:g[1]], start=True,
                                         stop=True).then_inc(spread_done.sem, 1)
                        i += 1

            @block.vector
            def _(dve):
                for z in range(2):
                    dve.tensor_copy(ones_of[32 * z:32 * z + 32, :, :], B.const("ident")[0:32, 0:top].unsqueeze(2).to_broadcast([32, top, width]))
                if before:
                    before(dve)
                for n, g in enumerate(groups):
                    x = root[:, n, 0:g[1]]
                    dve.wait_ge(root_done.sem, root_done.base + n + 1)
                    if kind == "norm":
                        dve.tensor_scalar(x, x, 1e-12, None, ALU.max).then_inc(K.dve_step.sem, 1)
                        dve.wait_ge(K.dve_step.sem, K.dve_step.next())
                    dve.reciprocal(x, x).then_inc(K.dve_step.sem, 1)
                    dve.wait_ge(K.dve_step.sem, K.dve_step.next())
                    high = split[0:32, n, 0:g[1]]
                    dve.tensor_copy(high, x).then_inc(K.dve_step.sem, 1)
                    dve.wait_ge(K.dve_step.sem, K.dve_step.next())
                    dve.tensor_tensor(split[32:64, n, 0:g[1]], x, high.bitcast(F32), ALU.subtract).then_inc(root_used.sem, 1)
                for i, (_, g, _, arg) in enumerate(every):
                    dve.wait_ge(spread_done.sem, spread_done.base + i + 1)
                    apply(dve, K.psum[0:rows, 4 + i % 4, 0:g[1]], arg).then_inc(spread_used.sem, 1)
        for c in (sq_done, sq_used, spread_done, spread_used):
            c.rise(len(every))
        for c in (root_done, root_used):
            c.rise(len(groups))


def columns():
    sizes = [("cond", 2 * KT), ("norm_g", 2 * KT), ("ada_b", 48), ("q_norm", 6), ("kv_norm", 2), ("q_gain", 1), ("k_gain", 1),
             ("gate_b", 4), ("gla_norm", 4), ("od_q_gain", 1), ("od_k_gain", 1), ("conv_k", 48), ("lam_re", 32), ("lam_im", 32),
             ("log_dt", 32), ("d_skip", 8), ("b_glu", 8), ("mu", 48), ("w0", 8), ("a0", 8), ("k_k", 8), ("k_a", 8), ("r_k", 8),
             ("lnx_g", 8), ("lnx_b", 8), ("ln_g", 32), ("ln_b", 32)]
    at, out = 0, {}
    for name, n in sizes:
        out[name] = (at, n)
        at += n
    return out, at


def shape_constants():
    import numpy as np
    i = np.arange(P)
    same = lambda a, n: (a[:, None] // n) == (a[None, :] // n)
    t = np.arange(SEQ)
    inv = 10000.0 ** (-np.arange(0, 16, 2, dtype=np.float32) / 16)
    cos, sin = np.zeros((P, SEQ)), np.zeros((P, SEQ))
    swap = np.zeros((P, 96))
    for d in range(A_ROPE):
        ax, half, k = d // 16, d // 8 % 2, d % 8
        ang = ((t // 64 if ax == 0 else t % 64).astype(np.float32) * inv[k].astype(np.float32)).astype(np.float64)
        cos[64 + d] = np.cos(ang)
        sin[64 + d] = np.sin(ang) * (1 if half else -1)
        swap[64 + (d ^ 8), 64 + d] = 1
    s, u = i[:, None] % 64, np.arange(64)[None, :]
    blk = (s // 16) == (u // 16)
    c = np.arange(64)
    start = np.clip(c - 8, 0, 48)
    keep = (c[None, :] >= start[:, None]) & (c[None, :] < start[:, None] + 16)
    out = [("ident", np.eye(P)), ("ones", np.ones((P, P))), ("ones64", same(i, 64)),
           ("pick1", np.tile(np.arange(64) == 32, (P, 1))), ("pick2", np.arange(64)[None, :] == 32 + (i[:, None] >= 64)),
           ("mask_f", same(i, 64) & (i[:, None] <= i[None, :])), ("mask_b", same(i, 64) & (i[:, None] >= i[None, :])),
           ("restart", np.tile(np.arange(TOK) % CH != 0, (P, 1))), 
           ("window", np.tile(np.where(keep, 0, -1e30), (2, 1))),
           ("before", s < u), ("upto", s <= u), ("before_in", (s < u) & blk), ("before_out", (s < u) & ~blk),
           ("after_in", (s > u) & blk), ("after_out", (s > u) & ~blk), ("eye64", s == u),
           ("eps", np.stack([np.full(P, EPS), np.full(P, LN_EPS), np.full(P, GN_EPS), np.full(P, 1.5707963), np.full(P, 1.0)], 1))]
    tables = np.concatenate([cos, sin, np.pad(swap, ((0, 0), (0, 32))), np.tile(np.arange(SEQ), (P, 1))], axis=1).astype(np.float32)
    at, where = 0, {}
    for name, a in out:
        where[name] = (at, a.shape[1])
        at += a.shape[1]
    return where, np.concatenate([a.astype(np.float32) for _, a in out], axis=1), tables


def plan_weights(K, A):
    def cut(w, a, b, n=512):
        return [[w[:, i:min(i + n, b)]] for i in range(a, b, n)]
    ev = A["ev_w_in"][0]
    K.plan("modulation0", cut(A["ada_w"][0], 0, 3 * D))
    K.plan("gla_qkz", cut(ev, 1568, 2080) + cut(ev, 2624, 3136))
    K.plan("gla_v", cut(ev, 2080, 2624, 512))
    K.plan("mla_in", cut(ev, 0, 1024) + cut(ev, 1056, 1568))
    K.plan("mla_rope", cut(ev, 1024, 1056))
    K.plan("q_up", cut(A["ev_w_uq"][0], 0, 768, 384))
    K.plan("kv_up", [[A["ev_w_ukv"][0]]])
    K.plan("ev_out", cut(A["ev_w_out"][0], 0, D))
    K.plan("modulation1", cut(A["ada_w"][1], 0, 3 * D))
    od = A["od_w_in"][0]
    K.plan("od_kq", cut(od, D, 2 * D) + cut(od, 0, D))
    K.plan("od_z", cut(od, 3 * D, 4 * D))
    K.plan("od_v", cut(od, 2 * D, 3 * D))
    K.plan("od_out", cut(A["od_w_out"][0], 0, D))
    for layer in range(4):
        kind, j = layer % 3, layer // 3
        if kind == 0:
            w = A["conv_w_in_2"][j]
            K.plan(f"conv_in{layer}", [[w[:, s * D + e * P:s * D + (e + 1) * P] for s in (1, 2, 3, 0)] for e in range(KT)])
            K.plan(f"mix_out{layer}", cut(A["conv_w_out_2"][j], 0, D))
        elif kind == 1:
            K.plan("ssm_in", cut(A["ssm_w_in_2"][0], 0, 2 * D))
            K.plan("ssm_glu", cut(A["ssm_w_glu_2"][0], 0, D))
            K.plan(f"mix_out{layer}", cut(A["ssm_w_out_2"][0], 0, D))
        else:
            r = A["rwkv_w_rkvz_2"][0]
            K.plan("rwkv_w", [[A["rwkv_w1_2"][0]]])
            K.plan("rwkv_a", [[A["rwkv_a1_2"][0]]])
            K.plan("rwkv_z", cut(r[3], 0, D))
            for half in range(2):
                for n, m in enumerate("rkv"):
                    K.plan(f"rwkv_{m}{half}", [[r[n][:, half * 512:half * 512 + 512]]])
            K.plan(f"mix_out{layer}", cut(A["rwkv_w_out_2"][0], 0, D))
        K.plan(f"ple_p{layer}", [[A["ple_proj_2"][layer]]])
        K.plan(f"ple_g{layer}", cut(A["ple_gate_2"][layer], 0, D))


def span(g):
    return slice(g[0], g[0] + g[1])


def one_engine(K, engine, program):
    with K.nc.Block() as block:
        {"vector": block.vector, "scalar": block.scalar, "gpsimd": block.gpsimd}[engine](program)


def copy_to(dst):
    def f(eng, _, ps):
        return eng.tensor_copy(dst, ps)
    return f


def act_to(nc, dst, func):
    def f(eng, _, ps):
        return nc.scalar.activation(dst, ps, func)
    return f


def wide(src, kt, g):
    return [src[:, k, span(g)] for k in range(kt)]


def linear_units(tiles, kt, src, groups, finish, width=4):
    units = []
    for t in tiles:
        for e in range(width):
            for g in groups:
                engine, f = finish(t * width + e, g)
                units.append((t, 0, P, g[1],
                              lambda w, e=e, g=g: [(w[:, k, e * P:(e + 1) * P], src[:, k, span(g)]) for k in range(kt)], engine, f))
    return units


def modulation(K, B, layer):
    nc = K.nc
    name = f"modulation{layer}"
    base, n_tiles, half = K.first[name], 6, KT // 2
    pieces = [(t, h) for t in range(n_tiles) for h in range(2)]
    high, low, used, row_done, summed = (K.count(n) for n in (
        "weights_high", "weights_low", "product_done", "scalar_part", "sum_done"))
    prepared = K.count("setup_ready")
    with ExitStack() as ctx:
        wh, wl = (K.sb(ctx, n, [P, 2, half, 512], FR) for n in ("weights_high", "weights_low"))
        cond = K.sb(ctx, "cond_split", [P, KT, 4], FR)
        rows = K.sb(ctx, "modulation_rows", [4, n_tiles, 512])
        pairs = K.sb(ctx, "pairs", [4, 2])
        with nc.Block() as block:
            @block.scalar
            def _(act):
                for i, (t, h) in enumerate(pieces):
                    if h == 0:
                        act.wait_ge(K.landed[(base + t) % RING], K.sent(base + t))
                    if i >= 2:
                        act.wait_ge(used.sem, used.base + i - 1)
                    nc.scalar.activation(wh[:, i % 2, :, :], K.slot(base + t)[:, h * half:(h + 1) * half, :], ACT.Copy).then_inc(high.sem, 1)
                    if h == 1 and t >= 1:
                        act.wait_ge(used.sem, used.base + 2 * t)
                        nc.scalar.activation(rows[:, t - 1, :], K.psum[0:4, t - 1, :], ACT.Copy).then_inc(row_done.sem, 1)
                act.wait_ge(used.sem, used.base + len(pieces))
                nc.scalar.activation(rows[:, n_tiles - 1, :], K.psum[0:4, n_tiles - 1, :], ACT.Copy).then_inc(row_done.sem, 1)

            @block.vector
            def _(dve):
                dve.tensor_tensor(pairs[:, :], B.const("ident")[0:4, 0:2], B.const("ident")[0:4, 2:4], ALU.add).then_inc(prepared.sem, 1)
                dve.tensor_copy(cond[:, :, 0:2], B.scond[:, :, :]).then_inc(prepared.sem, 1)
                dve.wait_ge(prepared.sem, prepared.base + 2)
                dve.tensor_tensor(cond[:, :, 2:4], B.scond[:, :, :], cond[:, :, 0:2].bitcast(F32), ALU.subtract).then_inc(prepared.sem, 1)
                for i, (t, h) in enumerate(pieces):
                    dve.wait_ge(high.sem, high.base + i + 1)
                    if i >= 2:
                        dve.wait_ge(used.sem, used.base + i - 1)
                    dve.tensor_tensor(wl[:, i % 2, :, :], K.slot(base + t)[:, h * half:(h + 1) * half, :], wh[:, i % 2, :, :].bitcast(F32),
                                      ALU.subtract).then_inc(low.sem, 1)
                dve.wait_ge(summed.sem, summed.base + 1)
                bias = B.col("ada_b")[:, 24 * layer:24 * layer + 24].unsqueeze(2).to_broadcast([P, 24, 2])
                dve.tensor_tensor(B.mod[:, layer, :, :], K.psum[:, 7, 0:48].rearrange("p (c z) -> p c z", z=2), bias, ALU.add)

            @block.tensor
            def _(pe):
                pe.wait_ge(prepared.sem, prepared.base + 3)
                for i, (t, h) in enumerate(pieces):
                    pe.wait_ge(low.sem, low.base + i + 1)
                    for k in range(half):
                        nc.tensor.matmul(K.psum[0:4, t, :], cond[:, h * half + k, :], wh[:, i % 2, k, :], start=h == 0 and k == 0, stop=False)
                        mm = nc.tensor.matmul(K.psum[0:4, t, :], cond[:, h * half + k, :], wl[:, i % 2, k, :], start=False,
                                              stop=h == 1 and k == half - 1)
                    mm.then_inc(used.sem, 1)
                for c in range(4 * n_tiles):
                    if c % 4 == 0:
                        pe.wait_ge(row_done.sem, row_done.base + c // 4 + 1)
                    mm = nc.tensor.matmul(K.psum[:, 7, 2 * c:2 * c + 2], rows[:, c // 4, c % 4 * P:c % 4 * P + P], pairs[:, :], start=c == 0,
                                          stop=c == 4 * n_tiles - 1, skip_group_check=True)
                mm.then_inc(summed.sem, 1)

            @block.sync
            def _(sp):
                for t in range(n_tiles):
                    sp.wait_ge(low.sem, low.base + 2 * (t + 1))
                    K.send_weights(sp, base + t + RING)
    for c in (high, low, used):
        c.rise(len(pieces))
    row_done.rise(n_tiles)
    summed.rise(1)
    prepared.rise(3)


class Buffers:
    pass


def setup(K, B, A):
    nc = K.nc
    loaded, x_in = K.count("setup_loaded"), K.count("activations_loaded")
    with nc.Block() as block:
        @block.sync
        def _(sp):
            sp.dma_start(B.cols[:, :], A["columns"]).then_inc(loaded.sem, 16)
            sp.dma_start(B.consts[:, :], A["constants"]).then_inc(loaded.sem, 16)
            sp.dma_start(B.X[:, :, :], A["x"].rearrange("(k p) t -> p k t", p=P)).then_inc(x_in.sem, 16)
            sp.dma_start(B.XC[:, :, :], A["ctx"].rearrange("(k p) t -> p k t", p=P)).then_inc(x_in.sem, 16)
            for n in range(RING):
                K.send_weights(sp, n)
            sp.wait_ge(loaded.sem, loaded.base + 32)
            sp.wait_ge(x_in.sem, x_in.base + 32)

        @block.scalar
        def _(act):
            act.wait_ge(loaded.sem, loaded.base + 32)
            nc.scalar.activation(B.scond.rearrange("p k c -> p (k c)"), B.col("cond"), ACT.Silu)
    loaded.rise(32)
    x_in.rise(32)


def normed(K, B, H):
    def apply(dve, r, g):
        for k in range(KT):
            i = dve.tensor_tensor(H[:, k, span(g)], B.x(k, g), r, ALU.mult)
        return i
    norms(K, [([B.x(k, g) for k in range(KT)], g) for g in (LAT, CTXG)], B.const("ones"), 1.0 / D, B.eps(0), apply)


def modulated(K, B, layer, H):
    nc = K.nc
    gains = K.count("vector_part")
    with nc.Block() as block:
        @block.vector
        def _(dve):
            for c in (1, 0):
                dve.scalar_tensor_tensor(B.gain[:, :, c], B.mod[:, layer, 8:16, c], 1.0, B.col("norm_g")[:, 8 * layer:8 * layer + 8],
                                         ALU.add, ALU.mult).then_inc(gains.sem, 1)
            dve.wait_ge(gains.sem, gains.base + 2)
            for k in range(KT):
                x = H[:, k, span(LAT)]
                dve.tensor_scalar(x, x, B.gain[:, k, 0:1], B.mod[:, layer, k, 0:1], ALU.mult, ALU.add)

        @block.scalar
        def _(act):
            act.wait_ge(gains.sem, gains.base + 1)
            for k in range(KT):
                x = H[:, k, span(CTXG)]
                nc.scalar.activation(x, x, ACT.Identity, scale=B.gain[:, k, 1:2], bias=B.mod[:, layer, k, 1:2])
    gains.rise(2)


def gla(K, B, ctx, H, A):
    nc = K.nc
    zb = K.sb(ctx, "gla_out", [P, B_HEADS, TOK])
    with ExitStack() as tmp:
        big = K.sb(tmp, "gla_state", [P, 8 * TOK])
        gq = big[:, 0:2 * TOK].rearrange("p (j t) -> p j t", j=2)
        gk = big[:, 2 * TOK:4 * TOK].rearrange("p (j t) -> p j t", j=2)
        bs = big[:, 4 * TOK:6 * TOK].rearrange("p (j t) -> p j t", j=2)
        ex = big[:, 6 * TOK:8 * TOK].rearrange("p (j t) -> p j t", j=2)
        st = big[:, :].rearrange("p (z j c e) -> p z j c e", z=2, j=2, c=NCH)
        lr = big[0:32, 4 * TOK:5 * TOK]
        gw = big[0:32, 5 * TOK:5 * TOK + 512].rearrange("p (z c) -> p z c", z=2)

        def take(e, g):
            if e < 4:
                return "vector", copy_to((gq if e < 2 else gk)[:, e % 2, span(g)])
            return "scalar", act_to(nc, zb[:, e - 4, span(g)], ACT.Silu)
        dense(K, "gla_qkz", lambda k, g: H[:, k, span(g)], (LAT, CTXG), 8, take)
        gv = K.sb(tmp, "gla_v", [P, TOK // P, 512])
        units = []
        for t in range(TOK // P):
            units.append((0, 0, P, 512, lambda w, t=t: [(H[:, k, t * P:(t + 1) * P], w[:, k, :]) for k in range(KT)],
                          "vector", copy_to(gv[:, t, :])))
        for g in (LAT, CTXG):
            units.append((1, 0, 32, g[1], lambda w, g=g: [(w[:, k, :], H[:, k, span(g)]) for k in range(KT)], "scalar", act_to(nc, lr[:, span(g)], ACT.Copy)))
        products(K, "gla_v", units)

        go = K.sb(tmp, "gla_kd", [P, 4, TOK])
        dirs = [[K.sb(tmp, f"gla_{n}{z}", [P, 2, TOK]) for n in ("qt", "kt")] + [go[:, 2 * z:2 * z + 2, :]] for z in range(2)]
        decay = K.sb(tmp, "gla_decay", [P, 2, 2, NCH])
        gl = K.sb(tmp, "gla_g", [P, 4, TOK])
        small = lambda i: dirs[i // 2][0][:, i % 2, :]
        loaded, cleared = K.count("setup_loaded"), K.count("setup_ready")
        logits, lg_used, a1, v1 = (K.count(x) for x in ("product_done", "vector_freed", "scalar_part", "vector_part"))
        with nc.Block() as block:
            @block.gpsimd
            def _(pool):
                nc.gpsimd.memset(gw[:, :, :], 0.0).then_inc(cleared.sem, 1)

            @block.sync
            def _(sp):
                sp.wait_ge(cleared.sem, cleared.base + 1)
                for z in range(2):
                    sp.dma_start(gw[16 * z:16 * z + 16, z, :], A["ev_gate_w"][0, z]).then_inc(loaded.sem, 16)

            @block.tensor
            def _(pe):
                pe.wait_ge(loaded.sem, loaded.base + 32)
                for i in range(4):
                    z, j = i // 2, i % 2
                    for n, g in enumerate((LAT, CTXG)):
                        nc.tensor.matmul(K.psum[:, 2 * i + n, 0:g[1]], gw[:, z, j * P:(j + 1) * P], lr[:, span(g)], start=True,
                                         stop=True).then_inc(logits.sem, 1)

            @block.scalar
            def _(act):
                for i in range(4):
                    act.wait_ge(logits.sem, logits.base + 2 * i + 2)
                    ps = K.psum[:, 2 * i:2 * i + 2, :].rearrange("p b n -> p (b n)")[:, 0:TOK]
                    bias = B.col("gate_b")[:, i:i + 1]
                    nc.scalar.activation(gl[:, i, :], ps, ACT.Identity, bias=bias).then_inc(a1.sem, 1)
                    nc.scalar.activation(small(i), ps, ACT.Abs, bias=bias).then_inc(K.act_step.sem, 1)
                K.act_step.rise(4)
                act.wait_ge(K.act_step.sem, K.act_step.base)
                for i in range(4):
                    nc.scalar.activation(small(i), small(i), ACT.Exp, scale=-1.0).then_inc(K.act_step.sem, 1)
                K.act_step.rise(4)
                act.wait_ge(K.act_step.sem, K.act_step.base)
                for i in range(4):
                    nc.scalar.activation(small(i), small(i), ACT.Ln, bias=B.eps(4)).then_inc(a1.sem, 1)

            @block.vector
            def _(dve):
                for i in range(4):
                    dve.wait_ge(a1.sem, a1.base + i + 1)
                    dve.tensor_scalar(gl[:, i, :], gl[:, i, :], 0.0, None, ALU.min).then_inc(v1.sem, 1)
                dve.wait_ge(v1.sem, v1.base + 4)
                for i in range(4):
                    dve.wait_ge(a1.sem, a1.base + 4 + i + 1)
                    dve.tensor_tensor(gl[:, i, :], gl[:, i, :], small(i), ALU.subtract)
        loaded.rise(32)
        cleared.rise(1)
        logits.rise(8)
        a1.rise(8)
        v1.rise(4)
        with nc.Block() as block:
            @block.vector
            def _(dve):
                def sums(i):
                    z, j = i // 2, i % 2
                    g, b = gl[:, i, :], bs[:, i % 2, :]
                    if i >= 2:
                        dve.wait_ge(a1.sem, a1.base + 3 * i - 3)
                    dve.tensor_scalar(g, g, 1.0 / TAU, None, ALU.mult).then_inc(K.dve_step.sem, 1)
                    dve.wait_ge(K.dve_step.sem, K.dve_step.next())
                    dve.tensor_tensor_scan(b, B.const("restart"), g, 0.0, ALU.mult, ALU.add).then_inc(K.dve_step.sem, 1)
                    dve.wait_ge(K.dve_step.sem, K.dve_step.next())
                    bc = b.rearrange("p (c t) -> p c t", t=CH)
                    gc = g.rearrange("p (c t) -> p c t", t=CH)
                    dve.tensor_copy(decay[:, z, j, :], bc[:, :, CH - 1]).then_inc(K.dve_step.sem, 1)
                    dve.wait_ge(K.dve_step.sem, K.dve_step.next())
                    total = decay[:, z, j, :].unsqueeze(2).to_broadcast([P, NCH, CH])
                    if z == 1:
                        dve.tensor_tensor(bc, total, bc, ALU.subtract).then_inc(K.dve_step.sem, 1)
                        dve.wait_ge(K.dve_step.sem, K.dve_step.next())
                        dve.tensor_tensor(b, b, g, ALU.add).then_inc(K.dve_step.sem, 1)
                        dve.wait_ge(K.dve_step.sem, K.dve_step.next())
                    dve.tensor_tensor(gc, total, bc, ALU.subtract).then_inc(v1.sem, 1)

                def scale(i):
                    j = i % 2
                    qt, kt, kd = (x[:, j, :] for x in dirs[i // 2])
                    dve.wait_ge(a1.sem, a1.base + 3 * i + 3)
                    dve.scalar_tensor_tensor(qt, gq[:, j, :], float(B_DK) ** -0.5, qt, ALU.mult, ALU.mult)
                    dve.tensor_tensor(kt, gk[:, j, :], kt, ALU.mult)
                    dve.tensor_tensor(kd, gk[:, j, :], kd, ALU.mult)
                for i in range(4):
                    sums(i)
                    if i >= 1:
                        scale(i - 1)
                scale(3)

            @block.scalar
            def _(act):
                for i in range(4):
                    z, j = i // 2, i % 2
                    qt, kt, kd = (x[:, j, :] for x in dirs[z])
                    act.wait_ge(v1.sem, v1.base + i + 1)
                    nc.scalar.activation(qt, bs[:, i % 2, :], ACT.Exp).then_inc(a1.sem, 1)
                    nc.scalar.activation(kt, bs[:, i % 2, :], ACT.Exp, scale=-1.0).then_inc(a1.sem, 1)
                    nc.scalar.activation(kd, gl[:, i, :], ACT.Exp).then_inc(a1.sem, 1)
                nc.scalar.activation(decay.rearrange("p z j c -> p (z j c)"), decay.rearrange("p z j c -> p (z j c)"), ACT.Exp)
        a1.rise(12)
        v1.rise(4)
        kdT = gl.rearrange("p a t -> p (a t)").rearrange("p (z t c) -> p z t c", z=2, c=256)
        units = []
        for z in range(2):
            for j in range(2):
                for t in range(TOK // P):
                    units.append((None, 0, P, P, lambda w, z=z, j=j, t=t: ("T", dirs[z][2][:, j, t * P:(t + 1) * P], B.const("ident")),
                                  ("vector", "scalar")[t % 2], (copy_to if t % 2 == 0 else lambda d: act_to(nc, d, ACT.Copy))(kdT[:, z, t, j * P:(j + 1) * P])))
        products(K, "", units)
        order = [[8, 9, 10, 11] + list(range(8)), [11, 10, 9, 8] + list(range(7, -1, -1))]
        sum_done, state_done = K.count("product_done"), K.count("vector_freed")
        work = [(n, z, j) for n in range(NCH - 1) for z in range(2) for j in range(2)]
        with nc.Block() as block:
            @block.tensor
            def _(pe):
                for i, (n, z, j) in enumerate(work):
                    if i >= 8:
                        pe.wait_ge(state_done.sem, state_done.base + i - 7)
                    c = order[z][n]
                    r = slice(CH * (c % 2), CH * (c % 2) + CH)
                    for h in range(2):
                        mm = nc.tensor.matmul(K.psum[CH * h:CH * h + CH, i % 8, 0:B_DV], kdT[r, z, c // 2, j * P + CH * h:j * P + CH * h + CH],
                                              gv[r, c // 2, (2 * j + h) * B_DV:(2 * j + h + 1) * B_DV], start=True, stop=True)
                    mm.then_inc(sum_done.sem, 1)

            @block.vector
            def _(dve):
                for z in range(2):
                    i = dve.memset(st[:, z, :, order[z][0], :], 0.0)
                i.then_inc(K.dve_step.sem, 1)
                dve.wait_ge(K.dve_step.sem, K.dve_step.next())
                for i, (n, z, j) in enumerate(work):
                    c, nxt = order[z][n], order[z][n + 1]
                    dve.wait_ge(sum_done.sem, sum_done.base + i + 1)
                    if i >= 4:
                        dve.wait_ge(state_done.sem, state_done.base + i - 3)
                    dve.scalar_tensor_tensor(st[:, z, j, nxt, :], st[:, z, j, c, :], decay[:, z, j, c:c + 1], K.psum[:, i % 8, 0:B_DV],
                                             ALU.mult, ALU.add).then_inc(state_done.sem, 1)
        sum_done.rise(len(work))
        state_done.rise(len(work))
        work = [(h, t) for h in range(B_HEADS) for t in range(TOK // P)]
        scores, masked, out_done, out_used = (K.count(x) for x in ("product_done", "vector_part", "sum_done", "scalar_freed"))
        att = K.sb(tmp, "gla_att", [P, 2, 2, P])
        with nc.Block() as block:
            @block.tensor
            def _(pe):
                def score(i):
                    h, t = work[i]
                    r, j = slice(CH * (h % 2), CH * (h % 2) + CH), h // 2
                    for z in range(2):
                        if i >= 2:
                            pe.wait_ge(masked.sem, masked.base + i - 1)
                        nc.tensor.matmul(K.psum[:, 2 * (i % 2) + z, 0:P], dirs[z][1][r, j, t * P:(t + 1) * P],
                                         dirs[z][0][r, j, t * P:(t + 1) * P], start=True, stop=True).then_inc(scores.sem, 1)
                score(0)
                for i, (h, t) in enumerate(work):
                    if i + 1 < len(work):
                        score(i + 1)
                    r, j = slice(CH * (h % 2), CH * (h % 2) + CH), h // 2
                    pe.wait_ge(masked.sem, masked.base + i + 1)
                    if i >= 2:
                        pe.wait_ge(out_used.sem, out_used.base + i - 1)
                    o = K.psum[:, 4 + i % 2, :]
                    nc.tensor.matmul(o[:, 0:P], gv[:, t, h * P:(h + 1) * P], att[:, i % 2, 0, :], start=True, stop=False)
                    for z in range(2):
                        for c in (2 * t, 2 * t + 1):
                            s = slice(c * CH, (c + 1) * CH)
                            mm = nc.tensor.matmul(o[:, (c % 2) * CH:(c % 2 + 1) * CH], st[r, z, j, c, :], dirs[z][0][r, j, s],
                                                  start=False, stop=z == 1 and c % 2 == 1)
                    mm.then_inc(out_done.sem, 1)

            @block.vector
            def _(dve):
                for i in range(len(work)):
                    dve.wait_ge(scores.sem, scores.base + 2 * i + 2)
                    if i >= 2:
                        dve.wait_ge(out_done.sem, out_done.base + i - 1)
                    dve.tensor_tensor(att[:, i % 2, 0, :], K.psum[:, 2 * (i % 2), 0:P], B.const("mask_f"), ALU.mult)
                    dve.tensor_tensor(att[:, i % 2, 1, :], K.psum[:, 2 * (i % 2) + 1, 0:P], B.const("mask_b"), ALU.mult).then_inc(K.dve_step.sem, 1)
                    dve.wait_ge(K.dve_step.sem, K.dve_step.next())
                    dve.tensor_tensor(att[:, i % 2, 0, :], att[:, i % 2, 0, :], att[:, i % 2, 1, :], ALU.add).then_inc(masked.sem, 1)

            @block.scalar
            def _(act):
                for i, (h, t) in enumerate(work):
                    act.wait_ge(out_done.sem, out_done.base + i + 1)
                    nc.scalar.activation(go[:, h, t * P:(t + 1) * P], K.psum[:, 4 + i % 2, 0:P], ACT.Copy).then_inc(out_used.sem, 1)
        scores.rise(2 * len(work))
        for c in (masked, out_done, out_used):
            c.rise(len(work))

        def apply(dve, r, arg):
            h, g = arg
            dve.scalar_tensor_tensor(go[:, h, span(g)], go[:, h, span(g)], B.col("gla_norm")[:, h:h + 1], r, ALU.mult, ALU.mult).then_inc(K.dve_step.sem, 1)
            dve.wait_ge(K.dve_step.sem, K.dve_step.next())
            return dve.tensor_tensor(zb[:, h, span(g)], zb[:, h, span(g)], go[:, h, span(g)], ALU.mult)
        head_norms(K, B, [(h, g, go[:, h, span(g)], (h, g)) for h in range(B_HEADS) for g in (LAT, CTXG)], P, 1, 1.0 / B_DV, B.eps(0), apply)
    return zb


def attention(K, B, ctx, name, n_heads, q_tiles, q_of, k_of, v_of, out_of, scale, scratch, table=None, table_src=None):
    nc = K.nc
    S, W, WT = (scratch[:, 2 * n:2 * n + 2, :] for n in range(3))
    m = K.sb(ctx, "att_max", [P, 2, 4])
    work = [(h, q) for h in range(n_heads) for q in q_tiles]
    nq = len(q_tiles)
    scores, maxed, exped, normed, turned, evac_v, evac_a, out_done, out_used = (K.count(x) for x in (
        "product_done", "vector_part", "scalar_part", "pool_part", "turned", "vector_freed", "scalar_freed", "sum_done", "root_used"))
    t_in = [K.count("table_loaded_even"), K.count("table_loaded_odd")]
    copied = K.count("ctx_scores_copied")
    ident = B.const("ident")
    with nc.Block() as block:
        @block.tensor
        def _(pe):
            def score(i):
                h, (q0, kt0, nk) = work[i]
                if i >= 2:
                    pe.wait_ge(exped.sem, exped.base + i - 1)
                k0 = kt0 * P
                first = min(nk * P, BANK)
                b = 2 * (i % 2)
                mm = nc.tensor.matmul(K.psum[:, b, 0:first], q_of(h)[:, q0:q0 + P], k_of(h)[:, k0:k0 + first], start=True, stop=True)
                if nk * P > BANK:
                    mm = nc.tensor.matmul(K.psum[:, b + 1, 0:nk * P - BANK], q_of(h)[:, q0:q0 + P], k_of(h)[:, k0 + BANK:k0 + nk * P],
                                          start=True, stop=True)
                mm.then_inc(scores.sem, 1)

            def turn(i):
                nk = work[i][1][2]
                pe.wait_ge(normed.sem, normed.base + i + 1)
                if i >= 1:
                    pe.wait_ge(evac_v.sem, evac_v.base + i)
                    pe.wait_ge(evac_a.sem, evac_a.base + i)
                for k in range(nk):
                    t = nc.tensor.transpose(K.psum[:, 4 + 2 * k // nk, k % (nk // 2) * P:(k % (nk // 2) + 1) * P], W[:, i % 2, k * P:(k + 1) * P], ident)
                t.then_inc(turned.sem, 1)

            def out(i):
                h, (q0, kt0, nk) = work[i]
                pe.wait_ge(evac_v.sem, evac_v.base + i + 1)
                pe.wait_ge(evac_a.sem, evac_a.base + i + 1)
                if i >= 2:
                    pe.wait_ge(out_used.sem, out_used.base + i - 1)
                o = K.psum[(h % 2) * 64:(h % 2) * 64 + 64, 6 + i % 2, 0:P]
                for k in range(nk):
                    mm = nc.tensor.matmul(o, v_of(h, kt0 + k), WT[:, i % 2, k * P:(k + 1) * P], start=k == 0, stop=k == nk - 1)
                mm.then_inc(out_done.sem, 1)

            score(0)
            for i in range(len(work)):
                if i + 1 < len(work):
                    score(i + 1)
                if i >= 1:
                    out(i - 1)
                turn(i)
            out(len(work) - 1)

        @block.vector
        def _(dve):
            def head(i):
                h, (q0, kt0, nk) = work[i]
                b = i % 2
                ps = K.psum[:, 2 * b:2 * b + 2, :].rearrange("p b n -> p (b n)")[:, 0:nk * P]
                if table is not None:
                    if i % nq == 0:
                        dve.wait_ge(t_in[h % 2].sem, t_in[h % 2].base + 16 * (h // 2 + 1))
                        dve.tensor_tensor(table[:, h % 2, :, :], table[:, h % 2, :, :],
                                                                B.const("window").unsqueeze(1).to_broadcast([P, 14, 64]), ALU.add).then_inc(K.dve_step.sem, 1)
                        dve.wait_ge(K.dve_step.sem, K.dve_step.next())
                    dve.wait_ge(scores.sem, scores.base + i + 1)
                    if i >= 2:
                        dve.wait_ge(exped.sem, exped.base + i - 1)
                    bias = table[:, h % 2, 6 - 2 * (q0 // P):14 - 2 * (q0 // P), :].rearrange("p m c -> p (m c)")
                    dve.scalar_tensor_tensor(S[:, b, 0:BANK], ps[:, 0:BANK], scale, bias, ALU.mult, ALU.add).then_inc(K.dve_step.sem, 1)
                    dve.wait_ge(K.dve_step.sem, K.dve_step.next())
                    dve.wait_ge(copied.sem, copied.base + i + 1)
                    src, f = S[:, b, 0:nk * P], -1.0
                else:
                    dve.wait_ge(scores.sem, scores.base + i + 1)
                    src, f = ps, -scale
                dve.tensor_reduce(m[:, b, 0:1], src, AX, ALU.max).then_inc(K.dve_step.sem, 1)
                dve.wait_ge(K.dve_step.sem, K.dve_step.next())
                dve.tensor_scalar(m[:, b, 1:2], m[:, b, 0:1], f, None, ALU.mult).then_inc(maxed.sem, 1)

            def probs(i):
                nk = work[i][1][2]
                b = i % 2
                dve.wait_ge(exped.sem, exped.base + i + 1)
                dve.reciprocal(m[:, b, 3:4], m[:, b, 2:3]).then_inc(K.dve_step.sem, 1)
                dve.wait_ge(K.dve_step.sem, K.dve_step.next())
                dve.tensor_scalar(W[:, b, 0:nk * P], W[:, b, 0:nk * P], m[:, b, 3:4], None, ALU.mult).then_inc(normed.sem, 1)

            def take(i):
                h, (q0, kt0, nk) = work[i]
                dve.wait_ge(turned.sem, turned.base + i + 1)
                if i >= 2:
                    dve.wait_ge(out_done.sem, out_done.base + i - 1)
                n = nk * P // 2
                dve.tensor_copy(WT[:, i % 2, 0:n], K.psum[:, 4, 0:n]).then_inc(evac_v.sem, 1)

            def finish(i):
                h, (q0, kt0, nk) = work[i]
                dve.wait_ge(out_done.sem, out_done.base + i + 1)
                o = out_of(h, slice(q0, q0 + P))
                dve.tensor_tensor(o, K.psum[(h % 2) * 64:(h % 2) * 64 + 64, 6 + i % 2, 0:P], o, ALU.mult).then_inc(out_used.sem, 1)

            head(0)
            for i in range(len(work)):
                probs(i)
                if i + 1 < len(work):
                    head(i + 1)
                take(i)
                if i >= 1:
                    finish(i - 1)
            finish(len(work) - 1)

        @block.scalar
        def _(act):
            def exp(i):
                nk = work[i][1][2]
                b = i % 2
                ps = K.psum[:, 2 * b:2 * b + 2, :].rearrange("p b n -> p (b n)")[:, 0:nk * P]
                if table is not None:
                    act.wait_ge(scores.sem, scores.base + i + 1)
                    nc.scalar.activation(S[:, b, BANK:TOK], ps[:, BANK:TOK], ACT.Copy, scale=scale).then_inc(copied.sem, 1)
                    src, f = S[:, b, 0:nk * P], 1.0
                else:
                    src, f = ps, scale
                act.wait_ge(maxed.sem, maxed.base + i + 1)
                if i >= 2:
                    act.wait_ge(turned.sem, turned.base + i - 1)
                nc.scalar.activation(W[:, b, 0:nk * P], src, ACT.Exp, bias=m[:, b, 1:2], scale=f, accum_out=m[:, b, 2:3]).then_inc(exped.sem, 1)

            def take(i):
                nk = work[i][1][2]
                act.wait_ge(turned.sem, turned.base + i + 1)
                if i >= 2:
                    act.wait_ge(out_done.sem, out_done.base + i - 1)
                n = nk * P // 2
                nc.scalar.activation(WT[:, i % 2, n:2 * n], K.psum[:, 5, 0:n], ACT.Copy).then_inc(evac_a.sem, 1)

            exp(0)
            for i in range(len(work)):
                if i + 1 < len(work):
                    exp(i + 1)
                take(i)

        if table is not None:
            @block.sync
            def _(sp):
                for h in range(n_heads):
                    if h >= 2:
                        sp.wait_ge(maxed.sem, maxed.base + (h - 1) * nq)
                    sp.dma_start(table[:, h % 2, :, :], table_src[h].rearrange("p (m c) -> p m c", c=64)).then_inc(t_in[h % 2].sem, 16)
    for c in (scores, maxed, exped, normed, turned, evac_v, evac_a, out_done, out_used):
        c.rise(len(work))
    if table is not None:
        copied.rise(len(work))
        for c in t_in:
            c.rise(8 * n_heads)


def mla(K, B, ctx, H, A):
    nc = K.nc
    za = K.sb(ctx, "mla_out", [P, 4, TOK])
    both = (LAT, CTXG)
    with ExitStack() as tmp:
        lat = K.sb(tmp, "mla_lat", [P, 8, TOK])
        krope = K.sb(tmp, "mla_rope", [96, TOK])[64:96, :]

        def take(e, g):
            if e < 8:
                return "vector", copy_to(lat[:, e, span(g)])
            return "scalar", act_to(nc, za[:, e - 8, span(g)], ACT.Silu)
        dense(K, "mla_in", lambda k, g: H[:, k, span(g)], both, 12, take)
        products(K, "mla_rope", [(0, 64, 32, g[1], lambda w, g=g: [(w[:, k, :], H[:, k, span(g)]) for k in range(KT)], "vector",
                                  copy_to(krope[:, span(g)])) for g in both])

        def apply(dve, r, arg):
            g, a, n, gain = arg
            for k in range(n):
                i = dve.scalar_tensor_tensor(lat[:, a + k, span(g)], lat[:, a + k, span(g)], B.col(gain)[:, k:k + 1], r, ALU.mult, ALU.mult)
            return i
        norms(K, [([lat[:, k, span(g)] for k in range(6)], (g, 0, 6, "q_norm")) for g in both], B.const("ones"), 1.0 / Q_LORA, B.eps(0), apply)
        norms(K, [([lat[:, 6 + k, span(g)] for k in range(2)], (g, 6, 2, "kv_norm")) for g in both], B.const("ones"), 1.0 / KV_LORA, B.eps(0), apply)

        qb = H
        dense(K, "q_up", lambda k, g: lat[:, k, span(g)], both, A_HEADS, lambda h, g: (
            ("vector", copy_to(qb[0:96, h, span(g)])) if h % 2 == 0 else ("scalar", act_to(nc, qb[0:96, h, span(g)], ACT.Copy))), kt=6, m=96)
        kb = K.sb(tmp, "mla_k", [96, A_HEADS, TOK])
        v = K.sb(tmp, "mla_v", [P, TOK // P, 512])
        units = []
        for h in range(A_HEADS):
            for g in both:
                units.append((0, 0, 64, g[1], lambda w, h=h, g=g: [(w[:, k, h * 128:h * 128 + 64], lat[:, 6 + k, span(g)]) for k in range(2)],
                              ("vector", "scalar")[h % 2], copy_to(kb[0:64, h, span(g)]) if h % 2 == 0 else act_to(nc, kb[0:64, h, span(g)], ACT.Copy)))
        for t in range(TOK // P):
            units.append((0, 0, P, 512, lambda w, t=t: [(lat[:, 6 + k, t * P:(t + 1) * P],
                                                         w[:, k, :].rearrange("p (h c) -> p h c", c=128)[:, :, 64:128]) for k in range(2)],
                          "vector", copy_to(v[:, t, :])))

        def spread(dve):
            for h in range(A_HEADS):
                dve.tensor_copy(kb[64:96, h, :], krope)
        products(K, "kv_up", units, before=spread)

        def apply_head(dve, r, arg):
            x, gain = arg
            return dve.scalar_tensor_tensor(x, x, B.col(gain)[0:96, 0:1], r, ALU.mult, ALU.mult)
        head_norms(K, B, [(8 * n + h, g, x[0:96, h, span(g)], (x[0:96, h, span(g)], gain)) for n, (x, gain) in enumerate(((qb, "q_gain"), (kb, "k_gain")))
                          for h in range(A_HEADS) for g in both], 96, 1, 1.0 / A_QK, B.eps(0), apply_head)

        rot = lat[0:96, 0:2, 0:SEQ]
        table = lat[:, 2:4, :].rearrange("p a t -> p (a t)")[:, 0:2 * SEQ + P]
        loaded = K.count("setup_loaded")
        with nc.Block() as block:
            @block.sync
            def _(sp):
                sp.dma_start(table, A["tables"][:, 0:2 * SEQ + P]).then_inc(loaded.sem, 16)
                sp.wait_ge(loaded.sem, loaded.base + 16)
        loaded.rise(16)
        units = []
        for n, (x, h) in enumerate([(x, h) for x in (qb, kb) for h in range(A_HEADS)]):
            def turn(eng, _, ps, x=x, h=h, n=n):
                t = x[64:96, h, 0:SEQ]
                eng.tensor_tensor(rot[64:96, n % 2, :], ps[64:96, :], table[64:96, SEQ:2 * SEQ], ALU.mult)
                eng.tensor_tensor(t, t, table[64:96, 0:SEQ], ALU.mult).then_inc(K.dve_step.sem, 1)
                eng.wait_ge(K.dve_step.sem, K.dve_step.next())
                return eng.tensor_tensor(t, t, rot[64:96, n % 2, :], ALU.add)
            units.append((None, 0, 96, SEQ, lambda w, x=x, h=h: [(table[0:96, 2 * SEQ:2 * SEQ + 96], x[0:96, h, 0:SEQ])], "vector", turn))
        products(K, "", units)
        with ExitStack() as att:
            tiles = [(q * P, 0, 6) for q in range(4)] + [(SEQ + q * P, 4, 2) for q in range(2)]
            attention(K, B, att, "mla", A_HEADS, tiles, lambda h: qb[0:96, h, :], lambda h: kb[0:96, h, :],
                      lambda h, t: v[:, t, h * 64:(h + 1) * 64],
                      lambda h, s: za[(h % 2) * 64:(h % 2) * 64 + 64, h // 2, s], float(A_QK) ** -0.5, K.sb(att, "attention", [P, 6, TOK]))
    return za


def add_residual(K, B, layer, name, src, groups):
    def finish(e, g):
        def f(eng, _, ps):
            return eng.scalar_tensor_tensor(B.x(e, g), ps, B.mod[:, layer, 16 + e, (0 if g == LAT else 1):(1 if g == LAT else 2)], B.x(e, g), ALU.mult, ALU.add)
        return "vector", f
    dense(K, name, src, groups, KT, finish)


def odd_layer(K, B, A):
    nc = K.nc
    both = (LAT, CTXG)
    with ExitStack() as ctx:
        H = K.sb(ctx, "h", [P, KT, TOK])
        normed(K, B, H)
        modulation(K, B, 1)
        modulated(K, B, 1, H)
        q, k = K.sb(ctx, "od_q", [P, KT, SEQ]), K.sb(ctx, "od_k", [P, KT, TOK])
        h_of = lambda j, g: H[:, j, span(g)]

        dense(K, "od_kq", h_of, [both] * 8 + [(LAT,)] * 8, 16,
              lambda e, g: ("vector", copy_to(k[:, e, span(g)] if e < 8 else q[:, e - 8, :])))
        z = K.sb(ctx, "od_z", [P, KT, SEQ])
        dense(K, "od_z", h_of, (LAT,), 8, lambda e, g: ("scalar", act_to(nc, z[:, e, :], ACT.Silu)))
        tmp = ctx.enter_context(ExitStack())
        v = K.sb(tmp, "od_v", [P, TOK // P, D])
        units = []
        for c in range(2):
            for t in range(TOK // P):
                units.append((c, 0, P, 512, lambda w, t=t: [(H[:, j, t * P:(t + 1) * P], w[:, j, :]) for j in range(KT)],
                              ("vector", "scalar")[t % 2], copy_to(v[:, t, c * 512:(c + 1) * 512]) if t % 2 == 0 else
                              act_to(nc, v[:, t, c * 512:(c + 1) * 512], ACT.Copy)))
        products(K, "od_v", units)

        def apply(dve, r, arg):
            x, gain = arg
            return dve.scalar_tensor_tensor(x, x, B.col(gain), r, ALU.mult, ALU.mult)
        head_norms(K, B, [(2 * e, LAT, q[:, e, :], (q[:, e, :], "od_q_gain")) for e in range(KT)] +
                   [(16 + 2 * e, g, k[:, e, span(g)], (k[:, e, span(g)], "od_k_gain")) for e in range(KT) for g in both],
                   P, 2, 1.0 / 64, B.eps(0), apply)
        table = K.sb(tmp, "bias_table", [P, 2, 14, 64])
        rows = lambda h: slice(64 * (h % 2), 64 * (h % 2) + 64)
        attention(K, B, tmp, "od", C_HEADS, [(i * P, 0, 6) for i in range(4)], lambda h: q[rows(h), h // 2, :], lambda h: k[rows(h), h // 2, :],
                  lambda h, t: v[:, t, h * 64:(h + 1) * 64], lambda h, s: z[rows(h), h // 2, s], 0.125, H, table, A["bias"])
        tmp.close()
        add_residual(K, B, 1, "od_out", lambda k, g: z[:, k, :], (LAT,))


def conv_mixer(K, B, A, layer, G):
    nc = K.nc
    j = layer // 3
    dve_done, act_done = K.count("vector_freed"), K.count("scalar_freed")
    with ExitStack() as ctx:
        cg = K.sb(ctx, "conv_cg", [P, SEQ])
        u = K.sb(ctx, "conv_u", [P, SEQ + 2])
        acc = K.sb(ctx, "conv_sum", [P, SEQ])
        sz = K.sb(ctx, "conv_z", [P, 2, SEQ])
        one_engine(K, "vector", lambda dve: dve.memset(u[:, 0:2], 0.0))
        units = []
        for e in range(KT):
            tap = [B.col("conv_k")[:, 24 * j + 8 * i + e:24 * j + 8 * i + e + 1] for i in range(3)]

            def take_cg(eng, _, ps, e=e):
                if e:
                    eng.wait_ge(dve_done.sem, dve_done.base + 3 * e)
                return eng.tensor_copy(cg[:, :], ps)

            def take_h(eng, _, ps, e=e, tap=tap):
                eng.wait_ge(dve_done.sem, dve_done.base + 3 * e + 1)
                eng.tensor_tensor(u[:, 2:SEQ + 2], ps, cg[:, :], ALU.mult).then_inc(K.dve_step.sem, 1)
                eng.wait_ge(K.dve_step.sem, K.dve_step.next())
                eng.tensor_scalar(acc[:, :], u[:, 2:SEQ + 2], tap[2], None, ALU.mult).then_inc(K.dve_step.sem, 1)
                eng.wait_ge(K.dve_step.sem, K.dve_step.next())
                eng.scalar_tensor_tensor(acc[:, :], u[:, 1:SEQ + 1], tap[1], acc[:, :], ALU.mult, ALU.add).then_inc(K.dve_step.sem, 1)
                eng.wait_ge(K.dve_step.sem, K.dve_step.next())
                return eng.scalar_tensor_tensor(acc[:, :], u[:, 0:SEQ], tap[0], acc[:, :], ALU.mult, ALU.add)

            def take_z(eng, _, ps, e=e):
                if e >= 2:
                    eng.wait_ge(dve_done.sem, dve_done.base + 3 * (e - 1))
                return nc.scalar.activation(sz[:, e % 2, :], ps, ACT.Silu)

            def take_bg(eng, _, ps, e=e):
                eng.wait_ge(dve_done.sem, dve_done.base + 3 * e + 2)
                eng.tensor_tensor(acc[:, :], ps, acc[:, :], ALU.mult).then_inc(K.dve_step.sem, 1)
                eng.wait_ge(K.dve_step.sem, K.dve_step.next())
                eng.wait_ge(act_done.sem, act_done.base + e + 1)
                return eng.tensor_tensor(G[:, e, :], acc[:, :], sz[:, e % 2, :], ALU.mult)
            units += [("vector", take_cg), ("vector", take_h), ("scalar", take_z), ("vector", take_bg)]
        dense(K, f"conv_in{layer}", lambda k, g: B.X[:, k, :], (LAT,), 4 * KT, lambda e, g: units[e])


def ssm_mixer(K, B, A, G):
    nc = K.nc
    PI2, MAGIC = 6.2831850, 12582912.0
    with ExitStack() as ctx:
        U = K.sb(ctx, "ssm_u", [P, KT, SEQ])
        Y = K.sb(ctx, "ssm_y", [P, KT, SEQ])
        dense(K, "ssm_in", lambda k, g: B.X[:, k, :], (LAT,), 16,
              lambda e, g: ("vector", copy_to(U[:, e, :])) if e < 8 else ("scalar", act_to(nc, G[:, e - 8, :], ACT.Silu)))
        NP = GROUPS // 2
        with ExitStack() as tmp:
            time = K.sb(tmp, "time", [P, SEQ])
            bw = K.sb(tmp, "ssm_b", [P, 2, KT, P])
            cw = K.sb(tmp, "ssm_c", [P, 2, NP, 32])
            cs = K.sb(tmp, "ssm_c_scaled", [P, 3, NP, 32])
            s = K.sb(tmp, "ssm_scalars", [P, 14, NP])
            dt, mag, turn, sn, csn, ar, ai, inv, cr, ci, t0, t1, xr, rnd = (s[:, i, :] for i in range(14))
            loaded, a1, v1 = K.count("setup_loaded"), K.count("scalar_part"), K.count("vector_part")
            with nc.Block() as block:
                @block.sync
                def _(sp):
                    sp.dma_start(time[:, :], A["tables"][:, 2 * SEQ + P:3 * SEQ + P]).then_inc(loaded.sem, 16)
                    for i, n in enumerate(("ssm_b_re_2", "ssm_b_im_2")):
                        sp.dma_start(bw[:, i, :, :], A[n].rearrange("k p m -> p k m")).then_inc(loaded.sem, 16)
                    for i, n in enumerate(("ssm_c_re_2", "ssm_c_im_2")):
                        sp.dma_start(cw[:, i, :, :], A[n]).then_inc(loaded.sem, 16)
                    sp.wait_ge(loaded.sem, loaded.base + 80)

                @block.scalar
                def _(act):
                    nc.scalar.activation(dt, B.col("log_dt"), ACT.Exp).then_inc(a1.sem, 1)
                    act.wait_ge(v1.sem, v1.base + 1)
                    nc.scalar.activation(mag, xr, ACT.Exp).then_inc(a1.sem, 1)
                    act.wait_ge(v1.sem, v1.base + 2)
                    nc.scalar.activation(sn, turn, ACT.Sin, scale=PI2)
                    nc.scalar.activation(csn, t0, ACT.Sin, scale=PI2).then_inc(a1.sem, 1)

                @block.vector
                def _(dve):

                    def wrap(dst, x):
                        dve.tensor_scalar(rnd, x, MAGIC, MAGIC, ALU.add, ALU.subtract).then_inc(K.dve_step.sem, 1)
                        dve.wait_ge(K.dve_step.sem, K.dve_step.next())
                        dve.tensor_tensor(dst, x, rnd, ALU.subtract).then_inc(K.dve_step.sem, 1)
                        dve.wait_ge(K.dve_step.sem, K.dve_step.next())
                    dve.wait_ge(a1.sem, a1.base + 1)
                    dve.tensor_tensor(xr, B.col("lam_re"), dt, ALU.mult).then_inc(v1.sem, 1)
                    dve.tensor_tensor(t1, B.col("lam_im"), dt, ALU.mult).then_inc(K.dve_step.sem, 1)
                    dve.wait_ge(K.dve_step.sem, K.dve_step.next())
                    dve.tensor_scalar(t1, t1, 0.15915494309189535, None, ALU.mult).then_inc(K.dve_step.sem, 1)
                    dve.wait_ge(K.dve_step.sem, K.dve_step.next())
                    wrap(turn, t1)
                    dve.tensor_scalar(t1, turn, 0.25, None, ALU.add).then_inc(K.dve_step.sem, 1)
                    dve.wait_ge(K.dve_step.sem, K.dve_step.next())
                    dve.tensor_scalar(rnd, t1, MAGIC, MAGIC, ALU.add, ALU.subtract).then_inc(K.dve_step.sem, 1)
                    dve.wait_ge(K.dve_step.sem, K.dve_step.next())
                    dve.tensor_tensor(t0, t1, rnd, ALU.subtract).then_inc(v1.sem, 1)
                    dve.wait_ge(a1.sem, a1.base + 3)
                    dve.tensor_tensor(ar, mag, csn, ALU.mult).then_inc(K.dve_step.sem, 1)
                    dve.wait_ge(K.dve_step.sem, K.dve_step.next())
                    dve.tensor_tensor(ai, mag, sn, ALU.mult).then_inc(K.dve_step.sem, 1)
                    dve.wait_ge(K.dve_step.sem, K.dve_step.next())
                    dve.tensor_scalar(ar, ar, -1.0, None, ALU.add).then_inc(K.dve_step.sem, 1)
                    dve.wait_ge(K.dve_step.sem, K.dve_step.next())
                    lr, li = B.col("lam_re"), B.col("lam_im")
                    dve.tensor_tensor(t0, lr, lr, ALU.mult).then_inc(K.dve_step.sem, 1)
                    dve.wait_ge(K.dve_step.sem, K.dve_step.next())
                    dve.tensor_tensor(t1, li, li, ALU.mult).then_inc(K.dve_step.sem, 1)
                    dve.wait_ge(K.dve_step.sem, K.dve_step.next())
                    dve.tensor_tensor(t0, t0, t1, ALU.add).then_inc(K.dve_step.sem, 1)
                    dve.wait_ge(K.dve_step.sem, K.dve_step.next())
                    dve.reciprocal(inv, t0).then_inc(K.dve_step.sem, 1)
                    dve.wait_ge(K.dve_step.sem, K.dve_step.next())
                    dve.tensor_tensor(t0, ar, lr, ALU.mult).then_inc(K.dve_step.sem, 1)
                    dve.wait_ge(K.dve_step.sem, K.dve_step.next())
                    dve.tensor_tensor(t1, ai, li, ALU.mult).then_inc(K.dve_step.sem, 1)
                    dve.wait_ge(K.dve_step.sem, K.dve_step.next())
                    dve.tensor_tensor(t0, t0, t1, ALU.add).then_inc(K.dve_step.sem, 1)
                    dve.wait_ge(K.dve_step.sem, K.dve_step.next())
                    dve.tensor_tensor(cr, t0, inv, ALU.mult).then_inc(K.dve_step.sem, 1)
                    dve.wait_ge(K.dve_step.sem, K.dve_step.next())
                    dve.tensor_tensor(t0, ai, lr, ALU.mult).then_inc(K.dve_step.sem, 1)
                    dve.wait_ge(K.dve_step.sem, K.dve_step.next())
                    dve.tensor_tensor(t1, ar, li, ALU.mult).then_inc(K.dve_step.sem, 1)
                    dve.wait_ge(K.dve_step.sem, K.dve_step.next())
                    dve.tensor_tensor(t0, t0, t1, ALU.subtract).then_inc(K.dve_step.sem, 1)
                    dve.wait_ge(K.dve_step.sem, K.dve_step.next())
                    dve.tensor_tensor(ci, t0, inv, ALU.mult).then_inc(K.dve_step.sem, 1)
                    dve.wait_ge(K.dve_step.sem, K.dve_step.next())
                    dve.wait_ge(loaded.sem, loaded.base + 80)
                    crb, cib = (x.unsqueeze(2).to_broadcast([P, NP, 32]) for x in (cr, ci))
                    dve.tensor_tensor(cs[:, 0, :, :], cw[:, 0, :, :], crb, ALU.mult).then_inc(K.dve_step.sem, 1)
                    dve.wait_ge(K.dve_step.sem, K.dve_step.next())
                    dve.tensor_tensor(cs[:, 1, :, :], cw[:, 1, :, :], cib, ALU.mult).then_inc(K.dve_step.sem, 1)
                    dve.wait_ge(K.dve_step.sem, K.dve_step.next())
                    dve.tensor_tensor(cs[:, 0, :, :], cs[:, 0, :, :], cs[:, 1, :, :], ALU.subtract).then_inc(K.dve_step.sem, 1)
                    dve.wait_ge(K.dve_step.sem, K.dve_step.next())
                    dve.tensor_scalar(cs[:, 1, :, :], cs[:, 0, :, :], -1.0, None, ALU.mult).then_inc(K.dve_step.sem, 1)
                    dve.wait_ge(K.dve_step.sem, K.dve_step.next())
                    dve.tensor_tensor(cw[:, 0, :, :], cw[:, 0, :, :], cib, ALU.mult).then_inc(K.dve_step.sem, 1)
                    dve.wait_ge(K.dve_step.sem, K.dve_step.next())
                    dve.tensor_tensor(cw[:, 1, :, :], cw[:, 1, :, :], crb, ALU.mult).then_inc(K.dve_step.sem, 1)
                    dve.wait_ge(K.dve_step.sem, K.dve_step.next())
                    dve.tensor_tensor(cw[:, 0, :, :], cw[:, 0, :, :], cw[:, 1, :, :], ALU.add).then_inc(K.dve_step.sem, 1)
                    dve.wait_ge(K.dve_step.sem, K.dve_step.next())
                    dve.tensor_scalar(cs[:, 2, :, :], cw[:, 0, :, :], -1.0, None, ALU.mult).then_inc(K.dve_step.sem, 1)
                    dve.wait_ge(K.dve_step.sem, K.dve_step.next())
            loaded.rise(80)
            a1.rise(3)
            v1.rise(2)

            ph = K.sb(tmp, "ssm_phase", [P, 2, 3, SEQ])
            tb = K.sb(tmp, "ssm_table", [P, 2, 2, SEQ])
            bu = K.sb(tmp, "ssm_bu", [P, 2, 2, SEQ])
            w = K.sb(tmp, "ssm_turned", [P, 4, SEQ])
            zz = K.sb(tmp, "ssm_scan", [P, 2, 2, SEQ])
            mm = K.sb(tmp, "ssm_products", [P, 2, 4, SEQ])
            bu_done, bu_taken, tables, phases, scanned, prod_v, prod_p, y_done, y_taken = (K.count(x) for x in (
                "product_done", "scalar_freed", "scalar_part", "pool_part", "vector_part", "vector_freed", "pool_freed", "sum_done", "root_used"))
            turned, turns_made, rounded = K.count("turned"), K.count("turns_made"), K.count("turns_rounded")
            rd = K.sb(tmp, "ssm_whole_turns", [P, 2, SEQ])
            with nc.Block() as block:
                @block.tensor
                def _(pe):
                    def bring(q):
                        r = slice(32 * (q % 4), 32 * (q % 4) + 32)
                        if q >= 2:
                            pe.wait_ge(bu_taken.sem, bu_taken.base + q - 1)
                        for i in range(2):
                            x = nc.tensor.matmul(K.psum[:, 2 * (q % 2) + i, :], bw[r, i, q // 4, :], U[r, q // 4, :], start=True, stop=True,
                                                 tile_position=(32 * (q % 4), 0))
                        x.then_inc(bu_done.sem, 1)
                    bring(0)
                    bring(1)
                    for q in range(NP):
                        if q + 2 < NP:
                            bring(q + 2)
                        if q % 4 == 0 and q >= 8:
                            pe.wait_ge(y_taken.sem, y_taken.base + q // 4 - 1)
                        pe.wait_ge(prod_v.sem, prod_v.base + q + 1)
                        pe.wait_ge(prod_p.sem, prod_p.base + q + 1)
                        o = K.psum[32 * (q % 4):32 * (q % 4) + 32, 4 + q // 4 % 2, :]
                        for n, c in enumerate((0, 1, 2, 2)):
                            x = nc.tensor.matmul(o, cs[:, c, q, :], mm[:, q % 2, n, :], start=n == 0, stop=n == 3, tile_position=(0, 32 * (q % 4)))
                        x.then_inc(y_done.sem, 1)

                @block.gpsimd
                def _(pool):
                    def fraction(q):
                        pool.wait_ge(rounded.sem, rounded.base + q + 1)
                        if q >= 2:
                            pool.wait_ge(tables.sem, tables.base + q - 1)
                        pool.tensor_tensor(ph[:, q % 2, 1, :], ph[:, q % 2, 0, :], rd[:, q % 2, :], ALU.subtract).then_inc(phases.sem, 1)

                    def finish(q):
                        pool.wait_ge(scanned.sem, scanned.base + q + 1)
                        if q >= 2:
                            pool.wait_ge(y_done.sem, y_done.base + q - 1)
                        pool.tensor_tensor(mm[:, q % 2, 2, :], tb[:, q % 2, 0, :], zz[:, q % 2, 0, :], ALU.mult)
                        pool.tensor_tensor(mm[:, q % 2, 3, :], tb[:, q % 2, 1, :], zz[:, q % 2, 1, :], ALU.mult).then_inc(prod_p.sem, 1)
                    fraction(0)
                    for q in range(NP):
                        if q + 1 < NP:
                            fraction(q + 1)
                        finish(q)

                @block.scalar
                def _(act):
                    def turns(q):
                        if q >= 2:
                            act.wait_ge(phases.sem, phases.base + q - 1)
                        nc.scalar.activation(ph[:, q % 2, 0, :], time[:, :], ACT.Copy, scale=turn[:, q:q + 1]).then_inc(turns_made.sem, 1)
                    turns(0)
                    for q in range(NP):
                        if q + 1 < NP:
                            turns(q + 1)
                        if q >= 2:
                            act.wait_ge(turned.sem, turned.base + q - 1)
                        act.wait_ge(bu_done.sem, bu_done.base + q + 1)
                        for i in range(2):
                            x = nc.scalar.activation(bu[:, q % 2, i, :], K.psum[:, 2 * (q % 2) + i, :], ACT.Copy)
                        x.then_inc(bu_taken.sem, 1)
                        if q >= 2:
                            act.wait_ge(prod_v.sem, prod_v.base + q - 1)
                            act.wait_ge(prod_p.sem, prod_p.base + q - 1)
                        act.wait_ge(phases.sem, phases.base + q + 1)
                        nc.scalar.activation(ph[:, q % 2, 2, :], ph[:, q % 2, 1, :], ACT.Abs).then_inc(K.act_step.sem, 1)
                        nc.scalar.activation(tb[:, q % 2, 0, :], ph[:, q % 2, 1, :], ACT.Sin, scale=PI2)
                        act.wait_ge(K.act_step.sem, K.act_step.next())
                        nc.scalar.activation(tb[:, q % 2, 1, :], ph[:, q % 2, 2, :], ACT.Sin, scale=-PI2, bias=B.eps(3)).then_inc(tables.sem, 1)

                @block.vector
                def _(dve):
                    def whole(q):
                        dve.wait_ge(turns_made.sem, turns_made.base + q + 1)
                        if q >= 2:
                            dve.wait_ge(phases.sem, phases.base + q - 1)
                        dve.tensor_scalar(rd[:, q % 2, :], ph[:, q % 2, 0, :], MAGIC, MAGIC, ALU.add, ALU.subtract).then_inc(rounded.sem, 1)
                    def readout(j):
                        dve.wait_ge(y_done.sem, y_done.base + 4 * j + 4)
                        dve.scalar_tensor_tensor(Y[:, j, :], U[:, j, :], B.col("d_skip")[:, j:j + 1], K.psum[:, 4 + j % 2, :],
                                                 ALU.mult, ALU.add).then_inc(y_taken.sem, 1)
                    whole(0)
                    for q in range(NP):
                        re, im, sn_, cs_ = bu[:, q % 2, 0, :], bu[:, q % 2, 1, :], tb[:, q % 2, 0, :], tb[:, q % 2, 1, :]
                        if q + 1 < NP:
                            whole(q + 1)
                        dve.wait_ge(bu_taken.sem, bu_taken.base + q + 1)
                        dve.wait_ge(tables.sem, tables.base + q + 1)
                        dve.tensor_tensor(w[:, 0, :], re, cs_, ALU.mult)
                        dve.tensor_tensor(w[:, 1, :], im, sn_, ALU.mult)
                        dve.tensor_tensor(w[:, 2, :], im, cs_, ALU.mult)
                        dve.tensor_tensor(w[:, 3, :], re, sn_, ALU.mult).then_inc(turned.sem, 1)
                        dve.wait_ge(turned.sem, turned.base + q + 1)
                        dve.tensor_tensor(w[:, 0, :], w[:, 0, :], w[:, 1, :], ALU.add)
                        dve.tensor_tensor(w[:, 2, :], w[:, 2, :], w[:, 3, :], ALU.subtract).then_inc(K.dve_step.sem, 1)
                        dve.wait_ge(K.dve_step.sem, K.dve_step.next())
                        if q >= 2:
                            dve.wait_ge(prod_p.sem, prod_p.base + q - 1)
                            dve.wait_ge(prod_v.sem, prod_v.base + q - 1)
                            dve.wait_ge(y_done.sem, y_done.base + q - 1)
                        r = mag[:, q:q + 1].to_broadcast([P, SEQ])
                        dve.tensor_tensor_scan(zz[:, q % 2, 0, :], r, w[:, 0, :], 0.0, ALU.mult, ALU.add)
                        dve.tensor_tensor_scan(zz[:, q % 2, 1, :], r, w[:, 2, :], 0.0, ALU.mult, ALU.add).then_inc(scanned.sem, 1)
                        dve.wait_ge(scanned.sem, scanned.base + q + 1)
                        dve.tensor_tensor(mm[:, q % 2, 0, :], cs_, zz[:, q % 2, 0, :], ALU.mult)
                        dve.tensor_tensor(mm[:, q % 2, 1, :], sn_, zz[:, q % 2, 1, :], ALU.mult).then_inc(prod_v.sem, 1)
                        if q % 4 == 1 and q >= 4:
                            readout(q // 4 - 1)
                    readout(NP // 4 - 1)
            for c in (bu_done, bu_taken, tables, phases, scanned, prod_v, prod_p, y_done, turned, turns_made, rounded):
                c.rise(NP)
            y_taken.rise(KT)

        gelued = K.count("scalar_part")
        with nc.Block() as block:
            @block.scalar
            def _(act):
                for e in range(KT):
                    nc.scalar.activation(Y[:, e, :], Y[:, e, :], ACT.Gelu_apprx_tanh).then_inc(gelued.sem, 1)

            @block.vector
            def _(dve):
                for e in range(KT):
                    dve.wait_ge(gelued.sem, gelued.base + e + 1)
                    dve.tensor_tensor(G[:, e, :], G[:, e, :], Y[:, e, :], ALU.mult)
        gelued.rise(KT)
        taken = K.count("scalar_freed")

        def sigm(e, g):
            def f(eng, _, ps):
                return nc.scalar.activation(U[:, e, :], ps, ACT.Sigmoid, bias=B.col("b_glu")[:, e:e + 1])
            return "scalar", f

        def beside(dve):
            for e in range(KT):
                dve.wait_ge(taken.sem, taken.base + e + 1)
                dve.tensor_tensor(G[:, e, :], G[:, e, :], U[:, e, :], ALU.mult)
        dense(K, "ssm_glu", lambda k, g: Y[:, k, :], (LAT,), 8, sigm, beside=beside)


def rwkv_mixer(K, B, A, G):
    nc = K.nc
    NC, HP = SEQ // CH, 4
    with ExitStack() as ctx:
        w2 = K.sb(ctx, "lora_w2", [64, 2, D])
        low = K.sb(ctx, "lora_low", [64, 2, SEQ])
        r, k, v = (K.sb(ctx, "rwkv_" + n, [P, HP, SEQ]) for n in "rkv")
        aw = K.sb(ctx, "rwkv_aw", [P, 2 * HP, SEQ])
        a, w = aw[:, 0:HP, :], aw[:, HP:2 * HP, :]

        def lerp(n, dx, xs, first=False):
            def f(dve):
                if first:
                    dve.tensor_scalar(dx[:, :, 0:1], B.X[:, :, 0:1], -1.0, None, ALU.mult).then_inc(K.dve_step.sem, 1)
                    dve.wait_ge(K.dve_step.sem, K.dve_step.next())
                    dve.tensor_tensor(dx[:, :, 1:SEQ], B.X[:, :, 0:SEQ - 1], B.X[:, :, 1:SEQ], ALU.subtract).then_inc(K.dve_step.sem, 1)
                    dve.wait_ge(K.dve_step.sem, K.dve_step.next())
                for e in range(KT):
                    c = 8 * n + e
                    dve.scalar_tensor_tensor(xs[:, e, :], dx[:, e, :], B.col("mu")[:, c:c + 1], B.X[:, e, 0:SEQ], ALU.mult, ALU.add)
            return f

        for half in range(2):
            tile0 = 4 * half
            with ExitStack() as pro:
                dx, xs = aw, K.sb(pro, "xs", [P, KT, SEQ])
                order = [4, 5, 3, 0, 1, 2] if half == 0 else [0, 1, 2]
                one_engine(K, "vector", lerp(order[0], dx, xs, True))
                for i, n in enumerate(order):
                    x = lambda k, g: xs[:, k, :]
                    nxt = lerp(order[i + 1], dx, G if order[i + 1] == 5 else xs) if i + 1 < len(order) else None
                    if n >= 4:
                        j, name, func = n - 4, ("rwkv_w", "rwkv_a")[n - 4], (ACT.Tanh, ACT.Copy)[n - 4]
                        products(K, name, [(0, 0, 64, SEQ, lambda s, j=j: [(s[:, c, :], (xs, G)[j][:, c, :]) for c in range(KT)], "scalar",
                                            act_to(nc, low[:, j, :], func))], beside=nxt,
                                 load=(w2[:, j, :], A[("rwkv_w2_2", "rwkv_a2_2")[j]][0]))
                    elif n == 3:
                        dense(K, "rwkv_z", x, (LAT,), 8, lambda e, g: ("scalar", act_to(nc, G[:, e, :], ACT.Silu)), beside=nxt)
                    else:
                        dst = (r, k, v)[n]
                        dense(K, f"rwkv_{'rkv'[n]}{half}", x, (LAT,), 4, lambda e, g, dst=dst: ("vector", copy_to(dst[:, e, :])), beside=nxt)
            units = []
            for n, (dst, bias) in enumerate(((w, "w0"), (a, "a0"))):
                for e in range(HP):
                    def f(eng, _, ps, dst=dst, bias=bias, e=e):
                        return nc.scalar.activation(dst[:, e, :], ps, ACT.Sigmoid, bias=B.col(bias)[:, tile0 + e:tile0 + e + 1])
                    c = (tile0 + e) * P
                    units.append((None, 0, P, SEQ, lambda s, n=n, c=c: [(w2[:, n, c:c + P], low[:, n, :])], "scalar", f))
            products(K, "", units)
            with ExitStack() as tmp:
                rwkv_chunks(K, B, tmp, half, r, k, v, a, w, G)


def rwkv_chunks(K, B, ctx, half, r, k, v, a, w, G):
    nc = K.nc
    NC, HP, tile0 = SEQ // CH, 4, 4 * half
    col = lambda n, e: B.col(n)[:, tile0 + e:tile0 + e + 1]
    O = K.sb(ctx, "rwkv_out", [P, HP, SEQ])
    kk = K.sb(ctx, "rwkv_kk", [P, HP, SEQ])
    pend = K.sb(ctx, "rwkv_end", [P, HP, NC])
    flat = lambda x: x.rearrange("p e t -> p (e t)")
    decay = -0.6065306597126334
    inner = ExitStack()
    ex = K.sb(inner, "rwkv_exp", [P, 3, HP, SEQ])

    scaled, summed, weighted, shifted, bonus = (K.count(x) for x in (
        "scalar_part", "vector_part", "vector_freed", "setup_ready", "product_done"))
    with nc.Block() as block:
        @block.scalar
        def _(act):
            for e in range(HP):
                nc.scalar.activation(w[:, e, :], w[:, e, :], ACT.Copy, scale=decay).then_inc(scaled.sem, 1)
            for e in range(HP):
                nc.scalar.activation(kk[:, e, :], k[:, e, :], ACT.Copy, scale=col("k_k", e)).then_inc(scaled.sem, 1)
            act.wait_ge(summed.sem, summed.base + HP)
            cum = flat(ex[:, 0, :, :])
            nc.scalar.activation(flat(ex[:, 1, :, :]), cum, ACT.Exp)
            nc.scalar.activation(flat(ex[:, 2, :, :]), cum, ACT.Exp, scale=-1.0)
            act.wait_ge(shifted.sem, shifted.base + 1)
            nc.scalar.activation(flat(w[:, :, :]), flat(w[:, :, :]), ACT.Exp)
            nc.scalar.activation(pend.rearrange("p e c -> p (e c)"), pend.rearrange("p e c -> p (e c)"), ACT.Exp)

        @block.vector
        def _(dve):
            for e in range(HP):
                dve.wait_ge(scaled.sem, scaled.base + e + 1)
                dve.tensor_tensor_scan(ex[:, 0, e, :], B.const("restart")[:, 0:SEQ], w[:, e, :], 0.0, ALU.mult, ALU.add).then_inc(summed.sem, 1)
            dve.wait_ge(summed.sem, summed.base + HP)
            dve.tensor_copy(pend[:, :, :], ex[:, 0, :, :].rearrange("p e (c t) -> p e c t", t=CH)[:, :, :, CH - 1])
            dve.tensor_tensor(flat(w[:, :, :]), flat(ex[:, 0, :, :]), flat(w[:, :, :]), ALU.subtract).then_inc(shifted.sem, 1)
            for e in range(HP):
                dve.tensor_scalar(O[:, e, :], a[:, e, :], -1.0, col("k_a", e), ALU.add, ALU.mult).then_inc(K.dve_step.sem, 1)
            K.dve_step.rise(HP)
            dve.wait_ge(K.dve_step.sem, K.dve_step.base)
            dve.wait_ge(scaled.sem, scaled.base + 2 * HP)
            for e in range(HP):
                dve.scalar_tensor_tensor(k[:, e, :], O[:, e, :], 1.0, k[:, e, :], ALU.add, ALU.mult).then_inc(K.dve_step.sem, 1)
            K.dve_step.rise(HP)
            dve.wait_ge(K.dve_step.sem, K.dve_step.base)
            for e in range(HP):
                dve.scalar_tensor_tensor(O[:, e, :], r[:, e, :], col("r_k", e), k[:, e, :], ALU.mult, ALU.mult).then_inc(weighted.sem, 1)
            for e in range(HP):
                dve.wait_ge(bonus.sem, bonus.base + e + 1)
                dve.tensor_tensor(O[:, e, :], K.psum[:, e, :], v[:, e, :], ALU.mult)

        @block.tensor
        def _(pe):
            for e in range(HP):
                pe.wait_ge(weighted.sem, weighted.base + e + 1)
                nc.tensor.matmul(K.psum[:, e, :], B.const("ones64"), O[:, e, :], start=True, stop=True).then_inc(bonus.sem, 1)
    scaled.rise(2 * HP)
    shifted.rise(1)
    for c in (summed, weighted, bonus):
        c.rise(HP)

    def scale_by_decay(dve):
        dve.tensor_tensor(flat(r[:, :, :]), flat(r[:, :, :]), flat(ex[:, 1, :, :]), ALU.mult)
        dve.tensor_tensor(flat(k[:, :, :]), flat(k[:, :, :]), flat(ex[:, 2, :, :]), ALU.mult)
        dve.tensor_tensor(flat(a[:, :, :]), flat(a[:, :, :]), flat(ex[:, 2, :, :]), ALU.mult).then_inc(K.dve_step.sem, 1)
        dve.wait_ge(K.dve_step.sem, K.dve_step.next())

    def apply(dve, rinv, e):
        dve.tensor_tensor(kk[:, e, :], kk[:, e, :], rinv, ALU.mult).then_inc(K.dve_step.sem, 1)
        dve.wait_ge(K.dve_step.sem, K.dve_step.next())
        dve.tensor_tensor(a[:, e, :], a[:, e, :], kk[:, e, :], ALU.mult)
        return dve.tensor_tensor(w[:, e, :], w[:, e, :], kk[:, e, :], ALU.mult)
    head_norms(K, B, [(2 * e, LAT, kk[:, e, :], e) for e in range(HP)], P, 2, 1.0, None, apply, "norm", before=scale_by_decay)
    inner.close()

    at, bt, kt, rt = w, a, k, r
    by_chunk = lambda x: x[:, :, :].rearrange("p e (c t) -> p e c t", t=CH)
    bT, RB, YT, XX = by_chunk(a), by_chunk(w), by_chunk(k), by_chunk(v)
    KV = K.sb(ctx, "rwkv_kv", [P, HP, NC, CH])
    HC = NC // 2
    wide = ("A", "B", "K", "V", "aT", "kT", "vT", "Bo", "AK", "Bi", "Ai", "B2", "A2", "R")
    inner = ExitStack()
    T = {n: K.sb(inner, "rwkv_" + n, [P, 2, HC, P]) for n in wide}
    T["RK"] = K.sb(inner, "rwkv_RK", [P, 2, HC, CH])
    T["E"] = T["AK"]
    done, taken, taken_act, widened, cleared = (K.count(x) for x in (
        "product_done", "vector_freed", "scalar_freed", "scalar_part", "setup_ready"))
    chunk = lambda x, e: x[:, e, :].rearrange("p (c t) -> p c t", t=CH)

    def masked(dve, ps, pairs):
        for dst, m in pairs:
            if ps.shape[2] == CH:
                i = dve.tensor_tensor(dst, ps, B.const(m).unsqueeze(1).to_broadcast([P, HC, CH]), ALU.mult)
            else:
                blocks = lambda x: x.rearrange("p c (h t) -> p (c h) t", t=CH)
                i = dve.tensor_tensor(blocks(dst), blocks(ps), B.const(m).unsqueeze(1).to_broadcast([P, 2 * HC, CH]), ALU.mult)
        return i

    def rounds(e, p):
        here = slice(HC * p, HC * p + HC)
        R_ = chunk(rt, e)[:, here, :]
        t = {n: x[:, p, :, :] for n, x in T.items()}
        A_, B_, K_, V_ = (t[n] for n in "ABKV")
        vT_narrow, GG = XX[:, e, here, :], YT[:, e, here, :]
        keep = lambda dst: lambda dve, ps: dve.tensor_copy(dst, ps)
        by_act = lambda dst: lambda act, ps: nc.scalar.activation(dst, ps, ACT.Copy)
        cut = lambda *pairs: lambda dve, ps: masked(dve, ps, pairs)
        plus = lambda dst: lambda dve, ps: dve.tensor_tensor(dst, ps, dst, ALU.add)
        minus = lambda dst, x: lambda dve, ps: dve.scalar_tensor_tensor(dst, ps, -1.0, x, ALU.mult, ALU.add)
        turn = B.const("ident").unsqueeze(1).to_broadcast([P, HC, P])
        turn_narrow = B.const("eye64").unsqueeze(1).to_broadcast([P, HC, CH])

        def narrow(dst):
            def f(dve, ps):
                for h in range(2):
                    i = dve.tensor_copy(dst[CH * h:CH * h + CH, :, :], ps[CH * h:CH * h + CH, :, CH * h:CH * h + CH])
                return i
            return f
        return [
            [(B_, A_, cut((t["Bi"], "before_in"), (t["Bo"], "before_out"))), (A_, B_, cut((t["Ai"], "after_in"))),
             (K_, A_, cut((t["AK"], "before"))), (A_, turn, by_act(t["aT"]), "scalar")],
            [(B_, R_, cut((RB[:, e, here, :], "upto"))), (B_, turn_narrow, keep(bT[:, e, here, :])),
             (K_, R_, cut((t["RK"], "upto"))), (K_, turn, by_act(t["kT"]), "scalar")],
            [(V_, turn, by_act(t["vT"]), "scalar"), (V_, turn_narrow, by_act(vT_narrow), "scalar"), (t["Ai"], t["Bi"], keep(t["B2"])), (t["Bi"], t["Ai"], keep(t["A2"])),
             lambda dve: dve.tensor_tensor(t["R"], turn, t["Bi"], ALU.subtract)],
            [(t["AK"], vT_narrow, by_act(GG), "scalar"), (t["kT"], vT_narrow, by_act(KV[:, e, here, :]), "scalar"),
             (t["vT"], t["RK"], by_act(chunk(kk, e)[:, here, :]), "scalar"),
             (t["A2"], t["R"], plus(t["R"]))],
            [(t["A2"], t["B2"], keep(t["Bi"])), (t["B2"], t["A2"], by_act(t["Ai"]), "scalar")],
            [(t["Ai"], t["R"], plus(t["R"])), (t["Bi"], t["Ai"], by_act(t["A2"]), "scalar")],
            [(t["A2"], t["R"], plus(t["R"]))],
            [(t["R"], turn, keep(t["E"]))],
            [(t["E"], t["Bo"], keep(t["Bi"])), (t["Bo"], t["E"], by_act(t["Ai"]), "scalar")],
            [(t["Bi"], t["Ai"], keep(t["A2"]))],
            [(t["A2"], t["R"], plus(t["R"]))],
            [(t["Ai"], t["R"], minus(t["B2"], t["R"]))],
            [(t["B2"], GG, by_act(XX[:, e, here, :]), "scalar"), (t["aT"], t["B2"], narrow(YT[:, e, here, :]))],
        ]

    of = [[rounds(e, p) for p in range(2)] for e in range(HP)]
    turns = [(e, p, r, of[e][p][r]) for e in range(HP) for r in range(len(of[0][0])) for p in range(2)]
    upto, upto_act, n_done = [0], [0], [0]
    for _, _, _, units in turns:
        upto.append(upto[-1] + sum(not isinstance(u, tuple) or len(u) == 3 for u in units))
        upto_act.append(upto_act[-1] + sum(isinstance(u, tuple) and len(u) == 4 for u in units))
        n_done.append(n_done[-1] + sum(isinstance(u, tuple) for u in units))
    last_wide = [n_done[n + 1] for n, (_, _, r, _) in enumerate(turns) if r == 2]
    with nc.Block() as block:
        @block.gpsimd
        def _(pool):
            for n in "ABKV":
                nc.gpsimd.memset(T[n][:, :, :, :], 0.0).then_inc(cleared.sem, 1)

        @block.scalar
        def _(act):
            def widen(n):
                e, p = n // 2, n % 2
                if n >= 2:
                    act.wait_ge(done.sem, done.base + last_wide[n - 2])
                for name, x in zip("ABKV", (at, bt, kt, v)):
                    for h in range(2):
                        s = slice(CH * h, CH * h + CH)
                        i = nc.scalar.activation(T[name][s, p, :, s], chunk(x, e)[s, HC * p:HC * p + HC, :], ACT.Copy)
                i.then_inc(widened.sem, 1)
            act.wait_ge(cleared.sem, cleared.base + 4)
            widen(0)
            widen(1)
            for n, (e, p, r, units) in enumerate(turns):
                if r == 6 and e + 1 < HP:
                    widen(2 * e + 2 + p)
                mine = [(i, u) for i, u in enumerate(x for x in units if isinstance(x, tuple)) if len(u) == 4]
                if mine:
                    act.wait_ge(done.sem, done.base + n_done[n + 1])
                    if n >= 2:
                        act.wait_ge(taken.sem, taken.base + upto[n - 1])
                for i, u in mine:
                    width = u[1].shape[2]
                    u[2](act, K.psum[:, 4 * p + i, 0:HC * width].rearrange("p (c t) -> p c t", t=width)).then_inc(taken_act.sem, 1)

        @block.tensor
        def _(pe):
            for n, (e, p, r, units) in enumerate(turns):
                if r == 0:
                    pe.wait_ge(widened.sem, widened.base + 2 * e + p + 1)
                if n >= 2:
                    pe.wait_ge(taken.sem, taken.base + upto[n - 1])
                    pe.wait_ge(taken_act.sem, taken_act.base + upto_act[n - 1])
                for i, u in enumerate(x for x in units if isinstance(x, tuple)):
                    width = u[1].shape[2]
                    for c in range(HC):
                        mm = nc.tensor.matmul(K.psum[:, 4 * p + i, c * width:(c + 1) * width], u[0][:, c, :], u[1][:, c, :], start=c == 0,
                                              stop=c == HC - 1, skip_group_check=True)
                    mm.then_inc(done.sem, 1)

        @block.vector
        def _(dve):
            for n, (e, p, r, units) in enumerate(turns):
                dve.wait_ge(done.sem, done.base + n_done[n + 1])
                if n >= 2:
                    dve.wait_ge(taken.sem, taken.base + upto[n - 1])
                for i, u in enumerate(units):
                    if isinstance(u, tuple) and len(u) == 4:
                        continue
                    if isinstance(u, tuple):
                        width = u[1].shape[2]
                        u[2](dve, K.psum[:, 4 * p + i, 0:HC * width].rearrange("p (c t) -> p c t", t=width)).then_inc(taken.sem, 1)
                    else:
                        u(dve).then_inc(taken.sem, 1)
    cleared.rise(4)
    widened.rise(2 * HP)
    done.rise(n_done[-1])
    taken_act.rise(upto_act[-1])
    taken.rise(upto[-1])

    two = lambda n: T[n][:, 0, :, :].rearrange("p (a c) (h t) -> p a (c h) t", a=2, t=CH)
    Hs, U, Hg = two("aT"), two("kT"), two("vT")[:, 0, :, :]
    uh, ud, od, hd, hs = (K.count(x) for x in ("product_done", "vector_part", "sum_done", "root_used", "vector_freed"))
    bank = lambda i: K.psum[:, i, 0:HP * CH].rearrange("p (e t) -> p e t", t=CH)
    with nc.Block() as block:
        @block.tensor
        def _(pe):
            def each(c, b, pairs, sem):
                for e in range(HP):
                    for h in range(2):
                        s = slice(64 * h, 64 * h + 64)
                        for n, (x, y) in enumerate(pairs):
                            mm = nc.tensor.matmul(bank(b)[s, e, :], x(s, e), y(s, e), start=n == 0 and e == 0, stop=n == len(pairs) - 1 and e == HP - 1,
                                                  skip_group_check=True)
                mm.then_inc(sem, 1)
            for c in range(NC):
                H, Uc = Hs[:, c % 2, :, :], U[:, c % 2, :, :]
                pe.wait_ge(hs.sem, hs.base + c + 1)
                if c >= 1:
                    pe.wait_ge(ud.sem, ud.base + c)
                each(c, 0, [(lambda s, e: YT[s, e, c, :], lambda s, e: H[s, e, :])], uh.sem)
                pe.wait_ge(ud.sem, ud.base + c + 1)
                if c >= 1:
                    pe.wait_ge(hd.sem, hd.base + c)
                each(c, 2, [(lambda s, e: bT[s, e, c, :], lambda s, e: Uc[s, e, :])], uh.sem)
                each(c, 4 + c % 2, [(lambda s, e: H[s, e, :], lambda s, e: chunk(rt, e)[s, c, :]),
                                    (lambda s, e: Uc[s, e, :], lambda s, e: RB[s, e, c, :])], od.sem)

        @block.vector
        def _(dve):
            dve.memset(Hs[:, 0, :, :], 0.0).then_inc(hs.sem, 1)
            for c in range(NC):
                H, Uc = Hs[:, c % 2, :, :], U[:, c % 2, :, :]
                dve.wait_ge(hs.sem, hs.base + c + 1)
                dve.tensor_tensor(Hg[:, :, :], H, KV[:, :, c, :], ALU.add)
                dve.wait_ge(uh.sem, uh.base + 2 * c + 1)
                dve.scalar_tensor_tensor(Uc, bank(0), -1.0, XX[:, :, c, :], ALU.mult, ALU.subtract).then_inc(ud.sem, 1)
                dve.wait_ge(ud.sem, ud.base + c + 1)
                dve.wait_ge(uh.sem, uh.base + 2 * c + 2)
                dve.tensor_tensor(Hg[:, :, :], bank(2), Hg[:, :, :], ALU.add).then_inc(K.dve_step.sem, 1)
                dve.wait_ge(K.dve_step.sem, K.dve_step.next())
                if c >= 1:
                    dve.wait_ge(od.sem, od.base + c)
                dve.tensor_tensor(Hs[:, (c + 1) % 2, :, :], Hg[:, :, :], pend[:, :, c].unsqueeze(2).to_broadcast([P, HP, CH]), ALU.mult).then_inc(hs.sem, 1)
                o = kk[:, :, c * CH:(c + 1) * CH]
                dve.wait_ge(od.sem, od.base + c + 1)
                dve.tensor_tensor(o, bank(4 + c % 2), o, ALU.add).then_inc(hd.sem, 1)
    uh.rise(2 * NC)
    ud.rise(NC)
    od.rise(NC)
    hd.rise(NC)
    hs.rise(NC + 1)

    center(K, B, [([kk[:, e, :]], [kk[:, e, :]]) for e in range(HP)], B.const("ones64"), 1.0 / CH, T["Bi"][:, 0, :, :].rearrange("p c t -> p (c t)"))
    inner.close()

    def readout(dve, rinv, e):
        x, g = kk[:, e, :], G[:, tile0 + e, :]
        dve.scalar_tensor_tensor(x, x, col("lnx_g", e), rinv, ALU.mult, ALU.mult).then_inc(K.dve_step.sem, 1)
        dve.wait_ge(K.dve_step.sem, K.dve_step.next())
        dve.scalar_tensor_tensor(x, x, col("lnx_b", e), O[:, e, :], ALU.add, ALU.add).then_inc(K.dve_step.sem, 1)
        dve.wait_ge(K.dve_step.sem, K.dve_step.next())
        return dve.tensor_tensor(g, g, x, ALU.mult)
    head_norms(K, B, [(2 * e, LAT, kk[:, e, :], e) for e in range(HP)], P, 2, 1.0 / CH, B.eps(2), readout)


def center(K, B, items, ones, scale, mean):
    nc = K.nc
    units = []
    freed = K.count("vector_freed")
    for n, (srcs, dsts) in enumerate(items):
        def f(eng, _, ps, n=n, srcs=srcs, dsts=dsts):
            if n:
                eng.wait_ge(freed.sem, freed.base + n)
            eng.tensor_scalar(mean, ps, scale, None, ALU.mult).then_inc(K.dve_step.sem, 1)
            eng.wait_ge(K.dve_step.sem, K.dve_step.next())
            for x, y in zip(srcs, dsts):
                i = eng.tensor_tensor(y, x, mean, ALU.subtract)
            return i
        units.append((None, 0, P, SEQ, lambda w, srcs=srcs: [(ones, x) for x in srcs], "vector", f))
    products(K, "", units)


def second_layer(K, B, A, layer, out):
    nc = K.nc
    with ExitStack() as ctx:
        G = K.sb(ctx, "mixer_gated", [P, KT, SEQ])
        (conv_mixer, ssm_mixer, rwkv_mixer)[layer % 3](*((K, B, A, layer, G) if layer % 3 == 0 else (K, B, A, G)))

        def add(e, g):
            def f(eng, _, ps):
                return eng.scalar_tensor_tensor(B.X[:, e, :], B.X[:, e, :], ALPHA, ps, ALU.mult, ALU.add)
            return "vector", f
        pT, pp = K.sb(ctx, "ple_in", [P, 2, SEQ]), K.sb(ctx, "ple", [P, KT, SEQ])
        dense(K, f"mix_out{layer}", lambda k, g: G[:, k, :], (LAT,), 8, add,
              load=(pT[:, :, :], A["p"][layer].rearrange("(k p) t -> p k t", p=P)))
        taken = K.count("scalar_freed")
        products(K, f"ple_p{layer}", linear_units([0], 2, pT, (LAT,), lambda e, g: ("vector", copy_to(pp[:, e, :])), width=8))

        def sigm(e, g):
            return "scalar", act_to(nc, G[:, e, :], ACT.Sigmoid)

        added = K.count("vector_part")

        def beside(dve):
            for e in range(KT):
                dve.wait_ge(taken.sem, taken.base + e + 1)
                dve.tensor_tensor(pp[:, e, :], pp[:, e, :], G[:, e, :], ALU.mult).then_inc(K.dve_step.sem, 1)
                dve.wait_ge(K.dve_step.sem, K.dve_step.next())
                dve.tensor_tensor(pp[:, e, :], pp[:, e, :], B.X[:, e, :], ALU.add).then_inc(added.sem, 1)

        def total(pool):
            pool.wait_ge(added.sem, added.base + 2)
            pool.tensor_tensor(pT[:, 0, :], pp[:, 0, :], pp[:, 1, :], ALU.add).then_inc(K.pool_step.sem, 1)
            for e in range(2, KT):
                pool.wait_ge(added.sem, added.base + e + 1)
                pool.wait_ge(K.pool_step.sem, K.pool_step.next())
                pool.tensor_tensor(pT[:, 0, :], pT[:, 0, :], pp[:, e, :], ALU.add).then_inc(K.pool_step.sem, 1)
            K.pool_step.rise(1)
        dense(K, f"ple_g{layer}", lambda k, g: B.X[:, k, :], (LAT,), 8, sigm, beside=beside, on_pool=total)
        added.rise(KT)
        layer_norm(K, B, layer, pp, pT[:, 0, :], pT[:, 1, :], out)


def layer_norm(K, B, layer, y, total, mean, out):
    nc = K.nc
    ones = B.const("ones")
    sums, centered, squared, root_done, scaled, shifted, stored = (K.count(n) for n in (
        "sum_done", "vector_part", "square_done", "root_done", "root_used", "scalar_part", "stored"))
    with ExitStack() as ctx:
        sq, root = K.sb(ctx, "squares", [P, 4, SEQ]), K.sb(ctx, "roots", [P, SEQ])
        with nc.Block() as block:
            @block.tensor
            def _(pe):
                nc.tensor.matmul(K.psum[:, 0, :], ones, total, start=True, stop=True).then_inc(sums.sem, 1)
                for e in range(KT):
                    pe.wait_ge(squared.sem, squared.base + e + 1)
                    nc.tensor.matmul(K.psum[:, 1, :], ones, sq[:, e % 4, :], start=e == 0, stop=e == KT - 1).then_inc(sums.sem, 1)

            @block.vector
            def _(dve):
                dve.wait_ge(sums.sem, sums.base + 1)
                dve.tensor_scalar(mean, K.psum[:, 0, :], 1.0 / D, None, ALU.mult).then_inc(K.dve_step.sem, 1)
                dve.wait_ge(K.dve_step.sem, K.dve_step.next())
                for e in range(KT):
                    dve.tensor_tensor(y[:, e, :], y[:, e, :], mean, ALU.subtract).then_inc(centered.sem, 1)
                dve.wait_ge(root_done.sem, root_done.base + 1)
                dve.reciprocal(mean, root[:, :]).then_inc(K.dve_step.sem, 1)
                dve.wait_ge(K.dve_step.sem, K.dve_step.next())
                dve.wait_ge(centered.sem, centered.base + KT)
                for e in range(KT):
                    dve.scalar_tensor_tensor(B.X[:, e, :], y[:, e, :], B.col("ln_g")[:, 8 * layer + e:8 * layer + e + 1], mean,
                                             ALU.mult, ALU.mult).then_inc(scaled.sem, 1)

            @block.scalar
            def _(act):
                for e in range(KT):
                    act.wait_ge(centered.sem, centered.base + e + 1)
                    if e >= 4:
                        act.wait_ge(sums.sem, sums.base + e - 2)
                    nc.scalar.activation(sq[:, e % 4, :], y[:, e, :], ACT.Square).then_inc(squared.sem, 1)
                act.wait_ge(sums.sem, sums.base + KT + 1)
                nc.scalar.activation(root[:, :], K.psum[:, 1, :], ACT.Sqrt, bias=B.eps(1), scale=1.0 / D).then_inc(root_done.sem, 1)
                for e in range(KT):
                    act.wait_ge(scaled.sem, scaled.base + e + 1)
                    nc.scalar.activation(B.X[:, e, :], B.X[:, e, :], ACT.Identity, bias=B.col("ln_b")[:, 8 * layer + e:8 * layer + e + 1]).then_inc(shifted.sem, 1)

            if out is not None:
                @block.sync
                def _(sp):
                    for e in range(KT):
                        sp.wait_ge(shifted.sem, shifted.base + e + 1)
                        sp.dma_start(out[e * P:(e + 1) * P, :], B.X[:, e, :]).then_inc(stored.sem, 16)
                    sp.wait_ge(stored.sem, stored.base + 16 * KT)
    sums.rise(KT + 1)
    for c in (centered, squared, scaled, shifted):
        c.rise(KT)
    root_done.rise(1)


def program(nc, A, out):
    with ExitStack() as ctx:
        K, B = Core(nc, ctx), Buffers()
        where_c, n_c = columns()
        where_k, packed, _ = shape_constants()
        B.X = K.sb(ctx, "residual", [P, KT, SEQ])
        B.cols = K.sb(ctx, "columns", [P, n_c])
        B.consts = K.sb(ctx, "constants", [P, packed.shape[1]])
        B.col = lambda n: B.cols[:, where_c[n][0]:where_c[n][0] + where_c[n][1]]
        B.const = lambda n: B.consts[:, where_k[n][0]:where_k[n][0] + where_k[n][1]]
        B.eps = lambda i: B.const("eps")[:, i:i + 1]
        B.x = lambda k, g: B.X[:, k, :] if g == LAT else B.XC[:, k, :]
        plan_weights(K, A)
        with ExitStack() as first:
            B.XC = K.sb(first, "residual_ctx", [P, KT, CTX])
            B.scond = K.sb(first, "silu_cond", [P, KT, 2])
            B.mod = K.sb(first, "modulation", [P, 2, 24, 2])
            B.gain = K.sb(first, "norm_gain", [P, KT, 2])
            setup(K, B, A)
            with ExitStack() as layer:
                H = K.sb(layer, "h", [P, KT, TOK])
                normed(K, B, H)
                modulation(K, B, 0)
                modulated(K, B, 0, H)
                zb = gla(K, B, layer, H, A)
                za = mla(K, B, layer, H, A)
                add_residual(K, B, 0, "ev_out", lambda k, g: (za[:, k, span(g)] if k < 4 else zb[:, k - 4, span(g)]), (LAT, CTXG))
            odd_layer(K, B, A)
        for layer in range(4):
            second_layer(K, B, A, layer, out if layer == 3 else None)


def host_layout(inputs):
    import numpy as np
    a = {n: np.asarray(v) for n, v in inputs.items()}
    col = lambda v: np.reshape(v, (-1, P)).T
    pad = lambda v: np.pad(np.reshape(v, (-1, 1)), ((0, P - v.size), (0, 0)))
    pairs = lambda v: np.reshape(v, (GROUPS // 2, P)).T
    where, n = columns()
    vectors = {
        "cond": np.stack([col(a["c"]), col(a["c_ctx"])], 2).reshape(P, 2 * KT), "norm_g": col(a["norm_g"]), "ada_b": col(a["ada_b"]),
        "q_norm": col(a["ev_q_norm"]), "kv_norm": col(a["ev_kv_norm"]), "q_gain": pad(a["ev_q_gain"]), "k_gain": pad(a["ev_k_gain"]),
        "gate_b": col(a["ev_gate_b"]), "gla_norm": col(a["ev_gla_norm"]), "od_q_gain": np.tile(a["od_q_gain"].reshape(-1, 1), (2, 1)),
        "od_k_gain": np.tile(a["od_k_gain"].reshape(-1, 1), (2, 1)), "conv_k": col(a["conv_k_2"]), "lam_re": pairs(a["ssm_lam_re_2"]),
        "lam_im": pairs(a["ssm_lam_im_2"]), "log_dt": pairs(np.repeat(a["ssm_log_dt_2"], STATE, axis=-1)), "d_skip": col(a["ssm_d_2"]),
        "b_glu": col(a["ssm_b_glu_2"]), "mu": col(a["rwkv_mu_2"]), "w0": col(a["rwkv_w0_2"]), "a0": col(a["rwkv_a0_2"]),
        "k_k": col(a["rwkv_k_k_2"]), "k_a": col(a["rwkv_k_a_2"]), "r_k": col(a["rwkv_r_k_2"]), "lnx_g": col(a["rwkv_lnx_g_2"]),
        "lnx_b": col(a["rwkv_lnx_b_2"]), "ln_g": col(a["ln_g_2"]), "ln_b": col(a["ln_b_2"])}
    out = {"columns": np.ascontiguousarray(np.concatenate([vectors[k] for k in where], axis=1)),
           "constants": shape_constants()[1], "tables": shape_constants()[2]}
    out["x"] = np.ascontiguousarray(a["x"][0].T)
    out["ctx"] = np.ascontiguousarray(a["ctx"][0].T)
    out["p"] = np.ascontiguousarray(a["p_2"][:, 0].transpose(0, 2, 1))
    c = np.arange(64)
    idx = np.clip(c[None, :] - c[:, None] + 15, 0, 30)
    r = a["od_rpb"][0]
    t = np.stack([r[:, 1 - e:15 - e][:, :, idx].transpose(0, 2, 1, 3) for e in (0, 1)], 1)
    out["bias"] = np.ascontiguousarray(t.reshape(C_HEADS, P, 14 * 64))
    for n in WEIGHTS:
        out[n] = np.ascontiguousarray(a[n])
    for n in ("ssm_b_re_2", "ssm_b_im_2"):
        z = np.zeros((GROUPS // 2, 2, GRP, 2, STATE), np.float32)
        for g in range(2):
            z[:, g, :, g, :] = a[n][0, g::2].transpose(0, 2, 1)
        out[n] = z.reshape(KT, P, P)
    for n in ("ssm_c_re_2", "ssm_c_im_2"):
        z = np.zeros((GROUPS // 2, 2, STATE, 2, GRP), np.float32)
        for g in range(2):
            z[:, g, :, g, :] = a[n][0, g::2].transpose(0, 2, 1)
        out[n] = np.ascontiguousarray(z.reshape(GROUPS // 2, P, 2 * GRP).transpose(1, 0, 2))
    return out


WEIGHTS = ("ada_w", "ev_w_in", "ev_w_uq", "ev_w_ukv", "ev_gate_w", "ev_w_out", "od_w_in", "od_w_out", "conv_w_in_2", "conv_w_out_2",
           "ssm_w_in_2", "ssm_w_glu_2", "ssm_w_out_2", "rwkv_w_rkvz_2", "rwkv_w1_2", "rwkv_w2_2", "rwkv_a1_2", "rwkv_a2_2", "rwkv_w_out_2",
           "ple_proj_2", "ple_gate_2")


def kernel(**inputs):
    import concourse.bacc as bacc
    from concourse.bass_utils import run_bass_kernel_spmd
    import numpy as np

    nc = bacc.Bacc("TRN2", target_bir_lowering=False, num_devices=1)
    host = host_layout(inputs)
    arrays = {f"{n}_dram": a for n, a in host.items()}
    A = {n: nc.dram_tensor(f"{n}_dram", a.shape, F32, kind="ExternalInput").ap() for n, a in host.items()}
    out = nc.dram_tensor("out_dram", (D, SEQ), F32, kind="ExternalOutput").ap()
    program(nc, A, out)
    got = run_bass_kernel_spmd(nc, [arrays], core_ids=[0])
    return np.ascontiguousarray(got.results[0]["out_dram"].T)[None]
```
